# Optimizing a Trainium2 kernel written in Bass

```python
import math
import jax, jax.numpy as jnp
from jax import lax
import numpy as np

D_MODEL = 1024
BATCH = 1
SEQ = 256
DEPTH = 2

GRID_W = 64
CTX_LEN = 256
N_MIXERS = 2
Q_BLOCK = 128
NORM_EPS = 1e-6
ROPE_THETA = 10000.0
N_MOD = 6

MLA_HEADS = 8
MLA_Q_RANK = 384
MLA_KV_RANK = 256
MLA_NOPE_DIM = 128
MLA_ROPE_DIM = 64
MLA_V_DIM = 128

GQA_HEADS = 8
GQA_KV_HEADS = 2
GQA_GROUP = GQA_HEADS // GQA_KV_HEADS
GQA_HEAD_DIM = 128

PEER_HEADS = 8
PEER_N_KEYS = 128
PEER_N_EXPERTS = PEER_N_KEYS * PEER_N_KEYS
PEER_KEY_DIM = 256
PEER_HALF_DIM = PEER_KEY_DIM // 2
PEER_TOPK = 16
PEER_CHUNK = 128

kernel_name = 'hybrid_mla_gqa_peer_dit'

def rmsnorm(x, g):
    xf = x.astype(jnp.float32)
    y = xf * lax.rsqrt(jnp.mean(xf * xf, axis=-1, keepdims=True) + NORM_EPS)
    return (y * g.astype(jnp.float32)).astype(x.dtype)

def modulate(h, shift, scale):
    return h * (1 + scale) + shift

def axial_rope_tables(n_tokens, rot_dim, dtype):
    rows = n_tokens // GRID_W
    row = jnp.repeat(jnp.arange(rows, dtype=jnp.float32), GRID_W)
    col = jnp.tile(jnp.arange(GRID_W, dtype=jnp.float32), rows)
    d_axis = rot_dim // 2
    inv_freq = ROPE_THETA ** (-jnp.arange(0, d_axis, 2, dtype=jnp.float32) / d_axis)
    ang_r = row[:, None] * inv_freq
    ang_c = col[:, None] * inv_freq
    ang = jnp.concatenate([ang_r, ang_r, ang_c, ang_c], axis=-1)
    return jnp.cos(ang).astype(dtype), jnp.sin(ang).astype(dtype)

def apply_axial_rope(x, cos, sin):
    a1, a2, b1, b2 = jnp.split(x, 4, axis=-1)
    rot = jnp.concatenate([-a2, a1, -b2, b1], axis=-1)
    return x * cos + rot * sin

def sweep_query_blocks(fn, *qs):
    b, n = qs[0].shape[:2]
    nb = n // Q_BLOCK
    blocks = tuple(jnp.swapaxes(q.reshape((b, nb, Q_BLOCK) + q.shape[2:]), 0, 1) for q in qs)
    out = lax.map(lambda args: fn(*args), blocks)
    out = jnp.swapaxes(out, 0, 1)
    return out.reshape((b, n) + out.shape[3:])

def mla_project(h, w_in, q_norm, w_uq, kv_norm, w_ukv):
    b, n, _ = h.shape
    a = h @ w_in
    cq, ckv, k_rope = jnp.split(a, [MLA_Q_RANK, MLA_Q_RANK + MLA_KV_RANK], axis=-1)
    q = (rmsnorm(cq, q_norm) @ w_uq).reshape(b, n, MLA_HEADS, MLA_NOPE_DIM + MLA_ROPE_DIM)
    kv = (rmsnorm(ckv, kv_norm) @ w_ukv).reshape(b, n, MLA_HEADS, MLA_NOPE_DIM + MLA_V_DIM)
    q_nope, q_rope = jnp.split(q, [MLA_NOPE_DIM], axis=-1)
    k_nope, v = jnp.split(kv, [MLA_NOPE_DIM], axis=-1)
    return q_nope, q_rope, k_nope, k_rope, v

def mla_attend(q_n, q_r, k_n, k_r, v):
    scale = 1.0 / math.sqrt(MLA_NOPE_DIM + MLA_ROPE_DIM)
    s = (jnp.einsum('bqhd,bkhd->bhqk', q_n, k_n, preferred_element_type=jnp.float32)
         + jnp.einsum('bqhd,bkd->bhqk', q_r, k_r, preferred_element_type=jnp.float32))
    p = jax.nn.softmax(s * scale, axis=-1).astype(v.dtype)
    return jnp.einsum('bhqk,bkhd->bqhd', p, v)

def mla_mixer(h, hc, w_in, q_norm, w_uq, kv_norm, w_ukv, w_o, need_ctx):
    b, n, _ = h.shape
    cos, sin = axial_rope_tables(n, MLA_ROPE_DIM, h.dtype)
    qn, qr, kn, kr, v = mla_project(h, w_in, q_norm, w_uq, kv_norm, w_ukv)
    qr = apply_axial_rope(qr, cos[:, None, :], sin[:, None, :])
    kr = apply_axial_rope(kr, cos, sin)
    qn_c, qr_c, kn_c, kr_c, v_c = mla_project(hc, w_in, q_norm, w_uq, kv_norm, w_ukv)
    kn_all = jnp.concatenate([kn_c, kn], axis=1)
    kr_all = jnp.concatenate([kr_c, kr], axis=1)
    v_all = jnp.concatenate([v_c, v], axis=1)
    y = sweep_query_blocks(lambda a, r: mla_attend(a, r, kn_all, kr_all, v_all), qn, qr)
    y = y.reshape(b, n, MLA_HEADS * MLA_V_DIM) @ w_o
    y_c = None
    if need_ctx:
        y_c = mla_attend(qn_c, qr_c, kn_c, kr_c, v_c).reshape(b, hc.shape[1], MLA_HEADS * MLA_V_DIM) @ w_o
    return y, y_c

def gqa_project(h, w_qkv, q_norm, k_norm):
    b, n, _ = h.shape
    q, k, v = jnp.split(h @ w_qkv, [GQA_HEADS * GQA_HEAD_DIM, (GQA_HEADS + GQA_KV_HEADS) * GQA_HEAD_DIM], axis=-1)
    q = rmsnorm(q.reshape(b, n, GQA_KV_HEADS, GQA_GROUP, GQA_HEAD_DIM), q_norm)
    k = rmsnorm(k.reshape(b, n, GQA_KV_HEADS, GQA_HEAD_DIM), k_norm)
    v = v.reshape(b, n, GQA_KV_HEADS, GQA_HEAD_DIM)
    return q, k, v

def gqa_attend(q, k, v):
    scale = 1.0 / math.sqrt(GQA_HEAD_DIM)
    s = jnp.einsum('bqgrd,bkgd->bgrqk', q, k, preferred_element_type=jnp.float32)
    p = jax.nn.softmax(s * scale, axis=-1).astype(v.dtype)
    return jnp.einsum('bgrqk,bkgd->bqgrd', p, v)

def gqa_mixer(h, hc, w_qkv, q_norm, k_norm, w_o, need_ctx):
    b, n, _ = h.shape
    cos, sin = axial_rope_tables(n, GQA_HEAD_DIM, h.dtype)
    q, k, v = gqa_project(h, w_qkv, q_norm, k_norm)
    q = apply_axial_rope(q, cos[:, None, None, :], sin[:, None, None, :])
    k = apply_axial_rope(k, cos[:, None, :], sin[:, None, :])
    q_c, k_c, v_c = gqa_project(hc, w_qkv, q_norm, k_norm)
    k_all = jnp.concatenate([k_c, k], axis=1)
    v_all = jnp.concatenate([v_c, v], axis=1)
    y = sweep_query_blocks(lambda qb: gqa_attend(qb, k_all, v_all), q)
    y = y.reshape(b, n, GQA_HEADS * GQA_HEAD_DIM) @ w_o
    y_c = None
    if need_ctx:
        y_c = gqa_attend(q_c, k_c, v_c).reshape(b, hc.shape[1], GQA_HEADS * GQA_HEAD_DIM) @ w_o
    return y, y_c

def peer_ffn(h, w_query, sub_k1, sub_k2, u_tab, v_tab):
    b, n, d = h.shape
    nt = b * n
    t = h.reshape(nt, d)
    q = (t @ w_query).reshape(nt, PEER_HEADS, 2, PEER_HALF_DIM)
    s1 = jnp.einsum('thd,hkd->thk', q[:, :, 0], sub_k1, preferred_element_type=jnp.float32)
    s2 = jnp.einsum('thd,hkd->thk', q[:, :, 1], sub_k2, preferred_element_type=jnp.float32)
    v1, i1 = lax.top_k(s1, PEER_TOPK)
    v2, i2 = lax.top_k(s2, PEER_TOPK)
    cand = (v1[..., :, None] + v2[..., None, :]).reshape(nt, PEER_HEADS, PEER_TOPK * PEER_TOPK)
    cand_idx = (i1[..., :, None] * PEER_N_KEYS + i2[..., None, :]).reshape(nt, PEER_HEADS, PEER_TOPK * PEER_TOPK)
    top_s, top_pos = lax.top_k(cand, PEER_TOPK)
    expert_idx = jnp.take_along_axis(cand_idx, top_pos, axis=-1)
    gates = jax.nn.softmax(top_s, axis=-1).astype(h.dtype)

    def chunk(args):
        tc, ec, gc = args
        a = jax.nn.gelu(jnp.einsum('td,thkd->thk', tc, u_tab[ec]), approximate=False)
        return jnp.einsum('thk,thkd->td', gc * a, v_tab[ec])

    nc = nt // PEER_CHUNK
    out = lax.map(chunk, (t.reshape(nc, PEER_CHUNK, d),
                          expert_idx.reshape(nc, PEER_CHUNK, PEER_HEADS, PEER_TOPK),
                          gates.reshape(nc, PEER_CHUNK, PEER_HEADS, PEER_TOPK)))
    return out.reshape(b, n, d)

def setup_inputs(seed: int = 0) -> dict:
    key = jax.random.key(seed)
    ks = jax.random.split(key, 64)
    counter = [0]

    def nrm(shape, scale):
        k = ks[counter[0]]
        counter[0] += 1
        return jax.random.normal(k, shape, jnp.float32) * scale

    def gain(n):
        return 1.0 + nrm((n,), 0.02)

    d = D_MODEL
    inp = {
        'x': nrm((BATCH, SEQ, d), 1.0),
        'c': nrm((BATCH, d), 1.0),
        'ctx': nrm((BATCH, CTX_LEN, d), 1.0),
        'c_ctx': nrm((d,), 1.0),
    }
    for i in range(DEPTH):
        pre = 'l%d_' % i
        inp[pre + 'ada_w'] = nrm((d, N_MOD * d), 0.5 * d ** -0.5)
        inp[pre + 'ada_b'] = nrm((N_MOD * d,), 0.01)
        inp[pre + 'norm_mix'] = gain(d)
        inp[pre + 'norm_ffn'] = gain(d)
        if i % N_MIXERS == 0:
            inp[pre + 'mla_w_in'] = nrm((d, MLA_Q_RANK + MLA_KV_RANK + MLA_ROPE_DIM), d ** -0.5)
            inp[pre + 'mla_q_norm'] = gain(MLA_Q_RANK)
            inp[pre + 'mla_w_uq'] = nrm((MLA_Q_RANK, MLA_HEADS * (MLA_NOPE_DIM + MLA_ROPE_DIM)), MLA_Q_RANK ** -0.5)
            inp[pre + 'mla_kv_norm'] = gain(MLA_KV_RANK)
            inp[pre + 'mla_w_ukv'] = nrm((MLA_KV_RANK, MLA_HEADS * (MLA_NOPE_DIM + MLA_V_DIM)), MLA_KV_RANK ** -0.5)
            inp[pre + 'mla_w_o'] = nrm((MLA_HEADS * MLA_V_DIM, d), (MLA_HEADS * MLA_V_DIM) ** -0.5)
        else:
            inp[pre + 'gqa_w_qkv'] = nrm((d, (GQA_HEADS + 2 * GQA_KV_HEADS) * GQA_HEAD_DIM), d ** -0.5)
            inp[pre + 'gqa_q_norm'] = gain(GQA_HEAD_DIM)
            inp[pre + 'gqa_k_norm'] = gain(GQA_HEAD_DIM)
            inp[pre + 'gqa_w_o'] = nrm((GQA_HEADS * GQA_HEAD_DIM, d), (GQA_HEADS * GQA_HEAD_DIM) ** -0.5)
        inp[pre + 'peer_w_query'] = nrm((d, PEER_HEADS * PEER_KEY_DIM), d ** -0.5)
        inp[pre + 'peer_k1'] = nrm((PEER_HEADS, PEER_N_KEYS, PEER_HALF_DIM), PEER_HALF_DIM ** -0.5)
        inp[pre + 'peer_k2'] = nrm((PEER_HEADS, PEER_N_KEYS, PEER_HALF_DIM), PEER_HALF_DIM ** -0.5)
        inp[pre + 'peer_u'] = nrm((PEER_N_EXPERTS, d), d ** -0.5)
        inp[pre + 'peer_v'] = nrm((PEER_N_EXPERTS, d), 1.0)
    inp['norm_out'] = gain(d)
    return inp

def reference(x, c, ctx, c_ctx,
              l0_ada_w, l0_ada_b, l0_norm_mix, l0_norm_ffn,
              l0_mla_w_in, l0_mla_q_norm, l0_mla_w_uq, l0_mla_kv_norm, l0_mla_w_ukv, l0_mla_w_o,
              l0_peer_w_query, l0_peer_k1, l0_peer_k2, l0_peer_u, l0_peer_v,
              l1_ada_w, l1_ada_b, l1_norm_mix, l1_norm_ffn,
              l1_gqa_w_qkv, l1_gqa_q_norm, l1_gqa_k_norm, l1_gqa_w_o,
              l1_peer_w_query, l1_peer_k1, l1_peer_k2, l1_peer_u, l1_peer_v,
              norm_out):
    layers = [
        dict(ada_w=l0_ada_w, ada_b=l0_ada_b, norm_mix=l0_norm_mix, norm_ffn=l0_norm_ffn,
             mixer=(l0_mla_w_in, l0_mla_q_norm, l0_mla_w_uq, l0_mla_kv_norm, l0_mla_w_ukv, l0_mla_w_o),
             peer=(l0_peer_w_query, l0_peer_k1, l0_peer_k2, l0_peer_u, l0_peer_v)),
        dict(ada_w=l1_ada_w, ada_b=l1_ada_b, norm_mix=l1_norm_mix, norm_ffn=l1_norm_ffn,
             mixer=(l1_gqa_w_qkv, l1_gqa_q_norm, l1_gqa_k_norm, l1_gqa_w_o),
             peer=(l1_peer_w_query, l1_peer_k1, l1_peer_k2, l1_peer_u, l1_peer_v)),
    ]
    mixers = (mla_mixer, gqa_mixer)
    xc = ctx
    for i in range(DEPTH):
        p = layers[i]
        need_ctx = i < DEPTH - 1
        mod = jax.nn.silu(c) @ p['ada_w'] + p['ada_b']
        mod_c = jax.nn.silu(c_ctx) @ p['ada_w'] + p['ada_b']
        sh_a, sc_a, g_a, sh_f, sc_f, g_f = [m[:, None, :] for m in jnp.split(mod, N_MOD, axis=-1)]
        csh_a, csc_a, cg_a, csh_f, csc_f, cg_f = jnp.split(mod_c, N_MOD, axis=-1)
        h = modulate(rmsnorm(x, p['norm_mix']), sh_a, sc_a)
        hc = modulate(rmsnorm(xc, p['norm_mix']), csh_a, csc_a)
        y, y_c = mixers[i % N_MIXERS](h, hc, *p['mixer'], need_ctx=need_ctx)
        x = x + g_a * y
        h = modulate(rmsnorm(x, p['norm_ffn']), sh_f, sc_f)
        x = x + g_f * peer_ffn(h, *p['peer'])
        if need_ctx:
            xc = xc + cg_a * y_c
            hc = modulate(rmsnorm(xc, p['norm_ffn']), csh_f, csc_f)
            xc = xc + cg_f * peer_ffn(hc, *p['peer'])
    return rmsnorm(x, norm_out)


_drawn_inputs = setup_inputs


def setup_inputs(seed=0):
    import zlib

    import numpy as np

    out = dict(_drawn_inputs(seed))
    spreads = {}
    factors = {'l0_norm_mix': 4.983,
     'l0_mla_q_norm': 7.521,
     'l0_mla_kv_norm': 4.278,
     'l1_ada_b': 2.704,
     'l1_norm_mix': 8.0,
     'l1_gqa_q_norm': 8.0,
     'l1_gqa_k_norm': 8.0,
     'norm_out': 7.697,
     'l1_norm_ffn': 6.757}
    for name, (base, spread) in spreads.items():
        noise = np.random.default_rng([zlib.crc32(name.encode()), seed]).standard_normal(out[name].shape)
        drawn = base * np.exp(spread * noise) if base else spread * noise
        out[name] = __import__('jax').numpy.asarray(drawn.astype(out[name].dtype))
    for name, factor in factors.items():
        out[name] = (out[name] * factor).astype(out[name].dtype)
    return out
```

```python
import math
from contextlib import ExitStack

import numpy as np
import concourse.bass as bass
from concourse import mybir

F32, BF16, U32, I32 = mybir.dt.float32, mybir.dt.bfloat16, mybir.dt.uint32, mybir.dt.int32
ALU = mybir.AluOpType
ACT = mybir.ActivationFunctionType
AX = mybir.AxisListType

P = 128
D = 1024
KD = D // P
CTX, SEQ = 256, 256
TOK = CTX + SEQ
NC = TOK // P
CC = CTX // P
EPS = 1e-6
H = 8
NOPE, ROPE = 128, 64
QR, KVR = 384, 256
KQ, KKV = QR // P, KVR // P
HALF = 384
GKV = 2
NKEY = 128
TOPK = 16
MODW = 6 * D
LAYERS = 2
SH_A, SC_A, G_A, SH_F, SC_F, G_F = range(6)
LAT, CON = 0, 1
NEG = -3.0e38
GRP = 4
NG = TOPK // GRP
RING = TOPK
ADA_SLOTS = 4
ADA_CHUNK = 512


def kind(c):
    return CON if c < CC else LAT


def phase(build):
    def built(self, *args, **more):
        self.phase_sems = []
        build(self, *args, **more)
        self.nc.clear_and_free_semaphores(self.phase_sems)
        self.nc.all_engine_barrier()
    return built


class Kernel:
    def __init__(self, nc, dram, out):
        self.nc, self.dram, self.out = nc, dram, out
        self.names = 0

    def sem(self, name):
        self.names += 1
        handle = self.nc.alloc_semaphore(name=f"{name}_{self.names}")
        self.phase_sems.append(handle)
        return handle

    def lasting_sem(self, name):
        self.names += 1
        return self.ctx.enter_context(self.nc.semaphore(f"{name}_{self.names}"))

    def view(self, region, at, *shape, dtype=None):
        n = int(np.prod(shape))
        v = region[:, at:at + n]
        if dtype is not None:
            v = v.bitcast(dtype)
        if len(shape) == 2:
            v = v.rearrange("p (a b) -> p a b", a=shape[0])
        if len(shape) == 3:
            v = v.rearrange("p (a b c) -> p a b c", a=shape[0], b=shape[1])
        return v

    def build(self):
        nc = self.nc
        with ExitStack() as ctx:
            self.ctx = ctx
            sb = lambda n, s, d=F32: ctx.enter_context(nc.sbuf_tensor(n, s, d))
            self.ident = sb("ident", [P, P])
            self.x = sb("x", [P, NC, D])
            self.h = sb("h", [P, NC * D])
            self.scores = sb("scores", [P, (NC * H + 2) * 2 * NKEY])
            self.arena = sb("arena", [P, RING * 2 * D])
            self.misc = sb("misc", [P, 2816])
            self.small = sb("small", [P, 384])
            self.bank = [ctx.enter_context(nc.psum_tensor(f"bank{i}", [P, 512], F32)) for i in range(8)]
            self.loaded_x = self.lasting_sem("loaded_x")
            self.adaln()
            self.layer(0)
            self.layer(1)
            self.finish()

    @phase
    def adaln(self):
        nc, d, v = self.nc, self.dram, self.view
        slots = v(self.arena, 0, ADA_SLOTS, KD * ADA_CHUNK)
        rows = self.arena[0:2, 16384:16384 + LAYERS * MODW]
        bias = self.scores[0:2, 0:MODW]
        gains = self.h[0:2, 0:2 * LAYERS * D]
        cols, cs = v(self.small, 0, KD, 2), v(self.small, 16, KD, 2)
        sem = self.sem
        loaded_c, loaded_bias, silu_done = sem("loaded_c"), sem("loaded_bias"), sem("silu_done")
        w_loaded = [sem(f"w_loaded{s}") for s in range(ADA_SLOTS)]
        w_free, mm_done, bank_free, dve, stored = sem("w_free"), sem("mm_done"), sem("bank_free"), sem("dve_step"), sem("stored")
        bias_used, bias1_loaded = sem("bias_used"), sem("bias1_loaded")
        per_layer = MODW // ADA_CHUNK
        rounds = per_layer // ADA_SLOTS
        self.modd = nc.dram_tensor("mod_rows", (2, LAYERS * MODW), F32, kind="Internal").ap()
        with nc.Block() as block:
            @block.sync
            def _(sp):
                sp.dma_start(cols, d["c_cols"]).then_inc(loaded_c, 16)
                with sp.Fori(0, LAYERS * rounds) as it:
                    for s in range(ADA_SLOTS):
                        sp.wait_ge(w_free, it * ADA_SLOTS + s + 1)
                        sp.dma_start(slots[:, s, :], d["ada"][bass.ds(it * ADA_SLOTS + s, 1), :, :].rearrange("a p n -> p (a n)")).then_inc(w_loaded[s], 16)
                sp.wait_ge(dve, 4)
                sp.dma_start(self.modd, rows).then_inc(stored, 16)
                sp.wait_ge(stored, 16)

            @block.scalar
            def _(act):
                act.dma_start(bias, d["ada_b"][0]).then_inc(loaded_bias, 16)
                act.dma_start(gains, d["gains"]).then_inc(loaded_bias, 16)
                act.dma_start(self.ident[:], d["ident"]).then_inc(self.loaded_x, 16)
                act.dma_start(self.x[:], d["tokens"]).then_inc(self.loaded_x, 16)
                act.wait_ge(loaded_c, 16)
                nc.scalar.activation(cs, cols, ACT.Silu).then_inc(silu_done, 1)
                act.wait_ge(bias_used, per_layer)
                act.dma_start(bias, d["ada_b"][1]).then_inc(bias1_loaded, 16)

            @block.tensor
            def _(pe):
                pe.wait_ge(silu_done, 1)
                pe.sem_inc(w_free, ADA_SLOTS)
                with pe.Fori(0, LAYERS * rounds) as it:
                    for s in range(ADA_SLOTS):
                        pe.wait_ge(w_loaded[s], it * 16 + 16)
                        pe.wait_ge(bank_free, it * ADA_SLOTS + s + 1)
                        for k in range(KD):
                            last = nc.tensor.matmul(self.bank[s][0:2, :], cs[:, k, :], slots[:, s, k * ADA_CHUNK:(k + 1) * ADA_CHUNK],
                                                    start=(k == 0), stop=(k == KD - 1))
                        last.then_inc(mm_done, 1)

            @block.vector
            def _(dve_e):
                dve_e.sem_inc(bank_free, ADA_SLOTS)
                for layer in range(LAYERS):
                    dve_e.wait_ge(loaded_bias if layer == 0 else bias1_loaded, 32 if layer == 0 else 16)
                    with dve_e.Fori(0, rounds) as it:
                        for s in range(ADA_SLOTS):
                            dve_e.wait_ge(mm_done, it * ADA_SLOTS + layer * per_layer + s + 1)
                            nc.vector.tensor_tensor(rows[:, bass.ds(it * (ADA_SLOTS * ADA_CHUNK) + layer * MODW + s * ADA_CHUNK, ADA_CHUNK)],
                                                    self.bank[s][0:2, :],
                                                    bias[:, bass.ds(it * (ADA_SLOTS * ADA_CHUNK) + s * ADA_CHUNK, ADA_CHUNK)],
                                                    ALU.add).then_inc(bank_free, 1)
                            dve_e.sem_inc(w_free, 1)
                    dve_e.wait_ge(bank_free, ADA_SLOTS + (layer + 1) * per_layer)
                    dve_e.sem_inc(bias_used, per_layer)
                    for n, seg in enumerate((SC_A, SC_F)):
                        r = rows[:, layer * MODW + seg * D:layer * MODW + (seg + 1) * D]
                        g = gains[:, (2 * layer + n) * D:(2 * layer + n + 1) * D]
                        nc.vector.scalar_tensor_tensor(out=r, in0=r, scalar=1.0, in1=g, op0=ALU.add, op1=ALU.mult).then_inc(dve, 1)

    @phase
    def norm(self, layer, seg_sh, seg_sc, chunks, prefetch=None):
        nc, v = self.nc, self.view
        bc = v(self.arena, 0, 4, D)
        hT = self.hT = v(self.arena, 4096, KD, TOK)
        junk = v(self.misc, 0, D)
        ssq, var, std, rstd = (v(self.small, 64 + 4 * i, NC) for i in range(4))
        sem = self.sem
        bc_loaded, sq_done, mean_done, sqrt_done, rstd_done = (sem(n) for n in ("bc_loaded", "sq_done", "mean_done", "sqrt_done", "rstd_done"))
        scaled, h_ready, t_done, t_copied = sem("scaled"), sem("h_ready"), sem("t_done"), sem("t_copied")
        first, n = chunks[0], len(chunks)
        base = layer * MODW
        with nc.Block() as block:
            @block.sync
            def _(sp):
                for kd in (LAT, CON):
                    for j, seg in enumerate((seg_sc, seg_sh)):
                        src = self.modd[kd:kd + 1, base + seg * D:base + (seg + 1) * D]
                        sp.dma_start(bc[:, 2 * kd + j, :], src.broadcast_to([P, D])).then_inc(bc_loaded, 16)
                if prefetch:
                    prefetch(sp)

            @block.scalar
            def _(act):
                act.wait_ge(self.loaded_x, 32)
                for i, c in enumerate(chunks):
                    if i:
                        act.wait_ge(sq_done, i)
                    nc.scalar.activation(junk, self.x[:, c, :], ACT.Square, accum_out=ssq[:, c:c + 1]).then_inc(sq_done, 1)
                act.wait_ge(mean_done, 1)
                nc.scalar.activation(std[:, first:], var[:, first:], ACT.Sqrt).then_inc(sqrt_done, 1)
                for i, c in enumerate(chunks):
                    for q in range(2):
                        act.wait_ge(t_done, 2 * i + q + 1)
                        nc.scalar.copy(hT[:, 4 * q:4 * q + 4, c * P:(c + 1) * P],
                                       self.bank[(2 * i + q) % 8][:].rearrange("p (a b) -> p a b", a=4)).then_inc(t_copied, 1)

            @block.vector
            def _(dve):
                dve.wait_ge(sq_done, n)
                nc.vector.tensor_scalar(var[:, first:], ssq[:, first:], 1.0 / D, EPS, ALU.mult, ALU.add).then_inc(mean_done, 1)
                dve.wait_ge(sqrt_done, 1)
                nc.vector.reciprocal(rstd[:, first:], std[:, first:]).then_inc(rstd_done, 1)
                dve.wait_ge(rstd_done, 1)
                dve.wait_ge(bc_loaded, 64)
                for i, c in enumerate(chunks):
                    hc = self.h[:, c * D:(c + 1) * D]
                    nc.vector.scalar_tensor_tensor(out=hc, in0=self.x[:, c, :], scalar=rstd[:, c:c + 1], in1=bc[:, 2 * kind(c), :],
                                                   op0=ALU.mult, op1=ALU.mult).then_inc(scaled, 1)
                    dve.wait_ge(scaled, i + 1)
                    nc.vector.tensor_tensor(hc, hc, bc[:, 2 * kind(c) + 1, :], ALU.add).then_inc(h_ready, 1)

            @block.tensor
            def _(pe):
                pe.wait_ge(self.loaded_x, 32)
                for i, c in enumerate(chunks):
                    pe.wait_ge(h_ready, i + 1)
                    for q in range(2):
                        for k in range(4):
                            kk = 4 * q + k
                            last = nc.tensor.transpose(self.bank[(2 * i + q) % 8][:, k * P:(k + 1) * P],
                                                       self.h[:, c * D + kk * P:c * D + (kk + 1) * P], self.ident[:])
                        last.then_inc(t_done, 1)

    def mla_weights(self, sp):
        v, d = self.view, self.dram
        self.w_in = v(self.arena, 8192, KD, 2 * HALF)
        self.rope_rows = v(self.arena, 14336, NC, 2 * ROPE)
        self.w_uq = v(self.arena, 19456, KQ, H * 256)
        self.w_uk = v(self.arena, 25600, KKV, H * P)
        self.w_uv = v(self.arena, 27648, KKV, H * P)
        self.rope_cols = v(self.arena, 14848, TOK)
        self.gcol = v(self.small, 80, 5)
        self.w_o = v(self.scores, 0, H, D)
        self.w_in_loaded, self.w_up_loaded, self.w_o_loaded = self.lasting_sem("w_in_loaded"), self.lasting_sem("w_up_loaded"), self.lasting_sem("w_o_loaded")
        sp.dma_start(self.w_in, d["w_in"]).then_inc(self.w_in_loaded, 16)
        sp.dma_start(self.rope_rows, d["rope_rows"]).then_inc(self.w_in_loaded, 16)
        sp.dma_start(self.gcol, d["gcol"]).then_inc(self.w_in_loaded, 16)
        sp.dma_start(self.w_uq, d["w_uq"]).then_inc(self.w_up_loaded, 16)
        sp.dma_start(self.w_uk, d["w_uk"]).then_inc(self.w_up_loaded, 16)
        sp.dma_start(self.w_uv, d["w_uv"]).then_inc(self.w_up_loaded, 16)
        sp.dma_start(self.rope_cols, d["rope_cols"]).then_inc(self.w_up_loaded, 16)
        sp.dma_start(self.w_o, d["w_o0"]).then_inc(self.w_o_loaded, 16)

    @phase
    def mla_in(self):
        nc, v, sem = self.nc, self.view, self.sem
        hT, rr = self.hT, self.rope_rows
        cT = self.cT = v(self.arena, 15360, 6, TOK)
        an = v(self.misc, 0, 2, 2 * HALF)
        kr = v(self.misc, 1536, 2, 2 * ROPE)
        junk = v(self.misc, 1792, 640)
        ssq, var, std, rstd = (v(self.small, 96 + 8 * i, NC, 2) for i in range(4))
        a_done, sq_done, mean_done, sqrt_done, rstd_done = (sem(n) for n in ("a_done", "sq_done", "mean_done", "sqrt_done", "rstd_done"))
        an_ready_a = sem("an_scaled")
        an_ready, kr_step, bank_free, t_done, t_copied = (sem(n) for n in ("an_ready", "kr_step", "bank_free", "t_done", "t_copied"))
        with nc.Block() as block:
            @block.tensor
            def _(pe):
                pe.wait_ge(self.w_in_loaded, 48)

                def project(c):
                    for half in range(2):
                        if c >= 2:
                            pe.wait_ge(bank_free, c - 1)
                        for k in range(KD):
                            last = nc.tensor.matmul(self.bank[2 * (c % 2) + half][:, 0:HALF], hT[:, k, c * P:(c + 1) * P],
                                                    self.w_in[:, k, half * HALF:(half + 1) * HALF], start=(k == 0), stop=(k == KD - 1))
                        last.then_inc(a_done, 1)

                def transposes(c):
                    pe.wait_ge(an_ready, c + 1)
                    if c >= 1:
                        pe.wait_ge(t_copied, 6 * c)
                    for j in range(6):
                        last = nc.tensor.transpose(self.bank[4 + j // 3][:, (j % 3) * P:(j % 3 + 1) * P], an[:, c % 2, j * P:(j + 1) * P], self.ident[:])
                        if j % 3 == 2:
                            last.then_inc(t_done, 1)

                for c in range(NC):
                    project(c)
                    if c:
                        transposes(c - 1)
                transposes(NC - 1)

            @block.scalar
            def _(act):
                for c in range(NC):
                    act.wait_ge(a_done, 2 * c + 2)
                    b = self.bank[2 * (c % 2)], self.bank[2 * (c % 2) + 1]
                    if c:
                        act.wait_ge(sq_done, 2 * c)
                    nc.scalar.activation(junk[:, 0:QR], b[0][:, 0:QR], ACT.Square, accum_out=ssq[:, c, 0:1]).then_inc(sq_done, 1)
                    nc.scalar.activation(junk[:, QR:QR + KVR], b[1][:, 0:KVR], ACT.Square, accum_out=ssq[:, c, 1:2]).then_inc(sq_done, 1)
                    act.wait_ge(mean_done, 2 * c + 2)
                    nc.scalar.activation(std[:, c, :], var[:, c, :], ACT.Sqrt).then_inc(sqrt_done, 1)
                    act.wait_ge(rstd_done, c + 1)
                    if c >= 2:
                        act.wait_ge(t_done, 2 * (c - 1))
                    nc.scalar.mul(an[:, c % 2, 0:QR], b[0][:, 0:QR], rstd[:, c, 0:1]).then_inc(an_ready_a, 1)
                    nc.scalar.mul(an[:, c % 2, QR:QR + KVR], b[1][:, 0:KVR], rstd[:, c, 1:2]).then_inc(an_ready_a, 1)

            @block.vector
            def _(dve):
                step = 0
                for c in range(NC):
                    b1 = self.bank[2 * (c % 2) + 1]
                    dve.wait_ge(sq_done, 2 * c + 2)
                    for j, width in enumerate((QR, KVR)):
                        nc.vector.tensor_scalar(var[:, c, j:j + 1], ssq[:, c, j:j + 1], 1.0 / width, EPS, ALU.mult, ALU.add).then_inc(mean_done, 1)
                    if c >= 1:
                        dve.wait_ge(kr_step, step)
                    if c >= 2:
                        dve.wait_ge(t_done, 2 * (c - 1))
                    dst = an[:, c % 2, QR + KVR:QR + KVR + ROPE]
                    nc.vector.tensor_tensor(kr[:, 0, 0:ROPE], b1[:, KVR:KVR + ROPE], rr[:, c, 0:ROPE], ALU.mult).then_inc(kr_step, 1)
                    nc.vector.tensor_tensor(kr[:, 1, 0:ROPE], b1[:, KVR + ROPE:KVR + 2 * ROPE], rr[:, c, ROPE:2 * ROPE], ALU.mult).then_inc(kr_step, 1)
                    dve.wait_ge(kr_step, step + 2)
                    nc.vector.tensor_tensor(dst, kr[:, 0, 0:ROPE], kr[:, 1, 0:ROPE], ALU.add).then_inc(kr_step, 1)
                    dve.wait_ge(kr_step, step + 3)
                    nc.vector.tensor_copy(an[:, c % 2, QR + KVR + ROPE:2 * HALF], dst).then_inc(kr_step, 1)
                    step += 4
                    dve.wait_ge(sqrt_done, c + 1)
                    nc.vector.reciprocal(rstd[:, c, :], std[:, c, :]).then_inc(rstd_done, 1)
                    dve.wait_ge(an_ready_a, 2 * c + 2)
                    dve.wait_ge(kr_step, step)
                    dve.sem_inc(an_ready, 1)
                    dve.sem_inc(bank_free, 1)
                    for j in range(6):
                        dve.wait_ge(t_done, 2 * c + j // 3 + 1)
                        src, dst = self.bank[4 + j // 3][:, (j % 3) * P:(j % 3 + 1) * P], cT[:, j, c * P:(c + 1) * P]
                        if j < 5:
                            nc.vector.tensor_scalar(dst, src, self.gcol[:, j:j + 1], None, ALU.mult).then_inc(t_copied, 1)
                        else:
                            nc.vector.tensor_copy(dst, src).then_inc(t_copied, 1)

    def attention(self, chunks, keys_of, v_rows, v_tiles_of, score_terms, scale, head_proj=None, pre=None):
        nc, v, sem = self.nc, self.view, self.sem
        probs = v(self.misc, 0, 2, TOK)
        pT = v(self.misc, 1024, 2, TOK)
        OT = self.OT = v(self.h, 0, H, TOK)
        nmax, nbias, rsum, rinv = (v(self.small, 128 + 32 * i, 32) for i in range(4))
        s_done, mx, mx_done, exp_done, rinv_done, p_ready, pt_done, pt_copied, pv_done, o_done, o_copied = (
            sem(n) for n in ("s_done", "mx", "mx_done", "exp_done", "rinv_done", "p_ready", "pt_done", "pt_copied", "pv_done", "o_done", "o_copied"))
        proj_done, proj_copied = sem("proj_done"), sem("proj_copied")
        nch = len(chunks)
        units = [(hd, c) for hd in range(H) for c in chunks]
        U = len(units)
        S_BANK, T_BANK, O_BANK = (3, 4), (5, 6), 7
        lo, hi = chunks[0] * P, (chunks[-1] + 1) * P

        with nc.Block() as block:
            @block.tensor
            def _(pe):
                if pre:
                    pre("pe", pe)
                def proj(hd):
                    if hd:
                        pe.wait_ge(proj_copied, 3 * hd)
                    head_proj("pe", pe, hd, proj_done)

                def scores(u):
                    hd, c = units[u]
                    if head_proj:
                        pe.wait_ge(proj_copied, 3 * hd + 3)
                    if u >= 2:
                        pe.wait_ge(exp_done, u - 1)
                    terms = score_terms(hd, c)
                    for i, (q, k) in enumerate(terms):
                        last = nc.tensor.matmul(self.bank[S_BANK[u % 2]][:, 0:keys_of(c)], q, k, start=(i == 0), stop=(i == len(terms) - 1))
                    last.then_inc(s_done, 1)

                def transposes(u):
                    c = units[u][1]
                    pe.wait_ge(p_ready, u + 1)
                    if u >= 2:
                        pe.wait_ge(pt_copied, u - 1)
                    for t in range(keys_of(c) // P):
                        last = nc.tensor.transpose(self.bank[T_BANK[u % 2]][:, t * P:(t + 1) * P], probs[:, u % 2, t * P:(t + 1) * P], self.ident[:])
                    last.then_inc(pt_done, 1)

                def values(u):
                    hd, c = units[u]
                    pe.wait_ge(pt_copied, u + 1)
                    if u % nch == 0 and hd:
                        pe.wait_ge(o_copied, hd)
                    n = keys_of(c) // P
                    for t in range(n):
                        last = nc.tensor.matmul(self.bank[O_BANK][:, c * P:(c + 1) * P], v_rows(hd, t), pT[:, u % 2, t * P:(t + 1) * P],
                                                start=(t == 0), stop=(t == n - 1))
                    last.then_inc(pv_done, 1)

                if head_proj:
                    proj(0)
                for u in range(U + 2):
                    if u < U:
                        scores(u)
                        if head_proj and u % nch == 1 and units[u][0] + 1 < H:
                            proj(units[u][0] + 1)
                    if 1 <= u <= U:
                        transposes(u - 1)
                    if u >= 2:
                        values(u - 2)

            @block.scalar
            def _(act):
                if pre:
                    pre("act", act)

                def exps(u):
                    c = units[u][1]
                    act.wait_ge(mx_done, u + 1)
                    if u >= 2:
                        act.wait_ge(pt_done, u - 1)
                    nc.scalar.activation(probs[:, u % 2, 0:keys_of(c)], self.bank[S_BANK[u % 2]][:, 0:keys_of(c)], ACT.Exp,
                                         bias=nbias[:, u:u + 1], scale=scale, accum_out=rsum[:, u:u + 1]).then_inc(exp_done, 1)

                def copy_pt(u):
                    c = units[u][1]
                    act.wait_ge(pt_done, u + 1)
                    if u >= 2:
                        act.wait_ge(pv_done, u - 1)
                    nc.scalar.copy(pT[:, u % 2, 0:keys_of(c)], self.bank[T_BANK[u % 2]][:, 0:keys_of(c)]).then_inc(pt_copied, 1)

                if head_proj:
                    head_proj("act", act, 0, proj_copied, proj_done, s_done)
                for u in range(U + 1):
                    if u < U:
                        exps(u)
                        if head_proj and u % nch == 1 and units[u][0] + 1 < H:
                            head_proj("act", act, units[u][0] + 1, proj_copied, proj_done, s_done)
                    if u >= 1:
                        copy_pt(u - 1)

            @block.vector
            def _(dve):
                if pre:
                    pre("dve", dve)

                def maxima(u):
                    c = units[u][1]
                    dve.wait_ge(s_done, u + 1)
                    nc.vector.tensor_reduce(nmax[:, u:u + 1], self.bank[S_BANK[u % 2]][:, 0:keys_of(c)], AX.X, ALU.max, negate=True).then_inc(mx, 1)
                    dve.wait_ge(mx, u + 1)
                    nc.vector.tensor_scalar(nbias[:, u:u + 1], nmax[:, u:u + 1], scale, None, ALU.mult).then_inc(mx_done, 1)

                def normalise(u):
                    c = units[u][1]
                    dve.wait_ge(exp_done, u + 1)
                    nc.vector.reciprocal(rinv[:, u:u + 1], rsum[:, u:u + 1]).then_inc(rinv_done, 1)
                    dve.wait_ge(rinv_done, u + 1)
                    pr = probs[:, u % 2, 0:keys_of(c)]
                    nc.vector.tensor_scalar(pr, pr, rinv[:, u:u + 1], None, ALU.mult).then_inc(p_ready, 1)

                def copy_out(hd):
                    dve.wait_ge(pv_done, nch * (hd + 1))
                    nc.vector.tensor_copy(OT[:, hd, lo:hi], self.bank[O_BANK][:, lo:hi]).then_inc(o_copied, 1)

                if head_proj:
                    head_proj("dve", dve, 0, proj_copied, proj_done, s_done)
                for u in range(U + 1):
                    if u < U:
                        maxima(u)
                        if head_proj and u % nch == 1 and units[u][0] + 1 < H:
                            head_proj("dve", dve, units[u][0] + 1, proj_copied, proj_done, s_done)
                    if u >= 1:
                        normalise(u - 1)
                    if u > nch and (u - 1) % nch == 0:
                        copy_out((u - 1) // nch - 1)
                if nch > 1:
                    copy_out(H - 1)

    @phase
    def mla_attention(self):
        nc, v = self.nc, self.view
        cT = self.cT
        V = v(self.arena, 0, NC, D)
        qn, qr, kn = (v(self.arena, 4096 + 1024 * i, 2, TOK) for i in range(3))
        v_done, v_copied = self.sem("v_done"), self.sem("v_copied")

        def pre(who, eng):
            if who == "pe":
                eng.wait_ge(self.w_up_loaded, 64)
                for c in range(NC):
                    for n in range(2):
                        for k in range(KKV):
                            last = nc.tensor.matmul(self.bank[2 * c + n][:], cT[:, KQ + k, c * P:(c + 1) * P], self.w_uv[:, k, n * 512:(n + 1) * 512],
                                                    start=(k == 0), stop=(k == KKV - 1))
                        last.then_inc(v_done, 1)
                eng.wait_ge(v_copied, 8)
            if who == "act":
                for i in range(0, 8, 2):
                    eng.wait_ge(v_done, i + 1)
                    nc.scalar.copy(V[:, i // 2, 0:512], self.bank[i][:]).then_inc(v_copied, 1)
            if who == "dve":
                for i in range(1, 8, 2):
                    eng.wait_ge(v_done, i + 1)
                    nc.vector.tensor_copy(V[:, i // 2, 512:1024], self.bank[i][:]).then_inc(v_copied, 1)

        def head_proj(who, eng, hd, *sems):
            if who == "pe":
                done, = sems
                for j in range(3):
                    src, w, tiles = [(0, self.w_uq[:, :, hd * 256:hd * 256 + 128], KQ), (0, self.w_uq[:, :, hd * 256 + 128:hd * 256 + 256], KQ),
                                     (KQ, self.w_uk[:, :, hd * P:(hd + 1) * P], KKV)][j]
                    for k in range(tiles):
                        last = nc.tensor.matmul(self.bank[j][:], w[:, k, :], cT[:, src + k, :], start=(k == 0), stop=(k == tiles - 1))
                    last.then_inc(done, 1)
                return
            copied, done, s_done = sems
            if hd >= 2:
                eng.wait_ge(s_done, NC * (hd - 1))
            if who == "act":
                for j, dst in ((0, qn), (2, kn)):
                    eng.wait_ge(done, 3 * hd + j + 1)
                    nc.scalar.copy(dst[:, hd % 2, :], self.bank[j][:]).then_inc(copied, 1)
            else:
                eng.wait_ge(done, 3 * hd + 2)
                nc.vector.tensor_tensor(qr[:, hd % 2, :], self.bank[1][:], self.rope_cols, ALU.mult).then_inc(copied, 1)

        self.attention(
            list(range(NC)), lambda c: CTX if c < CC else TOK, lambda hd, t: V[:, t, hd * P:(hd + 1) * P], None,
            lambda hd, c: [(qn[:, hd % 2, c * P:(c + 1) * P], kn[:, hd % 2, 0:CTX if c < CC else TOK]),
                           (qr[:, hd % 2, c * P:(c + 1) * P], cT[:, 5, 0:CTX if c < CC else TOK])],
            1.0 / math.sqrt(NOPE + ROPE), head_proj, pre)

    @phase
    def out_proj(self, layer, chunks, prefetch=None):
        nc, v, sem = self.nc, self.view, self.sem
        gate = v(self.arena, 0, 2, D)
        y = v(self.misc, 0, 2, 512)
        g_loaded, y_done, gated, added = sem("g_loaded"), sem("y_done"), sem("gated"), sem("added")
        with nc.Block() as block:
            @block.sync
            def _(sp):
                for kd in (LAT, CON):
                    seg = layer * MODW + G_A * D
                    sp.dma_start(gate[:, kd, :], self.modd[kd:kd + 1, seg:seg + D].broadcast_to([P, D])).then_inc(g_loaded, 16)
                if prefetch:
                    prefetch(sp)

            @block.tensor
            def _(pe):
                pe.wait_ge(self.w_o_loaded, 16)
                for i, c in enumerate(chunks):
                    for n in range(2):
                        for hd in range(H):
                            last = nc.tensor.matmul(self.bank[2 * i + n][:], self.OT[:, hd, c * P:(c + 1) * P], self.w_o[:, hd, n * 512:(n + 1) * 512],
                                                    start=(hd == 0), stop=(hd == H - 1))
                        last.then_inc(y_done, 1)

            @block.vector
            def _(dve):
                dve.wait_ge(g_loaded, 32)
                for i, c in enumerate(chunks):
                    for n in range(2):
                        u = 2 * i + n
                        dve.wait_ge(y_done, u + 1)
                        if u >= 2:
                            dve.wait_ge(added, u - 1)
                        nc.vector.tensor_tensor(y[:, n, :], self.bank[u][:], gate[:, kind(c), n * 512:(n + 1) * 512], ALU.mult).then_inc(gated, 1)
                        dve.wait_ge(gated, u + 1)
                        xs = self.x[:, c, n * 512:(n + 1) * 512]
                        nc.vector.tensor_tensor(xs, xs, y[:, n, :], ALU.add).then_inc(added, 1)

    @phase
    def peer_scores(self, layer, chunks):
        nc, v, sem = self.nc, self.view, self.sem
        SL = 8
        wq = v(self.arena, 8192, SL, KD * P)
        keys = v(self.arena, 16384, 2 * H, NKEY)
        qT = v(self.arena, 18432, 2, TOK)
        w_loaded = [sem(f"wq_loaded{s}") for s in range(SL)]
        k_loaded, q_done, q_copied, sc_done, sc_copied, pad = (sem(n) for n in ("k_loaded", "q_done", "q_copied", "sc_done", "sc_copied", "pad"))
        nch = len(chunks)
        lo, hi = chunks[0] * P, (chunks[-1] + 1) * P
        sc = self.scores[:, 0:nch * H * 2 * NKEY].rearrange("p (c j n) -> p c j n", c=nch, j=2 * H)
        with nc.Block() as block:
            @block.sync
            def _(sp):
                sp.dma_start(keys, self.dram["keys"][layer]).then_inc(k_loaded, 16)
                for j in range(2 * H):
                    if j >= SL:
                        sp.wait_ge(q_done, j - SL + 1)
                    sp.dma_start(wq[:, j % SL, :], self.dram["w_query"][layer, j]).then_inc(w_loaded[j % SL], 16)

            @block.tensor
            def _(pe):
                def query(j):
                    pe.wait_ge(w_loaded[j % SL], 16 * (j // SL + 1))
                    if j >= 2:
                        pe.wait_ge(q_copied, j - 1)
                    for k in range(KD):
                        last = nc.tensor.matmul(self.bank[j % 2][:, lo:hi], wq[:, j % SL, k * P:(k + 1) * P], self.hT[:, k, lo:hi], start=(k == 0), stop=(k == KD - 1))
                    last.then_inc(q_done, 1)

                def score(j):
                    pe.wait_ge(q_copied, j + 1)
                    if j >= 2:
                        pe.wait_ge(sc_copied, j - 1)
                    for i, c in enumerate(chunks):
                        last = nc.tensor.matmul(self.bank[2 + j % 2][:, i * NKEY:(i + 1) * NKEY], qT[:, j % 2, c * P:(c + 1) * P], keys[:, j, :], start=True, stop=True)
                    last.then_inc(sc_done, 1)

                pe.wait_ge(k_loaded, 16)
                for j in range(2 * H + 1):
                    if j < 2 * H:
                        query(j)
                    if j:
                        score(j - 1)

            @block.scalar
            def _(act):
                for j in range(2 * H):
                    act.wait_ge(q_done, j + 1)
                    if j >= 2:
                        act.wait_ge(sc_done, j - 1)
                    nc.scalar.copy(qT[:, j % 2, lo:hi], self.bank[j % 2][:, lo:hi]).then_inc(q_copied, 1)

            @block.vector
            def _(dve):
                nc.vector.memset(self.scores[:, nch * H * 2 * NKEY:(nch * H + 2) * 2 * NKEY], 0.0).then_inc(pad, 1)
                for j in range(2 * H):
                    dve.wait_ge(sc_done, j + 1)
                    nc.vector.tensor_copy(sc[:, :, j, :], self.bank[2 + j % 2][:, 0:nch * NKEY].rearrange("p (c n) -> p c n", c=nch)).then_inc(sc_copied, 1)

    @phase
    def peer(self, layer, chunks):
        nc, v, sem = self.nc, self.view, self.sem
        nch, first = len(chunks), chunks[0]
        ring = v(self.arena, 0, RING, 2 * D)
        diag = v(self.misc, 0, 2 * GRP, P)
        hcur = v(self.misc, 1024, D)
        S = v(self.misc, 2048, 2 * NKEY)
        C = v(self.misc, 2304, TOPK, TOPK)
        OH = v(self.misc, 2560, TOPK, TOPK)
        sm = self.small
        val = v(sm, 0, 2, TOPK)
        ind = v(sm, 32, 2, TOPK, dtype=U32)
        indf = v(sm, 64, 2, TOPK)
        top = v(sm, 96, TOPK)
        pos = v(sm, 112, TOPK, dtype=U32)
        posi = v(sm, 128, 2, TOPK, dtype=U32)
        sel = v(sm, 160, 2, TOPK)
        idx = v(sm, 192, 2, TOPK, dtype=I32)
        gate = v(sm, 224, 2, TOPK)
        a = v(sm, 256, 2, TOPK)
        w = v(sm, 288, 2, TOPK)
        iota = v(sm, 320, TOPK)
        iota_i = v(sm, 336, TOPK, dtype=I32)
        nb, es, er = sm[:, 352:353], sm[:, 354:355], sm[:, 356:357]
        units = nch * H
        gathered = [sem(f"gathered{k}") for k in range(RING)]
        slots_free, token, idx_ready, dots_done, gelu_done, w_ready, diag_ready = (
            sem(n) for n in ("slots_free", "token", "idx_ready", "dots_done", "gelu_done", "w_ready", "diag_ready"))
        acc_done, acc_free, chain, top_ready, exp_done, iota_done, hc_done, seeded = (
            sem(n) for n in ("acc_done", "acc_free", "chain", "top_ready", "exp_done", "iota_done", "hc_done", "seeded"))
        table = self.dram["uv"][layer]
        acc = self.bank[0], self.bank[1]
        zero_w, zero_x = self.zero[:], self.zero[:].unsqueeze(1).broadcast_to([P, 4, P])

        with nc.Block() as block:
            @block.gpsimd
            def _(pool):
                nc.gpsimd.iota(iota_i, pattern=[[1, TOPK]], base=0, channel_multiplier=0).then_inc(iota_done, 1)
                with pool.Fori(0, units // 2) as it:
                    for u in range(2):
                        pool.wait_ge(idx_ready, it * 2 + u + 1)
                        pool.sem_inc(token, 1)
                        for g in range(NG):
                            pool.wait_ge(slots_free, it * (2 * NG) + u * NG + g + 1)
                            pool.sem_inc(token, 1)
                            for k in range(g * GRP, (g + 1) * GRP):
                                nc.gpsimd.indirect_dma_start(
                                    out=ring[:, k, :], out_offset=None, in_=table,
                                    in_offset=bass.IndirectOffsetOnAxis(ap=idx[:, u, k:k + 1], axis=0)).then_inc(gathered[k], 16)

            @block.tensor
            def _(pe):
                pe.sem_inc(slots_free, NG)
                with pe.Fori(0, nch) as c:
                    pe.wait_ge(acc_free, c + 1)
                    for n in range(2):
                        nc.tensor.matmul(acc[n][:], zero_w, zero_x, start=True, stop=False)
                    with pe.Fori(0, H // 2) as it:
                        for u in range(2):
                            for g in range(NG):
                                pe.wait_ge(diag_ready, c * (H * NG) + it * (2 * NG) + u * NG + g + 1)
                                for k in range(GRP):
                                    for n in range(2):
                                        last = nc.tensor.matmul(acc[n][:], diag[:, (g % 2) * GRP + k, :], ring[:, g * GRP + k, D + n * 512:D + (n + 1) * 512],
                                                                start=False, stop=False)
                                last.then_inc(slots_free, 1)
                    for n in range(2):
                        last = nc.tensor.matmul(acc[n][:], zero_w, zero_x, start=False, stop=True)
                    last.then_inc(acc_done, 1)

            @block.scalar
            def _(act):
                act.sem_inc(acc_free, 1)
                act.wait_ge(top_ready, 1)
                nc.scalar.activation(gate[:, 0, :], top, ACT.Exp, bias=nb, accum_out=es).then_inc(exp_done, 1)
                act.wait_ge(top_ready, 2)
                nc.scalar.activation(gate[:, 1, :], top, ACT.Exp, bias=nb, accum_out=es).then_inc(exp_done, 1)
                with act.Fori(0, nch) as c:
                    with act.Fori(0, H // 2) as it:
                        for u in range(2):
                            for g in range(NG):
                                n = c * (H * NG) + it * (2 * NG) + u * NG + g
                                act.wait_ge(dots_done, n + 1)
                                ks = slice(g * GRP, (g + 1) * GRP)
                                nc.scalar.activation(w[:, u, ks], a[:, u, ks], ACT.Gelu).then_inc(gelu_done, 1)
                                act.wait_ge(w_ready, n + 1)
                                act.wait_ge(slots_free, n + 3)
                                for k in range(GRP):
                                    last = nc.scalar.mul(diag[:, (g % 2) * GRP + k, :], self.ident[:], w[:, u, g * GRP + k:g * GRP + k + 1])
                                last.then_inc(diag_ready, 1)
                            act.wait_ge(top_ready, c * H + it * 2 + u + 3)
                            nc.scalar.activation(gate[:, u, :], top, ACT.Exp, bias=nb, accum_out=es).then_inc(exp_done, 1)
                    act.wait_ge(acc_done, c + 1)
                    for n in range(2):
                        last = nc.scalar.copy(self.h[:, bass.ds(c * D + first * D + n * 512, 512)], acc[n][:])
                    last.then_inc(acc_free, 1)

            @block.vector
            def _(dve):
                count = [0]

                def link(ins):
                    count[0] += 1
                    ins.then_inc(chain, 1)
                    dve.wait_ge(chain, count[0])

                def restart():
                    dve.sem_clear(chain)
                    count[0] = 0

                def top16(values, out_v, out_i, src):
                    link(nc.vector.max(out_v[:, 0:8], src))
                    link(nc.vector.max_index(out_i[:, 0:8], out_v[:, 0:8], src))
                    link(nc.vector.match_replace(src, out_v[:, 0:8], src, NEG))
                    link(nc.vector.max(out_v[:, 8:16], src))
                    link(nc.vector.max_index(out_i[:, 8:16], out_v[:, 8:16], src))

                def choose(unit, u):
                    link(nc.vector.tensor_copy(S, self.scores[:, bass.ds(unit * (2 * NKEY), 2 * NKEY)]))
                    for side in range(2):
                        top16(None, val[:, side, :], ind[:, side, :], S[:, side * NKEY:(side + 1) * NKEY])
                    link(nc.vector.tensor_copy(indf, ind))
                    link(nc.vector.tensor_tensor(C, val[:, 0, :].unsqueeze(2).broadcast_to([P, TOPK, TOPK]),
                                                 val[:, 1, :].unsqueeze(1).broadcast_to([P, TOPK, TOPK]), ALU.add))
                    top16(None, top, pos, C.rearrange("p a b -> p (a b)"))
                    link(nc.vector.tensor_scalar(posi[:, 0, :], pos, 4, None, ALU.logical_shift_right))
                    link(nc.vector.tensor_scalar(posi[:, 1, :], pos, TOPK - 1, None, ALU.bitwise_and))
                    for side in range(2):
                        link(nc.vector.tensor_tensor(OH, posi[:, side, :].unsqueeze(2).broadcast_to([P, TOPK, TOPK]),
                                                     iota.unsqueeze(1).broadcast_to([P, TOPK, TOPK]), ALU.is_equal))
                        link(nc.vector.tensor_tensor(OH, OH, indf[:, side, :].unsqueeze(1).broadcast_to([P, TOPK, TOPK]), ALU.mult))
                        link(nc.vector.tensor_reduce(sel[:, side, :], OH, AX.X, ALU.add))
                    link(nc.vector.scalar_tensor_tensor(out=idx[:, u, :], in0=sel[:, 0, :], scalar=float(NKEY), in1=sel[:, 1, :], op0=ALU.mult, op1=ALU.add))
                    dve.sem_inc(idx_ready, 1)
                    link(nc.vector.tensor_scalar(nb, top[:, 0:1], -1.0, None, ALU.mult))
                    dve.sem_inc(top_ready, 1)

                def finish_gates(u):
                    link(nc.vector.reciprocal(er, es))
                    link(nc.vector.tensor_scalar(gate[:, u, :], gate[:, u, :], er, None, ALU.mult))

                dve.wait_ge(iota_done, 1)
                link(nc.vector.tensor_copy(iota, iota_i))
                for u in range(2):
                    choose(u, u)
                    dve.wait_ge(exp_done, u + 1)
                    finish_gates(u)
                restart()
                with dve.Fori(0, nch) as c:
                    link(nc.vector.tensor_copy(hcur, self.h[:, bass.ds(c * D + first * D, D)]))
                    restart()
                    with dve.Fori(0, H // 2) as it:
                        for u in range(2):
                            unit = c * H + it * 2 + u
                            for g in range(NG):
                                for k in range(g * GRP, (g + 1) * GRP):
                                    dve.wait_ge(gathered[k], unit * 16 + 16)
                                    last = nc.vector.tensor_tensor_reduce(out=ring[:, k, 0:D], in0=ring[:, k, 0:D], in1=hcur, scale=1.0, scalar=0.0,
                                                                          op0=ALU.mult, op1=ALU.add, accum_out=a[:, u, k:k + 1])
                                last.then_inc(dots_done, 1)
                                ks = slice(g * GRP, (g + 1) * GRP)
                                dve.wait_ge(gelu_done, unit * NG + g + 1)
                                nc.vector.tensor_tensor(w[:, u, ks], w[:, u, ks], gate[:, u, ks], ALU.mult).then_inc(w_ready, 1)
                            choose(unit + 2, u)
                            dve.wait_ge(exp_done, unit + 3)
                            finish_gates(u)
                            restart()

    @phase
    def peer_add(self, layer, chunks):
        nc, v, sem = self.nc, self.view, self.sem
        gate = v(self.arena, 0, 2, D)
        g_loaded, gated, added = sem("g_loaded"), sem("gated"), sem("added")
        with nc.Block() as block:
            @block.sync
            def _(sp):
                for kd in (LAT, CON):
                    seg = layer * MODW + G_F * D
                    sp.dma_start(gate[:, kd, :], self.modd[kd:kd + 1, seg:seg + D].broadcast_to([P, D])).then_inc(g_loaded, 16)

            @block.vector
            def _(dve):
                dve.wait_ge(g_loaded, 32)
                for i, c in enumerate(chunks):
                    y = self.h[:, c * D:(c + 1) * D]
                    nc.vector.tensor_tensor(y, y, gate[:, kind(c), :], ALU.mult).then_inc(gated, 1)
                    dve.wait_ge(gated, i + 1)
                    nc.vector.tensor_tensor(self.x[:, c, :], self.x[:, c, :], y, ALU.add).then_inc(added, 1)

    def gqa_weights(self, sp):
        v, d = self.view, self.dram
        self.w_qkv = v(self.arena, 8192, KD, (H + 2 * GKV) * P)
        self.rope_g = v(self.arena, 20480, NC, 2 * P)
        self.gain_g = v(self.arena, 21504, 2, P)
        self.w_o = v(self.scores, 0, H, D)
        self.w_qkv_loaded, self.w_o_loaded = self.lasting_sem("w_qkv_loaded"), self.lasting_sem("w_o_loaded")
        sp.dma_start(self.w_qkv, d["w_qkv"]).then_inc(self.w_qkv_loaded, 16)
        sp.dma_start(self.rope_g, d["rope_g"]).then_inc(self.w_qkv_loaded, 16)
        sp.dma_start(self.gain_g, d["gain_g"].broadcast_to([P, 2 * P]).rearrange("p (a b) -> p a b", a=2)).then_inc(self.w_qkv_loaded, 16)
        sp.dma_start(self.w_o, d["w_o1"]).then_inc(self.w_o_loaded, 16)

    @phase
    def gqa_in(self):
        nc, v, sem = self.nc, self.view, self.sem
        NQK = H + GKV
        V = self.gV = v(self.arena, 0, NC, GKV * P)
        qT = self.gqT = v(self.arena, 22528, H, TOK)
        kT = self.gkT = v(self.arena, 26624, GKV, TOK)
        n1 = v(self.arena, 27648, NQK, P)
        n2 = v(self.arena, 28928, NQK, P)
        n3 = v(self.arena, 30208, NQK, P)
        junk = v(self.misc, 0, NQK, P)
        ssq, var, std, rstd = (v(self.small, 128 + 40 * i, NC, NQK) for i in range(4))
        a_done, sq_done, chain, mean_done, sqrt_done, bank_free, r_ready, t_done, t_copied, v_copied = (
            sem(n) for n in ("a_done", "sq_done", "chain", "mean_done", "sqrt_done", "bank_free", "r_ready", "t_done", "t_copied", "v_copied"))

        def heads(c):
            return list(range(NQK)) if c >= CC else list(range(H, NQK))

        def src(c, j):
            b = self.bank[3 * (c % 2) + (2 if j >= H else j // 4)]
            return b[:, (j % 4 if j < H else j - H) * P:((j % 4 if j < H else j - H) + 1) * P]

        sq_before = [sum(len(heads(x)) for x in range(c)) for c in range(NC + 1)]
        t_before = [sum(3 if x >= CC else 1 for x in range(c)) for c in range(NC + 1)]

        with nc.Block() as block:
            @block.tensor
            def _(pe):
                pe.wait_ge(self.w_qkv_loaded, 48)

                def project(c):
                    if c >= 2:
                        pe.wait_ge(bank_free, c - 1)
                    for n in ((0, 1, 2) if c >= CC else (2,)):
                        for k in range(KD):
                            last = nc.tensor.matmul(self.bank[3 * (c % 2) + n][:], self.hT[:, k, c * P:(c + 1) * P], self.w_qkv[:, k, n * 512:(n + 1) * 512],
                                                    start=(k == 0), stop=(k == KD - 1))
                    last.then_inc(a_done, 1)

                def transposes(c):
                    pe.wait_ge(r_ready, c + 1)
                    groups = ([list(range(0, 4)), list(range(4, 8))] if c >= CC else []) + [[8, 9]]
                    for i, g in enumerate(groups):
                        n = t_before[c] + i
                        if n >= 2:
                            pe.wait_ge(t_copied, n - 1)
                        for jj, j in enumerate(g):
                            last = nc.tensor.transpose(self.bank[6 + n % 2][:, jj * P:(jj + 1) * P], n3[:, j, :], self.ident[:])
                        last.then_inc(t_done, 1)

                for c in range(NC):
                    project(c)
                    if c:
                        transposes(c - 1)
                transposes(NC - 1)

            @block.scalar
            def _(act):
                for c in range(NC):
                    act.wait_ge(a_done, c + 1)
                    if c:
                        act.wait_ge(sq_done, sq_before[c])
                    for j in heads(c):
                        nc.scalar.activation(junk[:, j, :], src(c, j), ACT.Square, accum_out=ssq[:, c, j:j + 1]).then_inc(sq_done, 1)
                    nc.scalar.copy(V[:, c, :], self.bank[3 * (c % 2) + 2][:, GKV * P:2 * GKV * P]).then_inc(v_copied, 1)
                    act.wait_ge(mean_done, c + 1)
                    j0 = heads(c)[0]
                    nc.scalar.activation(std[:, c, j0:], var[:, c, j0:], ACT.Sqrt).then_inc(sqrt_done, 1)

            @block.vector
            def _(dve):
                count = [0]

                def link(ins):
                    count[0] += 1
                    ins.then_inc(chain, 1)
                    dve.wait_ge(chain, count[0])

                for c in range(NC):
                    j0 = heads(c)[0]
                    nh = NQK - j0
                    dve.wait_ge(sq_done, sq_before[c + 1])
                    nc.vector.tensor_scalar(var[:, c, j0:], ssq[:, c, j0:], 1.0 / P, EPS, ALU.mult, ALU.add).then_inc(mean_done, 1)
                    dve.wait_ge(sqrt_done, c + 1)
                    link(nc.vector.reciprocal(rstd[:, c, j0:], std[:, c, j0:]))
                    for b, (lo, hi) in enumerate(((0, 4), (4, 8), (8, 10))):
                        if lo < j0:
                            continue
                        link(nc.vector.tensor_tensor(n1[:, lo:hi, :], self.bank[3 * (c % 2) + b][:, 0:(hi - lo) * P].rearrange("p (a b) -> p a b", b=P),
                                                     rstd[:, c, lo:hi].unsqueeze(2).broadcast_to([P, hi - lo, P]), ALU.mult))
                    dve.wait_ge(v_copied, c + 1)
                    dve.sem_inc(bank_free, 1)
                    for lo, hi, g in ((0, H, 0), (H, NQK, 1)):
                        if lo < j0:
                            continue
                        link(nc.vector.tensor_tensor(n1[:, lo:hi, :], n1[:, lo:hi, :], self.gain_g[:, g, :].unsqueeze(1).broadcast_to([P, hi - lo, P]), ALU.mult))
                    if c:
                        dve.wait_ge(t_done, t_before[c])
                    hs = slice(j0, NQK)
                    link(nc.vector.tensor_tensor(n3[:, hs, :], n1[:, hs, :], self.rope_g[:, c, 0:P].unsqueeze(1).broadcast_to([P, nh, P]), ALU.mult))
                    for b in range(4):
                        o = b ^ 1
                        link(nc.vector.tensor_tensor(n2[:, hs, 32 * b:32 * b + 32], n1[:, hs, 32 * o:32 * o + 32],
                                                     self.rope_g[:, c, P + 32 * b:P + 32 * b + 32].unsqueeze(1).broadcast_to([P, nh, 32]), ALU.mult))
                    link(nc.vector.tensor_tensor(n3[:, hs, :], n3[:, hs, :], n2[:, hs, :], ALU.add))
                    dve.sem_inc(r_ready, 1)
                    cols = slice(c * P, (c + 1) * P)
                    groups = ([(qT, 0, 4), (qT, 4, 4)] if c >= CC else []) + [(kT, 0, 2)]
                    for i, (dst, at, m) in enumerate(groups):
                        n = t_before[c] + i
                        dve.wait_ge(t_done, n + 1)
                        nc.vector.tensor_copy(dst[:, at:at + m, cols], self.bank[6 + n % 2][:, 0:m * P].rearrange("p (a b) -> p a b", b=P)).then_inc(t_copied, 1)

    @phase
    def gqa_attention(self):
        self.attention(
            list(range(CC, NC)), lambda c: TOK, lambda hd, t: self.gV[:, t, (hd // 4) * P:(hd // 4 + 1) * P], None,
            lambda hd, c: [(self.gqT[:, hd, c * P:(c + 1) * P], self.gkT[:, hd // 4, :])],
            1.0 / math.sqrt(P))

    def layer(self, i):
        every = list(range(NC))
        if i == 0:
            self.zero_operands()
            self.norm(0, SH_A, SC_A, every, self.mla_weights)
            self.mla_in()
            self.mla_attention()
            ffn = every
        else:
            self.norm(1, SH_A, SC_A, every, self.gqa_weights)
            self.gqa_in()
            self.gqa_attention()
            ffn = list(range(CC, NC))
        self.out_proj(i, ffn)
        self.norm(i, SH_F, SC_F, ffn)
        self.peer_scores(i, ffn)
        self.peer(i, ffn)
        self.peer_add(i, ffn)

    @phase
    def zero_operands(self):
        self.zero = self.ctx.enter_context(self.nc.sbuf_tensor("zero", [P, P], BF16))
        z = self.sem("zero_set")
        with self.nc.Block() as block:
            @block.vector
            def _(dve):
                self.nc.vector.memset(self.zero[:], 0.0).then_inc(z, 1)

    @phase
    def finish(self):
        nc, v, sem = self.nc, self.view, self.sem
        gain = v(self.arena, 0, D)
        junk = v(self.misc, 0, D)
        ssq, var, std, rstd = (v(self.small, 4 * i, CC) for i in range(4))
        g_loaded, sq_done, mean_done, sqrt_done, rstd_done, o_ready, stored = (
            sem(n) for n in ("g_loaded", "sq_done", "mean_done", "sqrt_done", "rstd_done", "o_ready", "stored"))
        with nc.Block() as block:
            @block.sync
            def _(sp):
                sp.dma_start(gain, self.dram["norm_out"].broadcast_to([P, D])).then_inc(g_loaded, 16)
                for i in range(2):
                    sp.wait_ge(o_ready, i + 1)
                    sp.dma_start(self.out[0, i * P:(i + 1) * P, :], self.h[:, i * D:(i + 1) * D]).then_inc(stored, 16)
                sp.wait_ge(stored, 32)

            @block.scalar
            def _(act):
                for i in range(2):
                    if i:
                        act.wait_ge(sq_done, i)
                    nc.scalar.activation(junk, self.x[:, CC + i, :], ACT.Square, accum_out=ssq[:, i:i + 1]).then_inc(sq_done, 1)
                act.wait_ge(mean_done, 1)
                nc.scalar.activation(std, var, ACT.Sqrt).then_inc(sqrt_done, 1)

            @block.vector
            def _(dve):
                dve.wait_ge(sq_done, 2)
                nc.vector.tensor_scalar(var, ssq, 1.0 / D, EPS, ALU.mult, ALU.add).then_inc(mean_done, 1)
                dve.wait_ge(sqrt_done, 1)
                nc.vector.reciprocal(rstd, std).then_inc(rstd_done, 1)
                dve.wait_ge(rstd_done, 1)
                dve.wait_ge(g_loaded, 16)
                for i in range(2):
                    nc.vector.scalar_tensor_tensor(out=self.h[:, i * D:(i + 1) * D], in0=self.x[:, CC + i, :], scalar=rstd[:, i:i + 1], in1=gain,
                                                   op0=ALU.mult, op1=ALU.mult).then_inc(o_ready, 1)


def rope_tables(rot):
    rows = SEQ // 64
    row = np.repeat(np.arange(rows, dtype=np.float32), 64)
    col = np.tile(np.arange(64, dtype=np.float32), rows)
    half = rot // 2
    inv = np.float32(10000.0) ** (-np.arange(0, half, 2, dtype=np.float32) / np.float32(half))
    ar, ac = row[:, None] * inv, col[:, None] * inv
    ang = np.concatenate([ar, ar, ac, ac], axis=-1).astype(np.float32)
    sign = np.repeat(np.array([-1, 1, -1, 1], np.float32), rot // 4)
    cos = np.concatenate([np.ones((CTX, rot), np.float32), np.cos(ang)])
    sin = np.concatenate([np.zeros((CTX, rot), np.float32), np.sin(ang) * sign])
    return cos.astype(np.float32), sin.astype(np.float32)


def kernel(**inputs):
    import concourse.bacc as bacc
    from concourse.bass_utils import run_bass_kernel_spmd as run

    g = {k: np.asarray(a) for k, a in inputs.items()}

    def tiles(w):
        return w.reshape(w.shape[0] // P, P, -1).transpose(1, 0, 2)

    def swap(w, n):
        s = w.shape
        return w.reshape(s[:-1] + (s[-1] // (2 * n), 2, n))[..., ::-1, :].reshape(s)

    cos, sin = rope_tables(ROPE)
    gcos, gsin = rope_tables(P)
    w_in = g["l0_mla_w_in"]
    uq = g["l0_mla_w_uq"].reshape(QR, H, NOPE + ROPE)
    uqr = uq[:, :, NOPE:]
    ukv = g["l0_mla_w_ukv"].reshape(KVR, H, 256)
    arrays = {
        "c_cols": np.stack([g["c"][0], g["c_ctx"]]).reshape(2, KD, P).transpose(2, 1, 0),
        "tokens": np.concatenate([g["ctx"][0], g["x"][0]]).reshape(NC, P, D).transpose(1, 0, 2),
        "ident": np.eye(P, dtype=np.float32),
        "ada": np.concatenate([g[f"l{i}_ada_w"].reshape(KD, P, MODW // ADA_CHUNK, ADA_CHUNK).transpose(2, 1, 0, 3).reshape(-1, P, KD * ADA_CHUNK) for i in range(LAYERS)]),
        "ada_b": np.stack([np.stack([g[f"l{i}_ada_b"]] * 2) for i in range(LAYERS)]),
        "gains": np.stack([np.concatenate([g[f"l{i}_{n}"] for i in range(LAYERS) for n in ("norm_mix", "norm_ffn")])] * 2),
        "w_in": tiles(np.concatenate([w_in, swap(w_in[:, QR + KVR:], ROPE // 4)], axis=1)),
        "rope_rows": np.concatenate([cos, sin], axis=1).reshape(NC, P, 2 * ROPE).transpose(1, 0, 2),
        "rope_cols": np.concatenate([cos, sin], axis=1).T,
        "gcol": np.concatenate([g["l0_mla_q_norm"].reshape(KQ, P), g["l0_mla_kv_norm"].reshape(KKV, P)]).T,
        "w_uq": tiles(np.concatenate([uq, swap(uqr, ROPE // 4)], axis=2).reshape(QR, H * 256)),
        "w_uk": tiles(ukv[:, :, :P].reshape(KVR, H * P)),
        "w_uv": tiles(ukv[:, :, P:].reshape(KVR, H * P)),
        "w_o0": tiles(g["l0_mla_w_o"]),
        "w_o1": tiles(g["l1_gqa_w_o"]),
        "w_qkv": tiles(g["l1_gqa_w_qkv"]),
        "rope_g": np.concatenate([gcos, gsin], axis=1).reshape(NC, P, 2 * P).transpose(1, 0, 2),
        "gain_g": np.concatenate([g["l1_gqa_q_norm"], g["l1_gqa_k_norm"]])[None],
        "keys": np.stack([np.stack([g[f"l{i}_peer_k1"], g[f"l{i}_peer_k2"]], axis=1).transpose(3, 0, 1, 2).reshape(P, 2 * H, NKEY) for i in range(LAYERS)]),
        "w_query": np.stack([g[f"l{i}_peer_w_query"].reshape(KD, P, 2 * H, P).transpose(2, 1, 0, 3).reshape(2 * H, P, KD * P) for i in range(LAYERS)]),
        "norm_out": g["norm_out"][None],
    }
    for i in range(LAYERS):
        arrays[f"uv{i}"] = np.concatenate([g[f"l{i}_peer_u"], g[f"l{i}_peer_v"]], axis=1)
    arrays = {k: np.ascontiguousarray(a) for k, a in arrays.items()}

    nc = bacc.Bacc("TRN2", target_bir_lowering=False, num_devices=1)
    dram = {k: nc.dram_tensor(f"in_{k}", a.shape, mybir.dt.from_np(a.dtype), kind="ExternalInput").ap() for k, a in arrays.items()}
    dram["uv"] = [dram[f"uv{i}"] for i in range(LAYERS)]
    out = nc.dram_tensor("out", (1, SEQ, D), F32, kind="ExternalOutput").ap()
    Kernel(nc, dram, out).build()
    r = run(nc, [{f"in_{k}": a for k, a in arrays.items()}], core_ids=[0])
    return r.results[0]["out"]
```

```python
import math
from contextlib import ExitStack

import numpy as np
import concourse.bass as bass
from concourse import mybir

F32, BF16, U32, I32 = mybir.dt.float32, mybir.dt.bfloat16, mybir.dt.uint32, mybir.dt.int32
ALU = mybir.AluOpType
ACT = mybir.ActivationFunctionType
AX = mybir.AxisListType

P = 128
D = 1024
KD = D // P
CTX, SEQ = 256, 256
TOK = CTX + SEQ
NC = TOK // P
CC = CTX // P
EPS = 1e-6
H = 8
NOPE, ROPE = 128, 64
QR, KVR = 384, 256
KQ, KKV = QR // P, KVR // P
HALF = 384
GKV = 2
NKEY = 128
TOPK = 16
MODW = 6 * D
LAYERS = 2
SH_A, SC_A, G_A, SH_F, SC_F, G_F = range(6)
LAT, CON = 0, 1
NEG = -3.0e38
GRP = 4
NG = TOPK // GRP
RING = TOPK
Q = 32
NQ = P // Q
ADA = NQ * 512
ADA_ROUNDS = MODW // ADA


def kind(c):
    return CON if c < CC else LAT


def phase(build):
    def built(self, *args, **more):
        self.phase_sems = []
        build(self, *args, **more)
        self.nc.clear_and_free_semaphores(self.phase_sems)
        self.nc.all_engine_barrier()
    return built


class Kernel:
    def __init__(self, nc, dram, out):
        self.nc, self.dram, self.out = nc, dram, out
        self.names = 0

    def sem(self, name):
        self.names += 1
        handle = self.nc.alloc_semaphore(name=f"{name}_{self.names}")
        self.phase_sems.append(handle)
        return handle

    def lasting_sem(self, name):
        self.names += 1
        return self.ctx.enter_context(self.nc.semaphore(f"{name}_{self.names}"))

    def view(self, region, at, *shape, dtype=None):
        n = int(np.prod(shape))
        v = region[:, at:at + n]
        if dtype is not None:
            v = v.bitcast(dtype)
        if len(shape) == 2:
            v = v.rearrange("p (a b) -> p a b", a=shape[0])
        if len(shape) == 3:
            v = v.rearrange("p (a b c) -> p a b c", a=shape[0], b=shape[1])
        return v

    def build(self):
        nc = self.nc
        with ExitStack() as ctx:
            self.ctx = ctx
            sb = lambda n, s, d=F32: ctx.enter_context(nc.sbuf_tensor(n, s, d))
            self.ident = sb("ident", [P, P])
            self.x = sb("x", [P, NC, D])
            self.h = sb("h", [P, NC * D])
            self.hT = self.view(sb("hT", [P, KD * TOK]), 0, KD, TOK)
            self.arena = sb("arena", [P, RING * 2 * D])
            self.aux = sb("aux", [P, 7296])
            self.small = sb("small", [P, 384 + P])
            self.bank = [ctx.enter_context(nc.psum_tensor(f"bank{i}", [P, 512], F32)) for i in range(8)]
            self.loaded_x = self.lasting_sem("loaded_x")
            self.adaln()
            self.layer(0)
            self.layer(1)
            self.finish()

    def ada_places(self, layer, rows_at, gains_at):
        self.rows = self.view(rows_at[0], rows_at[1], ADA_ROUNDS, 512)
        self.gains = gains_at[0][:, gains_at[1]:gains_at[1] + 512]
        self.ada_rows_loaded = self.sem("ada_rows_loaded")
        self.ada_sum, self.ada_added, self.ada_done = self.sem("ada_sum"), self.sem("ada_added"), self.sem("ada_done")
        self.mod_stored[layer] = self.lasting_sem("mod_stored")

    def ada_load_rows(self, layer, eng):
        bias = self.dram["ada_b"][layer:layer + 1, :].rearrange("o (i s n) -> s o i n", s=NQ, n=512)
        for s in range(NQ):
            eng.dma_start(self.rows[s * Q:(s + 1) * Q], bias[s].broadcast_to([Q, ADA_ROUNDS, 512])).then_inc(self.ada_rows_loaded, 16)
            eng.dma_start(self.gains[s * Q:(s + 1) * Q], self.dram["gains"][layer, s:s + 1, :].broadcast_to([Q, 512])).then_inc(self.ada_rows_loaded, 16)

    def ada_store(self, layer, eng):
        eng.wait_ge(self.ada_done, 5)
        dst = self.modd[:, layer * MODW:(layer + 1) * MODW].rearrange("k (i s n) -> s k i n", s=NQ, n=512)
        for s in range(NQ):
            eng.dma_start(dst[s], self.rows[s * Q:s * Q + 2]).then_inc(self.mod_stored[layer], 16)

    def ada_products(self, bank, k, weights):
        for s in range(NQ):
            last = self.nc.tensor.matmul(bank[s * Q:(s + 1) * Q, :], self.cs[:, k, :], weights[:, s * 512:(s + 1) * 512],
                                         start=(k == 0), stop=(k == KD - 1))
        return last

    def ada_add(self, bank, i):
        r = self.rows[:, i, :]
        return self.nc.vector.tensor_tensor(r, r, bank[:], ALU.add)

    def ada_scales(self, dve):
        for i, seg in ((0, SC_A), (2, SC_F)):
            first = seg * D // 512 - i * NQ
            r = self.rows[first * Q:(first + 2) * Q, i, :]
            self.nc.vector.scalar_tensor_tensor(out=r, in0=r, scalar=1.0, in1=self.gains[first * Q:(first + 2) * Q, :],
                                                op0=ALU.add, op1=ALU.mult).then_inc(self.ada_done, 1)
        dve.sem_inc(self.ada_done, 3)

    def ada_weights(self, layer, i, k):
        return self.dram["ada"][layer, bass.ds(i * KD + k, 1), :, :].rearrange("a p n -> p (a n)")

    @phase
    def adaln(self):
        nc, d, v = self.nc, self.dram, self.view
        slots = v(self.arena, 0, KD, ADA)
        self.cs = v(self.aux, 7040, KD, Q)
        cols = v(self.small, 0, KD, 2)
        sem = self.sem
        loaded_c, silu_done, cs_zero = sem("loaded_c"), sem("silu_done"), sem("cs_zero")
        w_loaded = [sem(f"w_loaded{k}") for k in range(KD)]
        w_free, bank_free = sem("w_free"), sem("bank_free")
        self.modd = nc.dram_tensor("mod_rows", (2, LAYERS * MODW), F32, kind="Internal").ap()
        self.mod_stored = [None] * LAYERS
        self.ada_places(0, (self.aux, 0), (self.aux, 1536))
        bank = self.bank[0]
        with nc.Block() as block:
            @block.sync
            def _(sp):
                with sp.Fori(0, ADA_ROUNDS) as it:
                    for k in range(KD):
                        sp.wait_ge(w_free, it * KD + k + 1)
                        sp.dma_start(slots[:, k, :], self.ada_weights(0, it, k)).then_inc(w_loaded[k], 16)
                self.ada_store(0, sp)
                sp.wait_ge(self.mod_stored[0], 16 * NQ)

            @block.scalar
            def _(act):
                act.dma_start(cols, d["c_cols"]).then_inc(loaded_c, 16)
                self.ada_load_rows(0, act)
                act.dma_start(self.ident[:], d["ident"]).then_inc(self.loaded_x, 16)
                act.dma_start(self.x[:], d["tokens"]).then_inc(self.loaded_x, 16)
                act.wait_ge(loaded_c, 16)
                act.wait_ge(cs_zero, 1)
                nc.scalar.activation(self.cs[:, :, 0:2], cols, ACT.Silu).then_inc(silu_done, 1)

            @block.tensor
            def _(pe):
                pe.sem_inc(w_free, KD)
                pe.wait_ge(silu_done, 1)
                with pe.Fori(0, ADA_ROUNDS) as it:
                    pe.wait_ge(bank_free, it + 1)
                    for k in range(KD):
                        pe.wait_ge(w_loaded[k], it * 16 + 16)
                        self.ada_products(bank, k, slots[:, k, :]).then_inc(w_free, 1)

            @block.vector
            def _(dve):
                nc.vector.memset(self.cs, 0.0).then_inc(cs_zero, 1)
                dve.sem_inc(bank_free, 1)
                dve.wait_ge(self.ada_rows_loaded, 32 * NQ)
                for i in range(ADA_ROUNDS):
                    dve.wait_ge(w_free, (i + 2) * KD)
                    self.ada_add(bank, i).then_inc(bank_free, 1)
                dve.wait_ge(bank_free, 1 + ADA_ROUNDS)
                self.ada_scales(dve)

    @phase
    def norm(self, layer, seg_sh, seg_sc, chunks, prefetch=None):
        nc, v = self.nc, self.view
        bc = v(self.arena, 0, 4, D)
        hT = self.hT
        junk = v(self.aux, 0, D)
        ssq, var, std, rstd = (v(self.small, 64 + 4 * i, NC) for i in range(4))
        sem = self.sem
        bc_loaded, sq_done, mean_done, sqrt_done, rstd_done = (sem(n) for n in ("bc_loaded", "sq_done", "mean_done", "sqrt_done", "rstd_done"))
        scaled, h_ready, t_done, t_copied = sem("scaled"), sem("h_ready"), sem("t_done"), sem("t_copied")
        first, n = chunks[0], len(chunks)
        base = layer * MODW
        with nc.Block() as block:
            @block.sync
            def _(sp):
                sp.wait_ge(self.mod_stored[layer], 16 * NQ)
                for kd in (LAT, CON):
                    for j, seg in enumerate((seg_sc, seg_sh)):
                        src = self.modd[kd:kd + 1, base + seg * D:base + (seg + 1) * D]
                        sp.dma_start(bc[:, 2 * kd + j, :], src.broadcast_to([P, D])).then_inc(bc_loaded, 16)
                if prefetch:
                    prefetch(sp)

            @block.scalar
            def _(act):
                act.wait_ge(self.loaded_x, 32)
                for i, c in enumerate(chunks):
                    if i:
                        act.wait_ge(sq_done, i)
                    nc.scalar.activation(junk, self.x[:, c, :], ACT.Square, accum_out=ssq[:, c:c + 1]).then_inc(sq_done, 1)
                act.wait_ge(mean_done, 1)
                nc.scalar.activation(std[:, first:], var[:, first:], ACT.Sqrt).then_inc(sqrt_done, 1)
                for i, c in enumerate(chunks):
                    for q in range(2):
                        act.wait_ge(t_done, 2 * i + q + 1)
                        nc.scalar.copy(hT[:, 4 * q:4 * q + 4, c * P:(c + 1) * P],
                                       self.bank[(2 * i + q) % 8][:].rearrange("p (a b) -> p a b", a=4)).then_inc(t_copied, 1)

            @block.vector
            def _(dve):
                dve.wait_ge(sq_done, n)
                nc.vector.tensor_scalar(var[:, first:], ssq[:, first:], 1.0 / D, EPS, ALU.mult, ALU.add).then_inc(mean_done, 1)
                dve.wait_ge(sqrt_done, 1)
                nc.vector.reciprocal(rstd[:, first:], std[:, first:]).then_inc(rstd_done, 1)
                dve.wait_ge(rstd_done, 1)
                dve.wait_ge(bc_loaded, 64)
                for i, c in enumerate(chunks):
                    hc = self.h[:, c * D:(c + 1) * D]
                    nc.vector.scalar_tensor_tensor(out=hc, in0=self.x[:, c, :], scalar=rstd[:, c:c + 1], in1=bc[:, 2 * kind(c), :],
                                                   op0=ALU.mult, op1=ALU.mult).then_inc(scaled, 1)
                    dve.wait_ge(scaled, i + 1)
                    nc.vector.tensor_tensor(hc, hc, bc[:, 2 * kind(c) + 1, :], ALU.add).then_inc(h_ready, 1)

            @block.tensor
            def _(pe):
                pe.wait_ge(self.loaded_x, 32)
                for i, c in enumerate(chunks):
                    pe.wait_ge(h_ready, i + 1)
                    for q in range(2):
                        for k in range(4):
                            kk = 4 * q + k
                            last = nc.tensor.transpose(self.bank[(2 * i + q) % 8][:, k * P:(k + 1) * P],
                                                       self.h[:, c * D + kk * P:c * D + (kk + 1) * P], self.ident[:])
                        last.then_inc(t_done, 1)

    def mla_weights(self, sp):
        v, d = self.view, self.dram
        self.w_in = v(self.arena, 21504, KD, 2 * HALF)
        self.rope_rows = v(self.arena, 7680, NC, 2 * ROPE)
        self.w_uq = v(self.arena, 11264, KQ, H * 256)
        self.w_uk = v(self.arena, 17408, KKV, H * P)
        self.w_uv = v(self.arena, 19456, KKV, H * P)
        self.rope_cols = v(self.arena, 7168, TOK)
        self.gcol = v(self.small, 80, 5)
        self.w_o = v(self.arena, 12 * 2 * D, H, D)
        self.w_in_loaded, self.w_up_loaded, self.w_o_loaded = self.lasting_sem("w_in_loaded"), self.lasting_sem("w_up_loaded"), self.lasting_sem("w_o_loaded")
        sp.dma_start(self.w_in, d["w_in"]).then_inc(self.w_in_loaded, 16)
        sp.dma_start(self.rope_rows, d["rope_rows"]).then_inc(self.w_in_loaded, 16)
        sp.dma_start(self.gcol, d["gcol"]).then_inc(self.w_in_loaded, 16)
        sp.dma_start(self.w_uq, d["w_uq"]).then_inc(self.w_up_loaded, 16)
        sp.dma_start(self.w_uk, d["w_uk"]).then_inc(self.w_up_loaded, 16)
        sp.dma_start(self.w_uv, d["w_uv"]).then_inc(self.w_up_loaded, 16)
        sp.dma_start(self.rope_cols, d["rope_cols"]).then_inc(self.w_up_loaded, 16)

    @phase
    def mla_in(self):
        nc, v, sem = self.nc, self.view, self.sem
        hT, rr = self.hT, self.rope_rows
        cT = self.cT = v(self.arena, 8192, 6, TOK)
        an = v(self.aux, 0, 2, 2 * HALF)
        kr = v(self.aux, 1536, 2, 2 * ROPE)
        junk = v(self.aux, 1792, 640)
        ssq, var, std, rstd = (v(self.small, 96 + 8 * i, NC, 2) for i in range(4))
        a_done, sq_done, mean_done, sqrt_done, rstd_done = (sem(n) for n in ("a_done", "sq_done", "mean_done", "sqrt_done", "rstd_done"))
        an_ready_a = sem("an_scaled")
        an_ready, kr_step, bank_free, t_done, t_copied = (sem(n) for n in ("an_ready", "kr_step", "bank_free", "t_done", "t_copied"))
        with nc.Block() as block:
            @block.tensor
            def _(pe):
                pe.wait_ge(self.w_in_loaded, 48)

                def project(c):
                    for half in range(2):
                        if c >= 2:
                            pe.wait_ge(bank_free, c - 1)
                        for k in range(KD):
                            last = nc.tensor.matmul(self.bank[2 * (c % 2) + half][:, 0:HALF], hT[:, k, c * P:(c + 1) * P],
                                                    self.w_in[:, k, half * HALF:(half + 1) * HALF], start=(k == 0), stop=(k == KD - 1))
                        last.then_inc(a_done, 1)

                def transposes(c):
                    pe.wait_ge(an_ready, c + 1)
                    if c >= 1:
                        pe.wait_ge(t_copied, 6 * c)
                    for j in range(6):
                        last = nc.tensor.transpose(self.bank[4 + j // 3][:, (j % 3) * P:(j % 3 + 1) * P], an[:, c % 2, j * P:(j + 1) * P], self.ident[:])
                        if j % 3 == 2:
                            last.then_inc(t_done, 1)

                for c in range(NC):
                    project(c)
                    if c:
                        transposes(c - 1)
                transposes(NC - 1)

            @block.scalar
            def _(act):
                for c in range(NC):
                    act.wait_ge(a_done, 2 * c + 2)
                    b = self.bank[2 * (c % 2)], self.bank[2 * (c % 2) + 1]
                    if c:
                        act.wait_ge(sq_done, 2 * c)
                    nc.scalar.activation(junk[:, 0:QR], b[0][:, 0:QR], ACT.Square, accum_out=ssq[:, c, 0:1]).then_inc(sq_done, 1)
                    nc.scalar.activation(junk[:, QR:QR + KVR], b[1][:, 0:KVR], ACT.Square, accum_out=ssq[:, c, 1:2]).then_inc(sq_done, 1)
                    act.wait_ge(mean_done, 2 * c + 2)
                    nc.scalar.activation(std[:, c, :], var[:, c, :], ACT.Sqrt).then_inc(sqrt_done, 1)
                    act.wait_ge(rstd_done, c + 1)
                    if c >= 2:
                        act.wait_ge(t_done, 2 * (c - 1))
                    nc.scalar.mul(an[:, c % 2, 0:QR], b[0][:, 0:QR], rstd[:, c, 0:1]).then_inc(an_ready_a, 1)
                    nc.scalar.mul(an[:, c % 2, QR:QR + KVR], b[1][:, 0:KVR], rstd[:, c, 1:2]).then_inc(an_ready_a, 1)

            @block.vector
            def _(dve):
                step = 0
                for c in range(NC):
                    b1 = self.bank[2 * (c % 2) + 1]
                    dve.wait_ge(sq_done, 2 * c + 2)
                    for j, width in enumerate((QR, KVR)):
                        nc.vector.tensor_scalar(var[:, c, j:j + 1], ssq[:, c, j:j + 1], 1.0 / width, EPS, ALU.mult, ALU.add).then_inc(mean_done, 1)
                    if c >= 1:
                        dve.wait_ge(kr_step, step)
                    if c >= 2:
                        dve.wait_ge(t_done, 2 * (c - 1))
                    dst = an[:, c % 2, QR + KVR:QR + KVR + ROPE]
                    nc.vector.tensor_tensor(kr[:, 0, 0:ROPE], b1[:, KVR:KVR + ROPE], rr[:, c, 0:ROPE], ALU.mult).then_inc(kr_step, 1)
                    nc.vector.tensor_tensor(kr[:, 1, 0:ROPE], b1[:, KVR + ROPE:KVR + 2 * ROPE], rr[:, c, ROPE:2 * ROPE], ALU.mult).then_inc(kr_step, 1)
                    dve.wait_ge(kr_step, step + 2)
                    nc.vector.tensor_tensor(dst, kr[:, 0, 0:ROPE], kr[:, 1, 0:ROPE], ALU.add).then_inc(kr_step, 1)
                    dve.wait_ge(kr_step, step + 3)
                    nc.vector.tensor_copy(an[:, c % 2, QR + KVR + ROPE:2 * HALF], dst).then_inc(kr_step, 1)
                    step += 4
                    dve.wait_ge(sqrt_done, c + 1)
                    nc.vector.reciprocal(rstd[:, c, :], std[:, c, :]).then_inc(rstd_done, 1)
                    dve.wait_ge(an_ready_a, 2 * c + 2)
                    dve.wait_ge(kr_step, step)
                    dve.sem_inc(an_ready, 1)
                    dve.sem_inc(bank_free, 1)
                    for j in range(6):
                        dve.wait_ge(t_done, 2 * c + j // 3 + 1)
                        src, dst = self.bank[4 + j // 3][:, (j % 3) * P:(j % 3 + 1) * P], cT[:, j, c * P:(c + 1) * P]
                        if j < 5:
                            nc.vector.tensor_scalar(dst, src, self.gcol[:, j:j + 1], None, ALU.mult).then_inc(t_copied, 1)
                        else:
                            nc.vector.tensor_copy(dst, src).then_inc(t_copied, 1)

    def attention(self, layer, chunks, keys_of, v_rows, score_terms, scale, head_proj=None, pre=None, between=None):
        nc, v, sem = self.nc, self.view, self.sem
        probs = v(self.aux, 0, 2, TOK)
        pT = v(self.aux, 1024, 2, TOK)
        OT = self.hT
        nmax, nbias, rsum, rinv = (v(self.small, 128 + 32 * i, 32) for i in range(4))
        s_done, mx, mx_done, exp_done, rinv_done, p_ready, pt_done, pt_copied, pv_done, o_done, o_copied = (
            sem(n) for n in ("s_done", "mx", "mx_done", "exp_done", "rinv_done", "p_ready", "pt_done", "pt_copied", "pv_done", "o_done", "o_copied"))
        proj_done = sem("proj_done")
        nch = len(chunks)
        units = [(hd, c) for hd in range(H) for c in chunks]
        U = len(units)
        S_BANK, T_BANK, O_BANK = (3, 4), (5, 6), 7
        lo, hi = chunks[0] * P, (chunks[-1] + 1) * P

        with nc.Block() as block:
            @block.sync
            def _(sp):
                if pre:
                    pre("sp", sp)
                self.first_queries(layer, sp)
                if between:
                    between("sp", sp, 0)

            @block.tensor
            def _(pe):
                if pre:
                    pre("pe", pe)
                def proj(hd):
                    head_proj("pe", pe, hd, proj_done)

                def scores(u):
                    hd, c = units[u]
                    if head_proj:
                        head_proj("scores", pe, hd)
                    if u >= 2:
                        pe.wait_ge(exp_done, u - 1)
                    terms = score_terms(hd, c)
                    for i, (q, k) in enumerate(terms):
                        last = nc.tensor.matmul(self.bank[S_BANK[u % 2]][:, 0:keys_of(c)], q, k, start=(i == 0), stop=(i == len(terms) - 1))
                    last.then_inc(s_done, 1)

                def transposes(u):
                    c = units[u][1]
                    pe.wait_ge(p_ready, u + 1)
                    if u >= 2:
                        pe.wait_ge(pt_copied, u - 1)
                    for t in range(keys_of(c) // P):
                        last = nc.tensor.transpose(self.bank[T_BANK[u % 2]][:, t * P:(t + 1) * P], probs[:, u % 2, t * P:(t + 1) * P], self.ident[:])
                    last.then_inc(pt_done, 1)

                def values(u):
                    hd, c = units[u]
                    pe.wait_ge(pt_copied, u + 1)
                    if u % nch == 0 and hd:
                        pe.wait_ge(o_copied, hd)
                    n = keys_of(c) // P
                    for t in range(n):
                        last = nc.tensor.matmul(self.bank[O_BANK][:, c * P:(c + 1) * P], v_rows(hd, t), pT[:, u % 2, t * P:(t + 1) * P],
                                                start=(t == 0), stop=(t == n - 1))
                    last.then_inc(pv_done, 1)

                if head_proj:
                    proj(0)
                for u in range(U + 2):
                    if u < U:
                        scores(u)
                        if head_proj and u % nch == 1 and units[u][0] + 1 < H:
                            proj(units[u][0] + 1)
                    if 1 <= u <= U:
                        transposes(u - 1)
                    if u >= 2:
                        values(u - 2)
                    if between:
                        between("pe", pe, u)

            @block.scalar
            def _(act):
                if pre:
                    pre("act", act)

                def exps(u):
                    c = units[u][1]
                    act.wait_ge(mx_done, u + 1)
                    if u >= 2:
                        act.wait_ge(pt_done, u - 1)
                    nc.scalar.activation(probs[:, u % 2, 0:keys_of(c)], self.bank[S_BANK[u % 2]][:, 0:keys_of(c)], ACT.Exp,
                                         bias=nbias[:, u:u + 1], scale=scale, accum_out=rsum[:, u:u + 1]).then_inc(exp_done, 1)

                def copy_pt(u):
                    c = units[u][1]
                    act.wait_ge(pt_done, u + 1)
                    if u >= 2:
                        act.wait_ge(pv_done, u - 1)
                    nc.scalar.copy(pT[:, u % 2, 0:keys_of(c)], self.bank[T_BANK[u % 2]][:, 0:keys_of(c)]).then_inc(pt_copied, 1)

                if head_proj:
                    head_proj("act", act, 0, proj_done, s_done)
                for u in range(U + 1):
                    if u < U:
                        exps(u)
                        if head_proj and u % nch == 1 and units[u][0] + 1 < H:
                            head_proj("act", act, units[u][0] + 1, proj_done, s_done)
                    if u >= 1:
                        copy_pt(u - 1)

            @block.vector
            def _(dve):
                if pre:
                    pre("dve", dve)

                def maxima(u):
                    c = units[u][1]
                    dve.wait_ge(s_done, u + 1)
                    nc.vector.tensor_reduce(nmax[:, u:u + 1], self.bank[S_BANK[u % 2]][:, 0:keys_of(c)], AX.X, ALU.max, negate=True).then_inc(mx, 1)
                    dve.wait_ge(mx, u + 1)
                    nc.vector.tensor_scalar(nbias[:, u:u + 1], nmax[:, u:u + 1], scale, None, ALU.mult).then_inc(mx_done, 1)

                def normalise(u):
                    c = units[u][1]
                    dve.wait_ge(exp_done, u + 1)
                    nc.vector.reciprocal(rinv[:, u:u + 1], rsum[:, u:u + 1]).then_inc(rinv_done, 1)
                    dve.wait_ge(rinv_done, u + 1)
                    pr = probs[:, u % 2, 0:keys_of(c)]
                    nc.vector.tensor_scalar(pr, pr, rinv[:, u:u + 1], None, ALU.mult).then_inc(p_ready, 1)

                def copy_out(hd):
                    dve.wait_ge(pv_done, nch * (hd + 1))
                    nc.vector.tensor_copy(OT[:, hd, lo:hi], self.bank[O_BANK][:, lo:hi]).then_inc(o_copied, 1)

                if head_proj:
                    head_proj("dve", dve, 0, proj_done, s_done)
                for u in range(U + 1):
                    if u < U:
                        maxima(u)
                        if head_proj and u % nch == 1 and units[u][0] + 1 < H:
                            head_proj("dve", dve, units[u][0] + 1, proj_done, s_done)
                    if u >= 1:
                        normalise(u - 1)
                    if u > nch and (u - 1) % nch == 0:
                        copy_out((u - 1) // nch - 1)
                    if between:
                        between("dve", dve, u)
                if nch > 1:
                    copy_out(H - 1)

    @phase
    def mla_attention(self):
        nc, v = self.nc, self.view
        cT = self.cT
        V = v(self.arena, 0, NC, D)
        qn, qr, kn = (v(self.arena, 4096 + 1024 * i, 2, TOK) for i in range(3))
        v_done, v_copied = self.sem("v_done"), self.sem("v_copied")
        qk_copied, rot_copied = self.sem("qk_copied"), self.sem("rot_copied")
        ada_slots = [v(self.h, 0, ADA), v(self.h, ADA, ADA), v(self.arena, 21504, ADA)]
        w_loaded = [self.sem(f"ada_loaded{i}") for i in range(len(ada_slots))]
        w_used, bank_read = self.sem("ada_used"), self.sem("ada_bank_read")
        self.ada_places(1, (self.aux, 4736), (self.arena, 21504 + ADA))
        ada_bank = self.bank[2]
        steps = ADA_ROUNDS * KD

        def pre(who, eng):
            if who == "sp":
                eng.dma_start(self.w_o, self.dram["w_o0"]).then_inc(self.w_o_loaded, 16)
            if who == "pe":
                eng.wait_ge(self.w_up_loaded, 64)
                for c in range(NC):
                    for n in range(2):
                        for k in range(KKV):
                            last = nc.tensor.matmul(self.bank[2 * c + n][:], cT[:, KQ + k, c * P:(c + 1) * P], self.w_uv[:, k, n * 512:(n + 1) * 512],
                                                    start=(k == 0), stop=(k == KKV - 1))
                        last.then_inc(v_done, 1)
                eng.wait_ge(v_copied, 8)
            if who == "act":
                for i in range(0, 8, 2):
                    eng.wait_ge(v_done, i + 1)
                    nc.scalar.copy(V[:, i // 2, 0:512], self.bank[i][:]).then_inc(v_copied, 1)
            if who == "dve":
                for i in range(1, 8, 2):
                    eng.wait_ge(v_done, i + 1)
                    nc.vector.tensor_copy(V[:, i // 2, 512:1024], self.bank[i][:]).then_inc(v_copied, 1)

        def between(who, eng, u):
            if who == "sp":
                self.ada_load_rows(1, eng)
                for n in range(steps):
                    if n >= len(ada_slots):
                        eng.wait_ge(w_used, n - len(ada_slots) + 1)
                    eng.dma_start(ada_slots[n % len(ada_slots)], self.ada_weights(1, n // KD, n % KD)).then_inc(w_loaded[n % len(ada_slots)], 16)
                self.ada_store(1, eng)
                eng.wait_ge(self.mod_stored[1], 16 * NQ)
            if who == "pe" and 3 <= u < 3 + steps:
                n = u - 3
                eng.wait_ge(w_loaded[n % len(ada_slots)], 16 * (n // len(ada_slots) + 1))
                if n and n % KD == 0:
                    eng.wait_ge(bank_read, n // KD)
                self.ada_products(ada_bank, n % KD, ada_slots[n % len(ada_slots)]).then_inc(w_used, 1)
            if who == "dve" and u > 3 and (u - 2) % KD == 0 and (u - 2) // KD <= ADA_ROUNDS:
                i = (u - 2) // KD - 1
                if i == 0:
                    eng.wait_ge(self.ada_rows_loaded, 32 * NQ)
                eng.wait_ge(w_used, (i + 1) * KD)
                self.ada_add(ada_bank, i).then_inc(bank_read, 1)
                if i == ADA_ROUNDS - 1:
                    eng.wait_ge(bank_read, ADA_ROUNDS)
                    self.ada_scales(eng)

        def head_proj(who, eng, hd, *sems):
            if who == "scores":
                eng.wait_ge(qk_copied, 2 * hd + 2)
                eng.wait_ge(rot_copied, hd + 1)
                return
            if who == "pe":
                done, = sems
                for j in range(3):
                    if j == 0 and hd:
                        eng.wait_ge(qk_copied, 2 * hd)
                    if j == 1 and hd:
                        eng.wait_ge(rot_copied, hd)
                    if j == 2:
                        eng.wait_ge(qk_copied, 2 * hd + 1)
                    src, w, tiles = [(0, self.w_uq[:, :, hd * 256:hd * 256 + 128], KQ), (0, self.w_uq[:, :, hd * 256 + 128:hd * 256 + 256], KQ),
                                     (KQ, self.w_uk[:, :, hd * P:(hd + 1) * P], KKV)][j]
                    for k in range(tiles):
                        last = nc.tensor.matmul(self.bank[j % 2][:], w[:, k, :], cT[:, src + k, :], start=(k == 0), stop=(k == tiles - 1))
                    last.then_inc(done, 1)
                return
            done, s_done = sems
            if hd >= 2:
                eng.wait_ge(s_done, NC * (hd - 1))
            if who == "act":
                for j, dst in ((0, qn), (2, kn)):
                    eng.wait_ge(done, 3 * hd + j + 1)
                    nc.scalar.copy(dst[:, hd % 2, :], self.bank[j % 2][:]).then_inc(qk_copied, 1)
            else:
                eng.wait_ge(done, 3 * hd + 2)
                nc.vector.tensor_tensor(qr[:, hd % 2, :], self.bank[1][:], self.rope_cols, ALU.mult).then_inc(rot_copied, 1)

        self.attention(
            0, list(range(NC)), lambda c: CTX if c < CC else TOK, lambda hd, t: V[:, t, hd * P:(hd + 1) * P],
            lambda hd, c: [(qn[:, hd % 2, c * P:(c + 1) * P], kn[:, hd % 2, 0:CTX if c < CC else TOK]),
                           (qr[:, hd % 2, c * P:(c + 1) * P], cT[:, 5, 0:CTX if c < CC else TOK])],
            1.0 / math.sqrt(NOPE + ROPE), head_proj, pre, between)

    def first_queries(self, layer, sp):
        v = self.view
        self.wq = v(self.aux, 2048, KD, P)
        self.keys = v(self.aux, 3072, NKEY)
        self.diag = v(self.aux, 3712, 2 * GRP, P)
        self.first = [(self.wq, self.keys), (v(self.aux, 3712, KD, P), v(self.small, 384, NKEY))]
        if layer == 1:
            for side in range(2):
                self.first.append((v(self.h, side * KD * P, KD, P), self.x[:, 0, side * NKEY:(side + 1) * NKEY]))
        self.first_loaded = self.lasting_sem("first_loaded")
        for j, (wq, keys) in enumerate(self.first):
            sp.dma_start(wq, self.w_query_rows(layer, j)).then_inc(self.first_loaded, 16)
            sp.dma_start(keys, self.key_rows(layer, j)).then_inc(self.first_loaded, 16)

    @phase
    def peer(self, layer, chunks):
        nc, v, sem = self.nc, self.view, self.sem
        nch = len(chunks)
        lead = 2 // (nch // 2)
        body = 2 * nch
        lo, hi = chunks[0] * P, (chunks[-1] + 1) * P
        ring = v(self.arena, 0, RING, 2 * D)
        scores = v(self.aux, 0, 2, NC, 2 * NKEY)
        wq, keys, diag = self.wq, self.keys, self.diag
        qT = v(self.aux, 3200, TOK)
        C = v(self.aux, 4736, TOPK, TOPK)
        OH = v(self.aux, 4992, TOPK, TOPK)
        gate_f = v(self.aux, 5248, 2, D)
        sm = self.small
        val = v(sm, 0, 2, TOPK)
        ind = v(sm, 32, 2, TOPK, dtype=U32)
        indf = v(sm, 64, 2, TOPK)
        top = v(sm, 96, TOPK)
        pos = v(sm, 112, TOPK, dtype=U32)
        posi = v(sm, 128, 2, TOPK, dtype=U32)
        sel = v(sm, 160, 2, TOPK)
        idx = v(sm, 192, 2, TOPK, dtype=I32)
        gate = v(sm, 224, 2, TOPK)
        a = v(sm, 256, 2, TOPK)
        w = v(sm, 288, 2, TOPK)
        iota = v(sm, 320, TOPK)
        iota_i = v(sm, 336, TOPK, dtype=I32)
        nb, es, er = sm[:, 352:353], sm[:, 354:355], sm[:, 356:357]
        before = 2 * GRP * 2 * D
        bc = v(self.arena, before, 4, D)
        gate_a = v(self.arena, before + 4 * D, 2, D)
        y = v(self.arena, before + 6 * D, 2, 512)
        junk = v(self.arena, before + 7 * D, D)
        ssq, var, std, rstd = (v(sm, 360 + 4 * i, NC) for i in range(4))
        kinds = sorted({kind(c) for c in chunks}, reverse=True)
        rows_loaded, y_done, gated, sq_done, mean_done, sqrt_done, h_ready, t_done, t_copied = (
            sem(n) for n in ("rows_loaded", "y_done", "gated", "sq_done", "mean_done", "sqrt_done", "h_ready", "t_done", "t_copied"))
        added, first_q_done, first_q_copied, first_sc_done, first_sc_copied = (
            sem(n) for n in ("added", "first_q_done", "first_q_copied", "first_sc_done", "first_sc_copied"))
        gathered = [sem(f"gathered{k}") for k in range(RING)]
        slots_free, token, idx_ready, dots_done, gelu_done, w_ready, diag_ready, acc_free = (
            sem(n) for n in ("slots_free", "token", "idx_ready", "dots_done", "gelu_done", "w_ready", "diag_ready", "acc_free"))
        chain, top_ready, exp_done, iota_done, gate_loaded = (sem(n) for n in ("chain", "top_ready", "exp_done", "iota_done", "gate_loaded"))
        wq_loaded, keys_loaded, q_done, q_copied, sc_done, sc_copied = (
            sem(n) for n in ("wq_loaded", "keys_loaded", "q_done", "q_copied", "sc_done", "sc_copied"))
        table = self.dram["uv"][layer]
        acc = ((self.bank[0], self.bank[1]), (self.bank[2], self.bank[3]))
        Q_BANK, S_BANK = self.bank[4], self.bank[5]
        first_jobs = 2 * lead
        qT_slots = 4 // first_jobs
        place = [divmod(i, nch) for i in range(body + 2)]

        def job_of(i, it):
            hd, c = place[i]
            return it * 4 + (2 * hd + c + first_jobs) if c < 2 else None

        def in_turn(norm, rest):
            norm(0)
            rest(0)
            norm(1)
            if nch > 2:
                norm(2)
            for i in range(1, nch):
                rest(i)
                if i + 2 < nch:
                    norm(i + 2)

        with nc.Block() as block:
            @block.sync
            def _(sp):
                for kd in kinds:
                    for dst, seg in ((gate_a[:, kd, :], G_A), (bc[:, 2 * kd, :], SC_F), (bc[:, 2 * kd + 1, :], SH_F)):
                        at = layer * MODW + seg * D
                        sp.dma_start(dst, self.modd[kd:kd + 1, at:at + D].broadcast_to([P, D])).then_inc(rows_loaded, 16)
                for kd in kinds:
                    seg = layer * MODW + G_F * D
                    sp.dma_start(gate_f[:, kd, :], self.modd[kd:kd + 1, seg:seg + D].broadcast_to([P, D])).then_inc(gate_loaded, 16)

                def load(j):
                    sp.wait_ge(q_done, j)
                    sp.dma_start(wq, self.w_query_rows(layer, j)).then_inc(wq_loaded, 16)
                    sp.wait_ge(sc_done, j)
                    sp.dma_start(keys, self.key_rows(layer, j)).then_inc(keys_loaded, 16)

                sp.sem_inc(wq_loaded, 16 * first_jobs)
                sp.sem_inc(keys_loaded, 16 * first_jobs)
                with sp.Fori(0, H // 2) as it:
                    for i in range(body):
                        j = job_of(i, it)
                        if j is not None:
                            load(j)

            @block.gpsimd
            def _(pool):
                nc.gpsimd.iota(iota_i, pattern=[[1, TOPK]], base=0, channel_multiplier=0).then_inc(iota_done, 1)
                with pool.Fori(0, H // 2) as it:
                    for i in range(body):
                        pool.wait_ge(idx_ready, it * body + i + 1)
                        pool.sem_inc(token, 1)
                        for g in range(NG):
                            pool.wait_ge(slots_free, it * (body * NG) + i * NG + g + 1)
                            pool.sem_inc(token, 1)
                            for k in range(g * GRP, (g + 1) * GRP):
                                nc.gpsimd.indirect_dma_start(
                                    out=ring[:, k, :], out_offset=None, in_=table,
                                    in_offset=bass.IndirectOffsetOnAxis(ap=idx[:, i % 2, k:k + 1], axis=0)).then_inc(gathered[k], 16)

            @block.tensor
            def _(pe):
                pe.sem_inc(slots_free, 2)

                def project(i, n):
                    if i >= 2:
                        pe.wait_ge(gated, 2 * i + n - 3)
                    c = chunks[i]
                    for hd in range(H):
                        last = nc.tensor.matmul(self.bank[2 * (i % 2) + n][:], self.hT[:, hd, c * P:(c + 1) * P], self.w_o[:, hd, n * 512:(n + 1) * 512],
                                                start=(hd == 0), stop=(hd == H - 1))
                    last.then_inc(y_done, 1)

                def front(i):
                    c = chunks[i]
                    pe.wait_ge(h_ready, i + 1)
                    if i == nch - 1:
                        pe.sem_inc(slots_free, NG - 2)
                    if i:
                        pe.wait_ge(t_copied, 2 * i)
                    for q in range(2):
                        for k in range(4):
                            kk = 4 * q + k
                            last = nc.tensor.transpose(self.bank[6 + q][:, k * P:(k + 1) * P], self.h[:, c * D + kk * P:c * D + (kk + 1) * P], self.ident[:])
                        last.then_inc(t_done, 1)
                    if i:
                        pe.wait_ge(first_q_copied, i)
                    else:
                        pe.wait_ge(self.first_loaded, 32 * first_jobs)
                    pe.wait_ge(t_copied, 2 * i + 2)
                    for j, (weights, sub) in enumerate(self.first):
                        for k in range(KD):
                            last = nc.tensor.matmul(Q_BANK[:, j * P:(j + 1) * P], weights[:, k, :], self.hT[:, k, c * P:(c + 1) * P],
                                                    start=(k == 0), stop=(k == KD - 1))
                    last.then_inc(first_q_done, 1)
                    pe.wait_ge(first_q_copied, i + 1)
                    if i:
                        pe.wait_ge(first_sc_copied, i)
                    for j, (weights, sub) in enumerate(self.first):
                        at = (first_jobs * (i % qT_slots) + j) * P
                        last = nc.tensor.matmul(S_BANK[:, j * NKEY:(j + 1) * NKEY], qT[:, at:at + P], sub, start=True, stop=True)
                    last.then_inc(first_sc_done, 1)

                def query(j):
                    pe.wait_ge(wq_loaded, j * 16 + 16)
                    for k in range(KD):
                        last = nc.tensor.matmul(Q_BANK[:, lo:hi], wq[:, k, :], self.hT[:, k, lo:hi], start=(k == 0), stop=(k == KD - 1))
                    last.then_inc(q_done, 1)

                def score(j):
                    pe.wait_ge(keys_loaded, j * 16 + 16)
                    pe.wait_ge(q_copied, j + 1)
                    for i, c in enumerate(chunks):
                        last = nc.tensor.matmul(S_BANK[:, i * NKEY:(i + 1) * NKEY], qT[:, c * P:(c + 1) * P], keys, start=True, stop=True)
                    last.then_inc(sc_done, 1)

                pe.wait_ge(self.w_o_loaded, 16)
                project(0, 0)
                project(0, 1)
                for i in range(1, nch):
                    project(i, 0)
                    if i == 1:
                        front(0)
                    project(i, 1)
                    if i >= 2:
                        front(i - 1)
                front(nch - 1)
                pe.wait_ge(first_sc_copied, nch)
                pe.sem_inc(q_done, first_jobs)
                pe.sem_inc(sc_done, first_jobs)
                with pe.Fori(0, H // 2) as it:
                    for i in range(body):
                        j = job_of(i, it)
                        pe.wait_ge(acc_free, it * body + i + 1)
                        for g in range(NG):
                            pe.wait_ge(diag_ready, it * (body * NG) + i * NG + g + 1)
                            for k in range(GRP):
                                kk = g * GRP + k
                                for n in range(2):
                                    last = nc.tensor.matmul(acc[i % 2][n][:], diag[:, (g % 2) * GRP + k, :], ring[:, kk, D + n * 512:D + (n + 1) * 512],
                                                            start=(kk == 0), stop=(kk == TOPK - 1))
                            last.then_inc(slots_free, 1)
                            if j is not None and g == 0:
                                query(j)
                            if j is not None and g == 2:
                                pe.wait_ge(sc_copied, j)
                                score(j)

            @block.scalar
            def _(act):
                def copy_query(j):
                    act.wait_ge(q_done, j + 1)
                    nc.scalar.copy(qT[:, lo:hi], Q_BANK[:, lo:hi]).then_inc(q_copied, 1)

                def first_gates(u):
                    act.wait_ge(top_ready, u + 1)
                    nc.scalar.activation(gate[:, u, :], top, ACT.Exp, bias=nb, accum_out=es).then_inc(exp_done, 1)

                def norm(i):
                    c = chunks[i]
                    act.wait_ge(added, 2 * i + 2)
                    if i:
                        act.wait_ge(sq_done, i)
                    nc.scalar.activation(junk, self.x[:, c, :], ACT.Square, accum_out=ssq[:, c:c + 1]).then_inc(sq_done, 1)
                    act.wait_ge(mean_done, i + 1)
                    nc.scalar.activation(std[:, c:c + 1], var[:, c:c + 1], ACT.Sqrt).then_inc(sqrt_done, 1)

                def copies(i):
                    c = chunks[i]
                    for q in range(2):
                        act.wait_ge(t_done, 2 * i + q + 1)
                        nc.scalar.copy(self.hT[:, 4 * q:4 * q + 4, c * P:(c + 1) * P],
                                       self.bank[6 + q][:].rearrange("p (a b) -> p a b", a=4)).then_inc(t_copied, 1)
                    act.wait_ge(first_q_done, i + 1)
                    if i >= qT_slots:
                        act.wait_ge(first_sc_done, i + 1 - qT_slots)
                    at = first_jobs * (i % qT_slots) * P
                    nc.scalar.copy(qT[:, at:at + first_jobs * P], Q_BANK[:, 0:first_jobs * P]).then_inc(first_q_copied, 1)
                    if i < 2:
                        first_gates(i)

                in_turn(norm, copies)
                act.wait_ge(first_sc_done, nch)
                act.sem_inc(q_copied, first_jobs)
                with act.Fori(0, H // 2) as it:
                    for i in range(body):
                        u = i % 2
                        j = job_of(i, it)
                        for g in range(NG):
                            n = it * (body * NG) + i * NG + g
                            ks = slice(g * GRP, (g + 1) * GRP)
                            act.wait_ge(dots_done, n + 1)
                            nc.scalar.activation(w[:, u, ks], a[:, u, ks], ACT.Gelu).then_inc(gelu_done, 1)
                            act.wait_ge(w_ready, n + 1)
                            act.wait_ge(slots_free, n + 3)
                            for k in range(GRP):
                                last = nc.scalar.mul(diag[:, (g % 2) * GRP + k, :], self.ident[:], w[:, u, g * GRP + k:g * GRP + k + 1])
                            last.then_inc(diag_ready, 1)
                            if j is not None and g == 1:
                                act.wait_ge(sc_done, j)
                                copy_query(j)
                        act.wait_ge(top_ready, it * body + i + 3)
                        nc.scalar.activation(gate[:, u, :], top, ACT.Exp, bias=nb, accum_out=es).then_inc(exp_done, 1)

            @block.vector
            def _(dve):
                count = [0]

                def link(ins):
                    count[0] += 1
                    ins.then_inc(chain, 1)
                    dve.wait_ge(chain, count[0])

                def restart():
                    dve.sem_clear(chain)
                    count[0] = 0

                def top16(out_v, out_i, src):
                    link(nc.vector.max(out_v[:, 0:8], src))
                    link(nc.vector.max_index(out_i[:, 0:8], out_v[:, 0:8], src))
                    link(nc.vector.match_replace(src, out_v[:, 0:8], src, NEG))
                    link(nc.vector.max(out_v[:, 8:16], src))
                    link(nc.vector.max_index(out_i[:, 8:16], out_v[:, 8:16], src))

                def choose(par, c, u):
                    for side in range(2):
                        top16(val[:, side, :], ind[:, side, :], scores[:, par, c, side * NKEY:(side + 1) * NKEY])
                    link(nc.vector.tensor_copy(indf, ind))
                    link(nc.vector.tensor_tensor(C, val[:, 0, :].unsqueeze(2).broadcast_to([P, TOPK, TOPK]),
                                                 val[:, 1, :].unsqueeze(1).broadcast_to([P, TOPK, TOPK]), ALU.add))
                    top16(top, pos, C.rearrange("p a b -> p (a b)"))
                    link(nc.vector.tensor_scalar(posi[:, 0, :], pos, 4, None, ALU.logical_shift_right))
                    link(nc.vector.tensor_scalar(posi[:, 1, :], pos, TOPK - 1, None, ALU.bitwise_and))
                    for side in range(2):
                        link(nc.vector.tensor_tensor(OH, posi[:, side, :].unsqueeze(2).broadcast_to([P, TOPK, TOPK]),
                                                     iota.unsqueeze(1).broadcast_to([P, TOPK, TOPK]), ALU.is_equal))
                        link(nc.vector.tensor_tensor(OH, OH, indf[:, side, :].unsqueeze(1).broadcast_to([P, TOPK, TOPK]), ALU.mult))
                        link(nc.vector.tensor_reduce(sel[:, side, :], OH, AX.X, ALU.add))
                    link(nc.vector.scalar_tensor_tensor(out=idx[:, u, :], in0=sel[:, 0, :], scalar=float(NKEY), in1=sel[:, 1, :], op0=ALU.mult, op1=ALU.add))
                    dve.sem_inc(idx_ready, 1)
                    link(nc.vector.tensor_scalar(nb, top[:, 0:1], -1.0, None, ALU.mult))
                    dve.sem_inc(top_ready, 1)

                def finish_gates(u):
                    link(nc.vector.reciprocal(er, es))
                    link(nc.vector.tensor_scalar(gate[:, u, :], gate[:, u, :], er, None, ALU.mult))

                def copy_scores(j, par, side):
                    dve.wait_ge(sc_done, j + 1)
                    nc.vector.tensor_copy(scores[:, par, 0:nch, side * NKEY:(side + 1) * NKEY],
                                          S_BANK[:, 0:nch * NKEY].rearrange("p (c n) -> p c n", c=nch)).then_inc(sc_copied, 1)
                    dve.wait_ge(sc_copied, j + 1)

                def first_choice(u):
                    choose(0, u, u)
                    dve.wait_ge(exp_done, u + 1)
                    finish_gates(u)

                dve.wait_ge(iota_done, 1)
                link(nc.vector.tensor_copy(iota, iota_i))
                dve.wait_ge(rows_loaded, 3 * 16 * len(kinds))
                def add_and_norm(i):
                    c = chunks[i]
                    kd = kind(c)
                    for n in range(2):
                        dve.wait_ge(y_done, 2 * i + n + 1)
                        if i:
                            dve.wait_ge(added, 2 * i + n - 1)
                        nc.vector.tensor_tensor(y[:, n, :], self.bank[2 * (i % 2) + n][:], gate_a[:, kd, n * 512:(n + 1) * 512], ALU.mult).then_inc(gated, 1)
                        dve.wait_ge(gated, 2 * i + n + 1)
                        xs = self.x[:, c, n * 512:(n + 1) * 512]
                        nc.vector.tensor_tensor(xs, xs, y[:, n, :], ALU.add).then_inc(added, 1)
                    dve.wait_ge(sq_done, i + 1)
                    nc.vector.tensor_scalar(var[:, c:c + 1], ssq[:, c:c + 1], 1.0 / D, EPS, ALU.mult, ALU.add).then_inc(mean_done, 1)
                    dve.wait_ge(sqrt_done, i + 1)
                    link(nc.vector.reciprocal(rstd[:, c:c + 1], std[:, c:c + 1]))
                    hc = self.h[:, c * D:(c + 1) * D]
                    dve.wait_ge(added, 2 * i + 2)
                    link(nc.vector.scalar_tensor_tensor(out=hc, in0=self.x[:, c, :], scalar=rstd[:, c:c + 1], in1=bc[:, 2 * kd, :],
                                                        op0=ALU.mult, op1=ALU.mult))
                    nc.vector.tensor_tensor(hc, hc, bc[:, 2 * kd + 1, :], ALU.add).then_inc(h_ready, 1)

                def first_scores(i):
                    dve.wait_ge(first_sc_done, i + 1)
                    nc.vector.tensor_copy(scores[:, 0:lead, i, :], S_BANK[:, 0:first_jobs * NKEY].rearrange("p (a n) -> p a n", a=lead)).then_inc(first_sc_copied, 1)
                    dve.wait_ge(first_sc_copied, i + 1)
                    if i < 2:
                        choose(0, i, i)
                        dve.wait_ge(exp_done, i + 1)
                        finish_gates(i)

                in_turn(add_and_norm, first_scores)
                dve.sem_inc(sc_copied, first_jobs)
                dve.wait_ge(h_ready, nch)
                restart()
                dve.wait_ge(gate_loaded, 16 * len(kinds))
                dve.sem_inc(acc_free, 2)
                with dve.Fori(0, H // 2) as it:
                    for i in range(body):
                        u = i % 2
                        hd, c = place[i]
                        unit = it * body + i
                        j = job_of(i, it)
                        for g in range(NG):
                            for k in range(g * GRP, (g + 1) * GRP):
                                dve.wait_ge(gathered[k], unit * 16 + 16)
                                last = nc.vector.tensor_tensor_reduce(
                                    out=ring[:, k, 0:D], in0=ring[:, k, 0:D], in1=self.h[:, chunks[c] * D:(chunks[c] + 1) * D], scale=1.0, scalar=0.0,
                                    op0=ALU.mult, op1=ALU.add, accum_out=a[:, u, k:k + 1])
                            last.then_inc(dots_done, 1)
                            ks = slice(g * GRP, (g + 1) * GRP)
                            dve.wait_ge(gelu_done, unit * NG + g + 1)
                            nc.vector.tensor_tensor(w[:, u, ks], w[:, u, ks], gate[:, u, ks], ALU.mult).then_inc(w_ready, 1)
                        choose(place[i + 2][0] % 2, place[i + 2][1], u)
                        dve.wait_ge(exp_done, unit + 3)
                        finish_gates(u)
                        if j is not None:
                            copy_scores(j, (hd + lead) % 2, c)
                        dve.wait_ge(slots_free, unit * NG + 2 * NG)
                        for n in range(2):
                            s = acc[u][n][:]
                            link(nc.vector.tensor_tensor(s, s, gate_f[:, kind(chunks[c]), n * 512:(n + 1) * 512], ALU.mult))
                        for n in range(2):
                            xs = self.x[:, chunks[c], n * 512:(n + 1) * 512]
                            link(nc.vector.tensor_tensor(xs, xs, acc[u][n][:], ALU.add))
                        dve.sem_inc(acc_free, 1)
                        restart()

    def w_query_rows(self, layer, j):
        return self.dram["w_query"][layer, bass.ds(j, 1), :, :].rearrange("a p (k n) -> p (a k) n", k=KD)

    def key_rows(self, layer, j):
        return self.dram["keys"][layer, bass.ds(j, 1), :, :].rearrange("a p n -> p (a n)")

    def gqa_weights(self, sp):
        v, d = self.view, self.dram
        self.w_qkv = v(self.arena, 9984, KD, (H + 2 * GKV) * P)
        self.rope_g = v(self.arena, 22272, NC, 2 * P)
        self.gain_g = v(self.arena, 23296, 2, P)
        self.w_o = v(self.arena, 12 * 2 * D, H, D)
        self.w_qkv_loaded, self.w_o_loaded = self.lasting_sem("w_qkv_loaded"), self.lasting_sem("w_o_loaded")
        sp.dma_start(self.w_qkv, d["w_qkv"]).then_inc(self.w_qkv_loaded, 16)
        sp.dma_start(self.rope_g, d["rope_g"]).then_inc(self.w_qkv_loaded, 16)
        sp.dma_start(self.gain_g, d["gain_g"].broadcast_to([P, 2 * P]).rearrange("p (a b) -> p a b", a=2)).then_inc(self.w_qkv_loaded, 16)
        sp.dma_start(self.w_o, d["w_o1"]).then_inc(self.w_o_loaded, 16)

    @phase
    def gqa_in(self):
        nc, v, sem = self.nc, self.view, self.sem
        NQK = H + GKV
        V = self.gV = v(self.arena, 0, NC, GKV * P)
        qT = self.gqT = v(self.arena, 1024, H, TOK)
        kT = self.gkT = v(self.arena, 5120, GKV, TOK)
        n1 = v(self.arena, 6144, NQK, P)
        n2 = v(self.arena, 7424, NQK, P)
        n3 = v(self.arena, 8704, NQK, P)
        junk = v(self.aux, 0, NQK, P)
        ssq, var, std, rstd = (v(self.small, 128 + 40 * i, NC, NQK) for i in range(4))
        a_done, sq_done, chain, mean_done, sqrt_done, bank_free, r_ready, t_done, t_copied, v_copied = (
            sem(n) for n in ("a_done", "sq_done", "chain", "mean_done", "sqrt_done", "bank_free", "r_ready", "t_done", "t_copied", "v_copied"))

        def heads(c):
            return list(range(NQK)) if c >= CC else list(range(H, NQK))

        def src(c, j):
            b = self.bank[3 * (c % 2) + (2 if j >= H else j // 4)]
            return b[:, (j % 4 if j < H else j - H) * P:((j % 4 if j < H else j - H) + 1) * P]

        sq_before = [sum(len(heads(x)) for x in range(c)) for c in range(NC + 1)]
        t_before = [sum(3 if x >= CC else 1 for x in range(c)) for c in range(NC + 1)]

        with nc.Block() as block:
            @block.tensor
            def _(pe):
                pe.wait_ge(self.w_qkv_loaded, 48)

                def project(c):
                    if c >= 2:
                        pe.wait_ge(bank_free, c - 1)
                    for n in ((0, 1, 2) if c >= CC else (2,)):
                        for k in range(KD):
                            last = nc.tensor.matmul(self.bank[3 * (c % 2) + n][:], self.hT[:, k, c * P:(c + 1) * P], self.w_qkv[:, k, n * 512:(n + 1) * 512],
                                                    start=(k == 0), stop=(k == KD - 1))
                    last.then_inc(a_done, 1)

                def transposes(c):
                    pe.wait_ge(r_ready, c + 1)
                    groups = ([list(range(0, 4)), list(range(4, 8))] if c >= CC else []) + [[8, 9]]
                    for i, g in enumerate(groups):
                        n = t_before[c] + i
                        if n >= 2:
                            pe.wait_ge(t_copied, n - 1)
                        for jj, j in enumerate(g):
                            last = nc.tensor.transpose(self.bank[6 + n % 2][:, jj * P:(jj + 1) * P], n3[:, j, :], self.ident[:])
                        last.then_inc(t_done, 1)

                for c in range(NC):
                    project(c)
                    if c:
                        transposes(c - 1)
                transposes(NC - 1)

            @block.scalar
            def _(act):
                for c in range(NC):
                    act.wait_ge(a_done, c + 1)
                    if c:
                        act.wait_ge(sq_done, sq_before[c])
                    for j in heads(c):
                        nc.scalar.activation(junk[:, j, :], src(c, j), ACT.Square, accum_out=ssq[:, c, j:j + 1]).then_inc(sq_done, 1)
                    nc.scalar.copy(V[:, c, :], self.bank[3 * (c % 2) + 2][:, GKV * P:2 * GKV * P]).then_inc(v_copied, 1)
                    act.wait_ge(mean_done, c + 1)
                    j0 = heads(c)[0]
                    nc.scalar.activation(std[:, c, j0:], var[:, c, j0:], ACT.Sqrt).then_inc(sqrt_done, 1)

            @block.vector
            def _(dve):
                count = [0]

                def link(ins):
                    count[0] += 1
                    ins.then_inc(chain, 1)
                    dve.wait_ge(chain, count[0])

                for c in range(NC):
                    j0 = heads(c)[0]
                    nh = NQK - j0
                    dve.wait_ge(sq_done, sq_before[c + 1])
                    nc.vector.tensor_scalar(var[:, c, j0:], ssq[:, c, j0:], 1.0 / P, EPS, ALU.mult, ALU.add).then_inc(mean_done, 1)
                    dve.wait_ge(sqrt_done, c + 1)
                    link(nc.vector.reciprocal(rstd[:, c, j0:], std[:, c, j0:]))
                    for b, (lo, hi) in enumerate(((0, 4), (4, 8), (8, 10))):
                        if lo < j0:
                            continue
                        link(nc.vector.tensor_tensor(n1[:, lo:hi, :], self.bank[3 * (c % 2) + b][:, 0:(hi - lo) * P].rearrange("p (a b) -> p a b", b=P),
                                                     rstd[:, c, lo:hi].unsqueeze(2).broadcast_to([P, hi - lo, P]), ALU.mult))
                    dve.wait_ge(v_copied, c + 1)
                    dve.sem_inc(bank_free, 1)
                    for lo, hi, g in ((0, H, 0), (H, NQK, 1)):
                        if lo < j0:
                            continue
                        link(nc.vector.tensor_tensor(n1[:, lo:hi, :], n1[:, lo:hi, :], self.gain_g[:, g, :].unsqueeze(1).broadcast_to([P, hi - lo, P]), ALU.mult))
                    if c:
                        dve.wait_ge(t_done, t_before[c])
                    hs = slice(j0, NQK)
                    link(nc.vector.tensor_tensor(n3[:, hs, :], n1[:, hs, :], self.rope_g[:, c, 0:P].unsqueeze(1).broadcast_to([P, nh, P]), ALU.mult))
                    for b in range(4):
                        o = b ^ 1
                        link(nc.vector.tensor_tensor(n2[:, hs, 32 * b:32 * b + 32], n1[:, hs, 32 * o:32 * o + 32],
                                                     self.rope_g[:, c, P + 32 * b:P + 32 * b + 32].unsqueeze(1).broadcast_to([P, nh, 32]), ALU.mult))
                    link(nc.vector.tensor_tensor(n3[:, hs, :], n3[:, hs, :], n2[:, hs, :], ALU.add))
                    dve.sem_inc(r_ready, 1)
                    cols = slice(c * P, (c + 1) * P)
                    groups = ([(qT, 0, 4), (qT, 4, 4)] if c >= CC else []) + [(kT, 0, 2)]
                    for i, (dst, at, m) in enumerate(groups):
                        n = t_before[c] + i
                        dve.wait_ge(t_done, n + 1)
                        nc.vector.tensor_copy(dst[:, at:at + m, cols], self.bank[6 + n % 2][:, 0:m * P].rearrange("p (a b) -> p a b", b=P)).then_inc(t_copied, 1)

    @phase
    def gqa_attention(self):
        self.attention(
            1, list(range(CC, NC)), lambda c: TOK, lambda hd, t: self.gV[:, t, (hd // 4) * P:(hd // 4 + 1) * P],
            lambda hd, c: [(self.gqT[:, hd, c * P:(c + 1) * P], self.gkT[:, hd // 4, :])],
            1.0 / math.sqrt(P))

    def layer(self, i):
        every = list(range(NC))
        if i == 0:
            self.norm(0, SH_A, SC_A, every, self.mla_weights)
            self.mla_in()
            self.mla_attention()
            ffn = every
        else:
            self.norm(1, SH_A, SC_A, every, self.gqa_weights)
            self.gqa_in()
            self.gqa_attention()
            ffn = list(range(CC, NC))
        self.peer(i, ffn)

    @phase
    def finish(self):
        nc, v, sem = self.nc, self.view, self.sem
        gain = v(self.arena, 0, D)
        junk = v(self.aux, 0, D)
        ssq, var, std, rstd = (v(self.small, 4 * i, CC) for i in range(4))
        g_loaded, sq_done, mean_done, sqrt_done, rstd_done, o_ready, stored = (
            sem(n) for n in ("g_loaded", "sq_done", "mean_done", "sqrt_done", "rstd_done", "o_ready", "stored"))
        with nc.Block() as block:
            @block.sync
            def _(sp):
                sp.dma_start(gain, self.dram["norm_out"].broadcast_to([P, D])).then_inc(g_loaded, 16)
                for i in range(2):
                    sp.wait_ge(o_ready, i + 1)
                    sp.dma_start(self.out[0, i * P:(i + 1) * P, :], self.h[:, i * D:(i + 1) * D]).then_inc(stored, 16)
                sp.wait_ge(stored, 32)

            @block.scalar
            def _(act):
                for i in range(2):
                    if i:
                        act.wait_ge(sq_done, i)
                    nc.scalar.activation(junk, self.x[:, CC + i, :], ACT.Square, accum_out=ssq[:, i:i + 1]).then_inc(sq_done, 1)
                act.wait_ge(mean_done, 1)
                nc.scalar.activation(std, var, ACT.Sqrt).then_inc(sqrt_done, 1)

            @block.vector
            def _(dve):
                dve.wait_ge(sq_done, 2)
                nc.vector.tensor_scalar(var, ssq, 1.0 / D, EPS, ALU.mult, ALU.add).then_inc(mean_done, 1)
                dve.wait_ge(sqrt_done, 1)
                nc.vector.reciprocal(rstd, std).then_inc(rstd_done, 1)
                dve.wait_ge(rstd_done, 1)
                dve.wait_ge(g_loaded, 16)
                for i in range(2):
                    nc.vector.scalar_tensor_tensor(out=self.h[:, i * D:(i + 1) * D], in0=self.x[:, CC + i, :], scalar=rstd[:, i:i + 1], in1=gain,
                                                   op0=ALU.mult, op1=ALU.mult).then_inc(o_ready, 1)


def rope_tables(rot):
    rows = SEQ // 64
    row, col = np.repeat(np.arange(rows), 64), np.tile(np.arange(64), rows)
    half = rot // 2
    inv = 10000.0 ** (-np.arange(0, half, 2) / half)
    ar, ac = row[:, None] * inv, col[:, None] * inv
    ang = np.concatenate([ar, ar, ac, ac], axis=-1)
    sign = np.repeat([-1.0, 1.0, -1.0, 1.0], rot // 4)
    cos = np.concatenate([np.ones((CTX, rot)), np.cos(ang)])
    sin = np.concatenate([np.zeros((CTX, rot)), np.sin(ang) * sign])
    return cos.astype(np.float32), sin.astype(np.float32)


def kernel(**inputs):
    import concourse.bacc as bacc
    from concourse.bass_utils import run_bass_kernel_spmd as run

    g = {k: np.asarray(a) for k, a in inputs.items()}

    def tiles(w):
        return w.reshape(w.shape[0] // P, P, -1).transpose(1, 0, 2)

    def swap(w, n):
        s = w.shape
        return w.reshape(s[:-1] + (s[-1] // (2 * n), 2, n))[..., ::-1, :].reshape(s)

    def ahead(w):
        return np.concatenate([w, w[0:4]])

    cos, sin = rope_tables(ROPE)
    gcos, gsin = rope_tables(P)
    w_in = g["l0_mla_w_in"]
    uq = g["l0_mla_w_uq"].reshape(QR, H, NOPE + ROPE)
    uqr = uq[:, :, NOPE:]
    ukv = g["l0_mla_w_ukv"].reshape(KVR, H, 256)
    arrays = {
        "c_cols": np.stack([g["c"][0], g["c_ctx"]]).reshape(2, KD, P).transpose(2, 1, 0),
        "tokens": np.concatenate([g["ctx"][0], g["x"][0]]).reshape(NC, P, D).transpose(1, 0, 2),
        "ident": np.eye(P, dtype=np.float32),
        "ada": np.stack([g[f"l{i}_ada_w"].reshape(KD, P, ADA_ROUNDS, ADA).transpose(2, 0, 1, 3).reshape(-1, P, ADA) for i in range(LAYERS)]),
        "ada_b": np.stack([g[f"l{i}_ada_b"] for i in range(LAYERS)]),
        "gains": np.stack([np.concatenate([g[f"l{i}_norm_ffn"], g[f"l{i}_norm_mix"]]).reshape(NQ, 512) for i in range(LAYERS)]),
        "w_in": tiles(np.concatenate([w_in, swap(w_in[:, QR + KVR:], ROPE // 4)], axis=1)),
        "rope_rows": np.concatenate([cos, sin], axis=1).reshape(NC, P, 2 * ROPE).transpose(1, 0, 2),
        "rope_cols": np.concatenate([cos, sin], axis=1).T,
        "gcol": np.concatenate([g["l0_mla_q_norm"].reshape(KQ, P), g["l0_mla_kv_norm"].reshape(KKV, P)]).T,
        "w_uq": tiles(np.concatenate([uq, swap(uqr, ROPE // 4)], axis=2).reshape(QR, H * 256)),
        "w_uk": tiles(ukv[:, :, :P].reshape(KVR, H * P)),
        "w_uv": tiles(ukv[:, :, P:].reshape(KVR, H * P)),
        "w_o0": tiles(g["l0_mla_w_o"]),
        "w_o1": tiles(g["l1_gqa_w_o"]),
        "w_qkv": tiles(g["l1_gqa_w_qkv"]),
        "rope_g": np.concatenate([gcos, gsin], axis=1).reshape(NC, P, 2 * P).transpose(1, 0, 2),
        "gain_g": np.concatenate([g["l1_gqa_q_norm"], g["l1_gqa_k_norm"]])[None],
        "keys": np.stack([ahead(np.stack([g[f"l{i}_peer_k1"], g[f"l{i}_peer_k2"]], axis=1).transpose(0, 1, 3, 2).reshape(2 * H, P, NKEY)) for i in range(LAYERS)]),
        "w_query": np.stack([ahead(g[f"l{i}_peer_w_query"].reshape(KD, P, 2 * H, P).transpose(2, 1, 0, 3).reshape(2 * H, P, KD * P)) for i in range(LAYERS)]),
        "norm_out": g["norm_out"][None],
    }
    for i in range(LAYERS):
        arrays[f"uv{i}"] = np.concatenate([g[f"l{i}_peer_u"], g[f"l{i}_peer_v"]], axis=1)
    arrays = {k: np.ascontiguousarray(a) for k, a in arrays.items()}

    nc = bacc.Bacc("TRN2", target_bir_lowering=False, num_devices=1)
    dram = {k: nc.dram_tensor(f"in_{k}", a.shape, mybir.dt.from_np(a.dtype), kind="ExternalInput").ap() for k, a in arrays.items()}
    dram["uv"] = [dram[f"uv{i}"] for i in range(LAYERS)]
    out = nc.dram_tensor("out", (1, SEQ, D), F32, kind="ExternalOutput").ap()
    Kernel(nc, dram, out).build()
    r = run(nc, [{f"in_{k}": a for k, a in arrays.items()}], core_ids=[0])
    return r.results[0]["out"]
```

```python
import math
from contextlib import ExitStack

import numpy as np
import concourse.bass as bass
from concourse import mybir

F32, BF16, U32, I32 = mybir.dt.float32, mybir.dt.bfloat16, mybir.dt.uint32, mybir.dt.int32
ALU = mybir.AluOpType
ACT = mybir.ActivationFunctionType
AX = mybir.AxisListType

P = 128
D = 1024
KD = D // P
CTX, SEQ = 256, 256
TOK = CTX + SEQ
NC = TOK // P
CC = CTX // P
EPS = 1e-6
H = 8
NOPE, ROPE = 128, 64
QR, KVR = 384, 256
KQ, KKV = QR // P, KVR // P
HALF = 384
GKV = 2
NKEY = 128
TOPK = 16
MODW = 6 * D
LAYERS = 2
SH_A, SC_A, G_A, SH_F, SC_F, G_F = range(6)
LAT, CON = 0, 1
NEG = -3.0e38
GRP = 4
NG = TOPK // GRP
RING = TOPK
Q = 32
NQ = P // Q
ADA = NQ * 512
ADA_ROUNDS = MODW // ADA


def kind(c):
    return CON if c < CC else LAT


def phase(build):
    def built(self, *args, **more):
        self.phase_sems = []
        build(self, *args, **more)
        self.nc.clear_and_free_semaphores(self.phase_sems)
        self.nc.all_engine_barrier()
    return built


class Kernel:
    def __init__(self, nc, dram, out):
        self.nc, self.dram, self.out = nc, dram, out
        self.names = 0

    def sem(self, name):
        self.names += 1
        handle = self.nc.alloc_semaphore(name=f"{name}_{self.names}")
        self.phase_sems.append(handle)
        return handle

    def lasting_sem(self, name):
        self.names += 1
        return self.ctx.enter_context(self.nc.semaphore(f"{name}_{self.names}"))

    def view(self, region, at, *shape, dtype=None):
        n = int(np.prod(shape))
        v = region[:, at:at + n]
        if dtype is not None:
            v = v.bitcast(dtype)
        if len(shape) == 2:
            v = v.rearrange("p (a b) -> p a b", a=shape[0])
        if len(shape) == 3:
            v = v.rearrange("p (a b c) -> p a b c", a=shape[0], b=shape[1])
        return v

    def build(self):
        nc = self.nc
        with ExitStack() as ctx:
            self.ctx = ctx
            sb = lambda n, s, d=F32: ctx.enter_context(nc.sbuf_tensor(n, s, d))
            self.ident = sb("ident", [P, P])
            self.x = sb("x", [P, NC, D])
            self.h = sb("h", [P, NC * D])
            self.hT = self.view(sb("hT", [P, KD * TOK]), 0, KD, TOK)
            self.arena = sb("arena", [P, RING * 2 * D])
            self.aux = sb("aux", [P, 7296])
            self.small = sb("small", [P, 384 + P])
            self.bank = [ctx.enter_context(nc.psum_tensor(f"bank{i}", [P, 512], F32)) for i in range(8)]
            self.loaded_x = self.lasting_sem("loaded_x")
            self.adaln()
            self.layer(0)
            self.layer(1)

    def ada_columns(self, vector, i):
        return vector[:, i * ADA:(i + 1) * ADA].rearrange("k (s n) -> s k n", s=NQ)

    def ada_load_rows(self, layer, i, rows, eng, loaded):
        bias = self.ada_columns(self.dram["ada_b"][layer:layer + 1, :], i)
        for s in range(NQ):
            eng.dma_start(rows[s * Q:(s + 1) * Q], bias[s].broadcast_to([Q, 512])).then_inc(loaded, 16)

    def ada_load_gains(self, layer, pieces, gains, eng, loaded):
        for s in pieces:
            eng.dma_start(gains[s * Q:(s + 1) * Q], self.dram["gains"][layer, s:s + 1, :].broadcast_to([Q, 512])).then_inc(loaded, 16)

    def ada_store(self, layer, i, rows, eng, stored):
        dst = self.ada_columns(self.modd[:, layer * MODW:(layer + 1) * MODW], i)
        for s in range(NQ):
            eng.dma_start(dst[s], rows[s * Q:s * Q + 2]).then_inc(stored, 16)

    def ada_products(self, bank, k, weights):
        for s in range(NQ):
            last = self.nc.tensor.matmul(bank[s * Q:(s + 1) * Q, :], self.cs[:, k, :], weights[:, s * 512:(s + 1) * 512],
                                         start=(k == 0), stop=(k == KD - 1))
        return last

    def ada_finish(self, dve, i, n, bank, rows, gains, bank_read, scaled):
        self.nc.vector.tensor_tensor(rows, rows, bank[:], ALU.add).then_inc(bank_read, 1)
        dve.wait_ge(bank_read, n + 1)
        for at, seg in ((0, SC_A), (2, SC_F)):
            if i == at:
                first = (seg * D - i * ADA) // 512 * Q
                r = rows[first:first + 2 * Q]
                self.nc.vector.scalar_tensor_tensor(out=r, in0=r, scalar=1.0, in1=gains[first:first + 2 * Q], op0=ALU.add, op1=ALU.mult).then_inc(scaled, 1)

    def ada_weights(self, layer, i, k):
        return self.dram["ada"][layer, bass.ds(i * KD + k, 1), :, :].rearrange("a p n -> p (a n)")

    @phase
    def adaln(self):
        nc, d, v = self.nc, self.dram, self.view
        slots = v(self.arena, 0, KD, ADA)
        rows, gains = self.aux[:, 0:512], self.aux[:, 512:1024]
        self.cs = v(self.aux, 7040, KD, Q)
        cols = v(self.small, 0, KD, 2)
        sem = self.sem
        loaded_c, silu_done, cs_zero, rows_loaded, w_used, bank_read, scaled, stored = (
            sem(n) for n in ("loaded_c", "silu_done", "cs_zero", "rows_loaded", "w_used", "bank_read", "scaled", "stored"))
        w_loaded = [sem(f"w_loaded{k}") for k in range(KD)]
        self.modd = nc.dram_tensor("mod_rows", (2, LAYERS * MODW), F32, kind="Internal").ap()
        self.mla_places()
        bank = self.bank[0]
        with nc.Block() as block:
            @block.sync
            def _(sp):
                for k in range(KD):
                    sp.dma_start(slots[:, k, :], self.ada_weights(0, 0, k)).then_inc(w_loaded[k], 16)
                sp.dma_start(self.x[:], d["tokens"]).then_inc(self.loaded_x, 16)
                sp.dma_start(self.ident[:], d["ident"]).then_inc(self.loaded_x, 16)
                sp.wait_ge(scaled, 1)
                self.ada_store(0, 0, rows, sp, stored)
                sp.dma_start(self.w_in[:, 0:KD // 2], d["w_in"][:, 0:KD // 2]).then_inc(self.w_in_loaded, 16)
                sp.dma_start(self.rope_rows, d["rope_rows"]).then_inc(self.w_in_loaded, 16)
                sp.dma_start(self.gcol, d["gcol"]).then_inc(self.w_in_loaded, 16)
                sp.wait_ge(stored, 16 * NQ)

            @block.scalar
            def _(act):
                act.dma_start(cols, d["c_cols"]).then_inc(loaded_c, 16)
                self.ada_load_rows(0, 0, rows, act, rows_loaded)
                self.ada_load_gains(0, (2, 3), gains, act, rows_loaded)
                act.wait_ge(loaded_c, 16)
                act.wait_ge(cs_zero, 1)
                nc.scalar.activation(self.cs[:, :, 0:2], cols, ACT.Silu).then_inc(silu_done, 1)

            @block.tensor
            def _(pe):
                pe.wait_ge(silu_done, 1)
                for k in range(KD):
                    pe.wait_ge(w_loaded[k], 16)
                    self.ada_products(bank, k, slots[:, k, :]).then_inc(w_used, 1)

            @block.vector
            def _(dve):
                nc.vector.memset(self.cs, 0.0).then_inc(cs_zero, 1)
                dve.wait_ge(rows_loaded, 16 * (NQ + 2))
                dve.wait_ge(w_used, KD)
                self.ada_finish(dve, 0, 0, bank, rows, gains, bank_read, scaled)

    def norm_steps(self, layer, order, bc, junk):
        nc, sem = self.nc, self.sem
        ssq, var, std, rstd = (self.view(self.small, 64 + 4 * i, NC) for i in range(4))
        bc_loaded = sem("bc_loaded_first"), sem("bc_loaded_second")
        sq_done, mean_done, sqrt_done, h_step, h_ready, nt_done, nt_copied = (
            sem(n) for n in ("sq_done", "mean_done", "sqrt_done", "h_step", "h_ready", "nt_done", "nt_copied"))
        banks = self.bank[6], self.bank[7]

        class Steps:
            copied = nt_copied

            def load(sp, places=(0, 1)):
                for place in places:
                    kd = list(dict.fromkeys(kind(c) for c in order))[place]
                    for j, seg in enumerate((SC_A, SH_A)):
                        at = layer * MODW + seg * D
                        sp.dma_start(bc[:, 2 * kd + j, :], self.modd[kd:kd + 1, at:at + D].broadcast_to([P, D])).then_inc(bc_loaded[place], 16)

            def statistics(act):
                for i, c in enumerate(order):
                    if i:
                        act.wait_ge(sq_done, i)
                    nc.scalar.activation(junk, self.x[:, c, :], ACT.Square, accum_out=ssq[:, i:i + 1]).then_inc(sq_done, 1)
                    if i == 0:
                        act.wait_ge(mean_done, 1)
                        nc.scalar.activation(std[:, 0:1], var[:, 0:1], ACT.Sqrt).then_inc(sqrt_done, 1)
                act.wait_ge(mean_done, 2)
                nc.scalar.activation(std[:, 1:], var[:, 1:], ACT.Sqrt).then_inc(sqrt_done, 1)

            def copies(act, i):
                c = order[i]
                for q in range(2):
                    act.wait_ge(nt_done, 2 * i + q + 1)
                    nc.scalar.copy(self.hT[:, 4 * q:4 * q + 4, c * P:(c + 1) * P], banks[q][:].rearrange("p (a b) -> p a b", a=4)).then_inc(nt_copied, 1)

            def rows(dve):
                steps = 0
                for i, c in enumerate(order):
                    if i < 2:
                        n = slice(0, 1) if i == 0 else slice(1, NC)
                        dve.wait_ge(sq_done, 1 if i == 0 else NC)
                        nc.vector.tensor_scalar(var[:, n], ssq[:, n], 1.0 / D, EPS, ALU.mult, ALU.add).then_inc(mean_done, 1)
                        dve.wait_ge(sqrt_done, i + 1)
                        nc.vector.reciprocal(rstd[:, n], std[:, n]).then_inc(h_step, 1)
                        steps += 1
                        dve.wait_ge(h_step, steps)
                    if i == 0 or kind(c) != kind(order[i - 1]):
                        dve.wait_ge(bc_loaded[0 if i == 0 else 1], 32)
                    hc = self.h[:, c * D:(c + 1) * D]
                    nc.vector.scalar_tensor_tensor(out=hc, in0=self.x[:, c, :], scalar=rstd[:, i:i + 1], in1=bc[:, 2 * kind(c), :],
                                                   op0=ALU.mult, op1=ALU.mult).then_inc(h_step, 1)
                    steps += 1
                    dve.wait_ge(h_step, steps)
                    nc.vector.tensor_tensor(hc, hc, bc[:, 2 * kind(c) + 1, :], ALU.add).then_inc(h_ready, 1)

            def transposes(pe, i):
                c = order[i]
                pe.wait_ge(h_ready, i + 1)
                if i:
                    pe.wait_ge(nt_copied, 2 * i)
                for q in range(2):
                    for k in range(4):
                        kk = 4 * q + k
                        last = nc.tensor.transpose(banks[q][:, k * P:(k + 1) * P], self.h[:, c * D + kk * P:c * D + (kk + 1) * P], self.ident[:])
                    last.then_inc(nt_done, 1)

        return Steps

    def mla_places(self):
        v = self.view
        self.w_in = v(self.arena, 16384, KD, 2 * HALF)
        self.rope_rows = v(self.arena, 22528, NC, 2 * ROPE)
        self.w_uq = v(self.arena, 24576, KQ, H * 256)
        self.w_uk = v(self.arena, 11264, KKV, H * P)
        self.w_uv = v(self.arena, 13312, KKV, H * P)
        self.rope_cols = v(self.arena, 7168, TOK)
        self.gcol = v(self.small, 80, 5)
        self.w_o = v(self.arena, 8 * 2 * D, H, D)
        self.w_in_rest_loaded = self.lasting_sem("w_in_rest_loaded")
        self.w_in_loaded, self.w_up_loaded, self.w_o_loaded = self.lasting_sem("w_in_loaded"), self.lasting_sem("w_up_loaded"), self.lasting_sem("w_o_loaded")

    def mla_weights(self, sp):
        d = self.dram
        sp.dma_start(self.w_uq, d["w_uq"]).then_inc(self.w_up_loaded, 16)
        sp.dma_start(self.w_uk, d["w_uk"]).then_inc(self.w_up_loaded, 16)
        sp.dma_start(self.w_uv, d["w_uv"]).then_inc(self.w_up_loaded, 16)
        sp.dma_start(self.rope_cols, d["rope_cols"]).then_inc(self.w_up_loaded, 16)

    @phase
    def mla_in(self):
        nc, v, sem = self.nc, self.view, self.sem
        hT, rr = self.hT, self.rope_rows
        cT = self.cT = v(self.arena, 8192, 6, TOK)
        an = v(self.aux, 0, 2, 2 * HALF)
        kr = v(self.aux, 1536, 2, 2 * ROPE)
        junk = v(self.aux, 1792, 640)
        ssq, var, std, rstd = (v(self.small, 96 + 8 * i, NC, 2) for i in range(4))
        a_done, sq_done, mean_done, sqrt_done, rstd_done = (sem(n) for n in ("a_done", "sq_done", "mean_done", "sqrt_done", "rstd_done"))
        an_ready_a = sem("an_scaled")
        norm = self.norm_steps(0, list(range(NC)), v(self.arena, 0, 4, D), v(self.arena, 4 * D, D))
        an_ready, kr_step, bank_free, t_done, t_copied = (sem(n) for n in ("an_ready", "kr_step", "bank_free", "t_done", "t_copied"))
        with nc.Block() as block:
            @block.sync
            def _(sp):
                norm.load(sp, (0,))
                sp.dma_start(self.w_in[:, KD // 2:], self.dram["w_in"][:, KD // 2:]).then_inc(self.w_in_rest_loaded, 16)
                norm.load(sp, (1,))
                self.mla_weights(sp)

            @block.tensor
            def _(pe):
                pe.wait_ge(self.loaded_x, 32)

                def project(c):
                    norm.transposes(pe, c)
                    if c == 0:
                        pe.wait_ge(self.w_in_loaded, 48)
                    pe.wait_ge(norm.copied, 2 * c + 2)
                    for half in range(2):
                        if c >= 2:
                            pe.wait_ge(bank_free, c - 1)
                        for k in range(KD):
                            if c == 0 and half == 0 and k == KD // 2:
                                pe.wait_ge(self.w_in_rest_loaded, 16)
                            last = nc.tensor.matmul(self.bank[2 * (c % 2) + half][:, 0:HALF], hT[:, k, c * P:(c + 1) * P],
                                                    self.w_in[:, k, half * HALF:(half + 1) * HALF], start=(k == 0), stop=(k == KD - 1))
                        last.then_inc(a_done, 1)

                def transposes(c):
                    pe.wait_ge(an_ready, c + 1)
                    if c >= 1:
                        pe.wait_ge(t_copied, 6 * c)
                    for j in range(6):
                        last = nc.tensor.transpose(self.bank[4 + j // 3][:, (j % 3) * P:(j % 3 + 1) * P], an[:, c % 2, j * P:(j + 1) * P], self.ident[:])
                        if j % 3 == 2:
                            last.then_inc(t_done, 1)

                for c in range(NC):
                    project(c)
                    if c:
                        transposes(c - 1)
                transposes(NC - 1)

            @block.scalar
            def _(act):
                act.wait_ge(self.loaded_x, 32)
                norm.statistics(act)
                norm.copies(act, 0)
                for c in range(NC):
                    if c + 1 < NC:
                        norm.copies(act, c + 1)
                    act.wait_ge(a_done, 2 * c + 2)
                    b = self.bank[2 * (c % 2)], self.bank[2 * (c % 2) + 1]
                    if c:
                        act.wait_ge(sq_done, 2 * c)
                    nc.scalar.activation(junk[:, 0:QR], b[0][:, 0:QR], ACT.Square, accum_out=ssq[:, c, 0:1]).then_inc(sq_done, 1)
                    nc.scalar.activation(junk[:, QR:QR + KVR], b[1][:, 0:KVR], ACT.Square, accum_out=ssq[:, c, 1:2]).then_inc(sq_done, 1)
                    act.wait_ge(mean_done, 2 * c + 2)
                    nc.scalar.activation(std[:, c, :], var[:, c, :], ACT.Sqrt).then_inc(sqrt_done, 1)
                    act.wait_ge(rstd_done, c + 1)
                    if c >= 2:
                        act.wait_ge(t_done, 2 * (c - 1))
                    nc.scalar.mul(an[:, c % 2, 0:QR], b[0][:, 0:QR], rstd[:, c, 0:1]).then_inc(an_ready_a, 1)
                    nc.scalar.mul(an[:, c % 2, QR:QR + KVR], b[1][:, 0:KVR], rstd[:, c, 1:2]).then_inc(an_ready_a, 1)

            @block.vector
            def _(dve):
                norm.rows(dve)
                step = 0
                for c in range(NC):
                    b1 = self.bank[2 * (c % 2) + 1]
                    dve.wait_ge(sq_done, 2 * c + 2)
                    for j, width in enumerate((QR, KVR)):
                        nc.vector.tensor_scalar(var[:, c, j:j + 1], ssq[:, c, j:j + 1], 1.0 / width, EPS, ALU.mult, ALU.add).then_inc(mean_done, 1)
                    if c >= 1:
                        dve.wait_ge(kr_step, step)
                    if c >= 2:
                        dve.wait_ge(t_done, 2 * (c - 1))
                    dst = an[:, c % 2, QR + KVR:QR + KVR + ROPE]
                    nc.vector.tensor_tensor(kr[:, 0, 0:ROPE], b1[:, KVR:KVR + ROPE], rr[:, c, 0:ROPE], ALU.mult).then_inc(kr_step, 1)
                    nc.vector.tensor_tensor(kr[:, 1, 0:ROPE], b1[:, KVR + ROPE:KVR + 2 * ROPE], rr[:, c, ROPE:2 * ROPE], ALU.mult).then_inc(kr_step, 1)
                    dve.wait_ge(kr_step, step + 2)
                    nc.vector.tensor_tensor(dst, kr[:, 0, 0:ROPE], kr[:, 1, 0:ROPE], ALU.add).then_inc(kr_step, 1)
                    dve.wait_ge(kr_step, step + 3)
                    nc.vector.tensor_copy(an[:, c % 2, QR + KVR + ROPE:2 * HALF], dst).then_inc(kr_step, 1)
                    step += 4
                    dve.wait_ge(sqrt_done, c + 1)
                    nc.vector.reciprocal(rstd[:, c, :], std[:, c, :]).then_inc(rstd_done, 1)
                    dve.wait_ge(an_ready_a, 2 * c + 2)
                    dve.wait_ge(kr_step, step)
                    dve.sem_inc(an_ready, 1)
                    dve.sem_inc(bank_free, 1)
                    for j in range(6):
                        dve.wait_ge(t_done, 2 * c + j // 3 + 1)
                        src, dst = self.bank[4 + j // 3][:, (j % 3) * P:(j % 3 + 1) * P], cT[:, j, c * P:(c + 1) * P]
                        if j < 5:
                            nc.vector.tensor_scalar(dst, src, self.gcol[:, j:j + 1], None, ALU.mult).then_inc(t_copied, 1)
                        else:
                            nc.vector.tensor_copy(dst, src).then_inc(t_copied, 1)

    def attention(self, layer, chunks, keys_of, v_rows, score_terms, scale, head_proj=None, pre=None, between=None):
        nc, v, sem = self.nc, self.view, self.sem
        probs = v(self.aux, 0, 2, TOK)
        pT = v(self.aux, 1024, 2, TOK)
        OT = self.hT
        nmax, nbias, rsum, rinv = (v(self.small, 128 + 32 * i, 32) for i in range(4))
        s_done, mx, mx_done, exp_done, rinv_done, p_ready, pt_done, pt_copied, pv_done, o_done, o_copied = (
            sem(n) for n in ("s_done", "mx", "mx_done", "exp_done", "rinv_done", "p_ready", "pt_done", "pt_copied", "pv_done", "o_done", "o_copied"))
        proj_done = sem("proj_done")
        nch = len(chunks)
        units = [(hd, c) for hd in range(H) for c in chunks]
        U = len(units)
        S_BANK, T_BANK, O_BANK = (3, 4), (5, 6), 7
        lo, hi = chunks[0] * P, (chunks[-1] + 1) * P

        with nc.Block() as block:
            @block.sync
            def _(sp):
                if pre:
                    pre("sp", sp)
                self.first_queries(layer, sp)
                if between:
                    between("sp", sp, 0)

            @block.tensor
            def _(pe):
                if pre:
                    pre("pe", pe)
                def proj(hd):
                    head_proj("pe", pe, hd, proj_done)

                def scores(u):
                    hd, c = units[u]
                    if head_proj:
                        head_proj("scores", pe, hd)
                    if u >= 2:
                        pe.wait_ge(exp_done, u - 1)
                    terms = score_terms(hd, c)
                    for i, (q, k) in enumerate(terms):
                        last = nc.tensor.matmul(self.bank[S_BANK[u % 2]][:, 0:keys_of(c)], q, k, start=(i == 0), stop=(i == len(terms) - 1))
                    last.then_inc(s_done, 1)

                def transposes(u):
                    c = units[u][1]
                    pe.wait_ge(p_ready, u + 1)
                    if u >= 2:
                        pe.wait_ge(pt_copied, u - 1)
                    for t in range(keys_of(c) // P):
                        last = nc.tensor.transpose(self.bank[T_BANK[u % 2]][:, t * P:(t + 1) * P], probs[:, u % 2, t * P:(t + 1) * P], self.ident[:])
                    last.then_inc(pt_done, 1)

                def values(u):
                    hd, c = units[u]
                    pe.wait_ge(pt_copied, u + 1)
                    if u % nch == 0 and hd:
                        pe.wait_ge(o_copied, hd)
                    n = keys_of(c) // P
                    for t in range(n):
                        last = nc.tensor.matmul(self.bank[O_BANK][:, c * P:(c + 1) * P], v_rows(hd, t), pT[:, u % 2, t * P:(t + 1) * P],
                                                start=(t == 0), stop=(t == n - 1))
                    last.then_inc(pv_done, 1)

                if head_proj:
                    proj(0)
                for u in range(U + 2):
                    if u < U:
                        scores(u)
                        if head_proj and u % nch == 1 and units[u][0] + 1 < H:
                            proj(units[u][0] + 1)
                    if 1 <= u <= U:
                        transposes(u - 1)
                    if u >= 2:
                        values(u - 2)
                    if between:
                        between("pe", pe, u)

            @block.scalar
            def _(act):
                if pre:
                    pre("act", act)

                def exps(u):
                    c = units[u][1]
                    act.wait_ge(mx_done, u + 1)
                    if u >= 2:
                        act.wait_ge(pt_done, u - 1)
                    nc.scalar.activation(probs[:, u % 2, 0:keys_of(c)], self.bank[S_BANK[u % 2]][:, 0:keys_of(c)], ACT.Exp,
                                         bias=nbias[:, u:u + 1], scale=scale, accum_out=rsum[:, u:u + 1]).then_inc(exp_done, 1)

                def copy_pt(u):
                    c = units[u][1]
                    act.wait_ge(pt_done, u + 1)
                    if u >= 2:
                        act.wait_ge(pv_done, u - 1)
                    nc.scalar.copy(pT[:, u % 2, 0:keys_of(c)], self.bank[T_BANK[u % 2]][:, 0:keys_of(c)]).then_inc(pt_copied, 1)

                if head_proj:
                    head_proj("act", act, 0, proj_done, s_done)
                for u in range(U + 1):
                    if u < U:
                        exps(u)
                        if head_proj and u % nch == 1 and units[u][0] + 1 < H:
                            head_proj("act", act, units[u][0] + 1, proj_done, s_done)
                    if u >= 1:
                        copy_pt(u - 1)

            @block.vector
            def _(dve):
                if pre:
                    pre("dve", dve)

                def maxima(u):
                    c = units[u][1]
                    dve.wait_ge(s_done, u + 1)
                    nc.vector.tensor_reduce(nmax[:, u:u + 1], self.bank[S_BANK[u % 2]][:, 0:keys_of(c)], AX.X, ALU.max, negate=True).then_inc(mx, 1)
                    dve.wait_ge(mx, u + 1)
                    nc.vector.tensor_scalar(nbias[:, u:u + 1], nmax[:, u:u + 1], scale, None, ALU.mult).then_inc(mx_done, 1)

                def normalise(u):
                    c = units[u][1]
                    dve.wait_ge(exp_done, u + 1)
                    nc.vector.reciprocal(rinv[:, u:u + 1], rsum[:, u:u + 1]).then_inc(rinv_done, 1)
                    dve.wait_ge(rinv_done, u + 1)
                    pr = probs[:, u % 2, 0:keys_of(c)]
                    nc.vector.tensor_scalar(pr, pr, rinv[:, u:u + 1], None, ALU.mult).then_inc(p_ready, 1)

                def copy_out(hd):
                    dve.wait_ge(pv_done, nch * (hd + 1))
                    nc.vector.tensor_copy(OT[:, hd, lo:hi], self.bank[O_BANK][:, lo:hi]).then_inc(o_copied, 1)

                if head_proj:
                    head_proj("dve", dve, 0, proj_done, s_done)
                for u in range(U + 1):
                    if u >= 1:
                        normalise(u - 1)
                    if u < U:
                        maxima(u)
                        if head_proj and u % nch == 1 and units[u][0] + 1 < H:
                            head_proj("dve", dve, units[u][0] + 1, proj_done, s_done)
                    if u > nch and (u - 1) % nch == 0:
                        copy_out((u - 1) // nch - 1)
                    if between:
                        between("dve", dve, u)
                if nch > 1:
                    copy_out(H - 1)

    @phase
    def mla_attention(self):
        nc, v = self.nc, self.view
        cT = self.cT
        V = v(self.arena, 0, NC, D)
        qn, qr, kn = (v(self.arena, 4096 + 1024 * i, 2, TOK) for i in range(3))
        v_done, v_copied = self.sem("v_done"), self.sem("v_copied")
        qk_copied, rot_copied = self.sem("qk_copied"), self.sem("rot_copied")
        ada_slots = [v(self.h, 0, ADA), v(self.h, ADA, ADA), v(self.arena, 30720, ADA)]
        ada_gains = self.arena[:, 15360:15872], self.aux[:, 6272:6784]
        rows_at = (self.aux[:, 3200:3712], self.arena[:, 15872:16384]) + tuple(self.aux[:, 4736 + 512 * i:5248 + 512 * i] for i in range(3))
        gain_pieces = (0, 1), (0, 1, 2, 3)
        rounds = [(0, 1), (0, 2), (1, 0), (1, 1), (1, 2)]
        w_loaded = [self.sem(f"ada_loaded{i}") for i in range(len(ada_slots))]
        w_used, bank_read, scaled, rows_loaded, stored = (self.sem(n) for n in ("ada_used", "ada_bank_read", "ada_scaled", "ada_rows_loaded", "ada_stored"))
        ada_bank = self.bank[2]
        steps = len(rounds) * KD
        ada_first, ada_last = 2, H * NC - 2

        def ada_steps(u):
            n, m = max(u - ada_first, 0), ada_last - ada_first
            return range(min(n * steps // m, steps), min((n + 1) * steps // m, steps)) if u >= ada_first else range(0)

        def pre(who, eng):
            if who == "sp":
                eng.dma_start(self.w_o, self.dram["w_o0"]).then_inc(self.w_o_loaded, 16)
            if who == "pe":
                eng.wait_ge(self.w_up_loaded, 64)
                for c in range(NC):
                    for n in range(2):
                        for k in range(KKV):
                            last = nc.tensor.matmul(self.bank[2 * c + n][:], cT[:, KQ + k, c * P:(c + 1) * P], self.w_uv[:, k, n * 512:(n + 1) * 512],
                                                    start=(k == 0), stop=(k == KKV - 1))
                        last.then_inc(v_done, 1)
                eng.wait_ge(v_copied, 8)
            if who == "act":
                for i in range(0, 8, 2):
                    eng.wait_ge(v_done, i + 1)
                    nc.scalar.copy(V[:, i // 2, 0:512], self.bank[i][:]).then_inc(v_copied, 1)
            if who == "dve":
                for i in range(1, 8, 2):
                    eng.wait_ge(v_done, i + 1)
                    nc.vector.tensor_copy(V[:, i // 2, 512:1024], self.bank[i][:]).then_inc(v_copied, 1)

        def between(who, eng, u):
            if who == "sp":
                for (layer, i), rows in zip(rounds, rows_at):
                    self.ada_load_rows(layer, i, rows, eng, rows_loaded)
                for layer in range(LAYERS):
                    self.ada_load_gains(layer, gain_pieces[layer], ada_gains[layer], eng, rows_loaded)
                for n in range(steps):
                    layer, i = rounds[n // KD]
                    if n >= len(ada_slots):
                        eng.wait_ge(w_used, n - len(ada_slots) + 1)
                    eng.dma_start(ada_slots[n % len(ada_slots)], self.ada_weights(layer, i, n % KD)).then_inc(w_loaded[n % len(ada_slots)], 16)
                eng.wait_ge(bank_read, len(rounds))
                eng.wait_ge(scaled, 3)
                for (layer, i), rows in zip(rounds, rows_at):
                    self.ada_store(layer, i, rows, eng, stored)
                eng.wait_ge(stored, 16 * NQ * len(rounds))
            for n in ada_steps(u):
                if who == "pe":
                    eng.wait_ge(w_loaded[n % len(ada_slots)], 16 * (n // len(ada_slots) + 1))
                    if n and n % KD == 0:
                        eng.wait_ge(bank_read, n // KD)
                    self.ada_products(ada_bank, n % KD, ada_slots[n % len(ada_slots)]).then_inc(w_used, 1)
                if who == "dve" and n % KD == KD - 1:
                    r = n // KD
                    if r == 0:
                        eng.wait_ge(rows_loaded, 16 * (NQ * len(rounds) + len(gain_pieces[0]) + len(gain_pieces[1])))
                    eng.wait_ge(w_used, n + 1)
                    self.ada_finish(eng, rounds[r][1], r, ada_bank, rows_at[r], ada_gains[rounds[r][0]], bank_read, scaled)

        def head_proj(who, eng, hd, *sems):
            if who == "scores":
                eng.wait_ge(qk_copied, 2 * hd + 2)
                eng.wait_ge(rot_copied, hd + 1)
                return
            if who == "pe":
                done, = sems
                for j in range(3):
                    if j == 0 and hd:
                        eng.wait_ge(qk_copied, 2 * hd)
                    if j == 1 and hd:
                        eng.wait_ge(rot_copied, hd)
                    if j == 2:
                        eng.wait_ge(qk_copied, 2 * hd + 1)
                    src, w, tiles = [(0, self.w_uq[:, :, hd * 256:hd * 256 + 128], KQ), (0, self.w_uq[:, :, hd * 256 + 128:hd * 256 + 256], KQ),
                                     (KQ, self.w_uk[:, :, hd * P:(hd + 1) * P], KKV)][j]
                    for k in range(tiles):
                        last = nc.tensor.matmul(self.bank[j % 2][:], w[:, k, :], cT[:, src + k, :], start=(k == 0), stop=(k == tiles - 1))
                    last.then_inc(done, 1)
                return
            done, s_done = sems
            if hd >= 2:
                eng.wait_ge(s_done, NC * (hd - 1))
            if who == "act":
                for j, dst in ((0, qn), (2, kn)):
                    eng.wait_ge(done, 3 * hd + j + 1)
                    nc.scalar.copy(dst[:, hd % 2, :], self.bank[j % 2][:]).then_inc(qk_copied, 1)
            else:
                eng.wait_ge(done, 3 * hd + 2)
                nc.vector.tensor_tensor(qr[:, hd % 2, :], self.bank[1][:], self.rope_cols, ALU.mult).then_inc(rot_copied, 1)

        self.attention(
            0, list(range(NC)), lambda c: CTX if c < CC else TOK, lambda hd, t: V[:, t, hd * P:(hd + 1) * P],
            lambda hd, c: [(qn[:, hd % 2, c * P:(c + 1) * P], kn[:, hd % 2, 0:CTX if c < CC else TOK]),
                           (qr[:, hd % 2, c * P:(c + 1) * P], cT[:, 5, 0:CTX if c < CC else TOK])],
            1.0 / math.sqrt(NOPE + ROPE), head_proj, pre, between)

    def first_queries(self, layer, sp):
        v = self.view
        self.wq = v(self.aux, 2048, KD, P)
        self.keys = v(self.aux, 3072, NKEY)
        self.diag = v(self.aux, 3712, 2 * GRP, P)
        self.first = [(self.wq, self.keys), (v(self.aux, 3712, KD, P), v(self.small, 384, NKEY))]
        if layer == 1:
            for side in range(2):
                self.first.append((v(self.h, side * KD * P, KD, P), self.x[:, 0, side * NKEY:(side + 1) * NKEY]))
        self.first_loaded = self.lasting_sem("first_loaded")
        for j, (wq, keys) in enumerate(self.first):
            sp.dma_start(wq, self.w_query_rows(layer, j)).then_inc(self.first_loaded, 16)
            sp.dma_start(keys, self.key_rows(layer, j)).then_inc(self.first_loaded, 16)

    @phase
    def peer(self, layer, chunks):
        nc, v, sem = self.nc, self.view, self.sem
        nch = len(chunks)
        lead = 2 // (nch // 2)
        body = 2 * nch
        lo, hi = chunks[0] * P, (chunks[-1] + 1) * P
        ring = v(self.arena, 0, RING, 2 * D)
        scores = v(self.aux, 0, 2, NC, 2 * NKEY)
        wq, keys, diag = self.wq, self.keys, self.diag
        qT = v(self.aux, 3200, TOK)
        C = v(self.aux, 4736, TOPK, TOPK)
        OH = v(self.aux, 4992, TOPK, TOPK)
        gate_f = v(self.aux, 5248, 2, D)
        sm = self.small
        val = v(sm, 0, 2, TOPK)
        ind = v(sm, 32, 2, TOPK, dtype=U32)
        indf = v(sm, 64, 2, TOPK)
        top = v(sm, 96, TOPK)
        pos = v(sm, 112, TOPK, dtype=U32)
        posi = v(sm, 128, 2, TOPK, dtype=U32)
        sel = v(sm, 160, 2, TOPK)
        idx = v(sm, 192, 2, TOPK, dtype=I32)
        gate = v(sm, 224, 2, TOPK)
        a = v(sm, 256, 2, TOPK)
        w = v(sm, 288, 2, TOPK)
        iota = v(sm, 320, TOPK)
        iota_i = v(sm, 336, TOPK, dtype=I32)
        nb, es, er = sm[:, 352:353], sm[:, 354:355], sm[:, 356:357]
        before = 3 * GRP * 2 * D
        bc = v(self.arena, before, 4, D)
        gate_a = v(self.arena, before + 4 * D, 2, D)
        y = v(self.arena, before + 6 * D, 2, 512)
        junk = v(self.arena, before + 7 * D, D)
        ssq, var, std, rstd = (v(sm, 360 + 4 * i, NC) for i in range(4))
        kinds = sorted({kind(c) for c in chunks}, reverse=True)
        rows_loaded, y_done, gated, sq_done, mean_done, sqrt_done, h_ready, t_done, t_copied = (
            sem(n) for n in ("rows_loaded", "y_done", "gated", "sq_done", "mean_done", "sqrt_done", "h_ready", "t_done", "t_copied"))
        added, first_q_done, first_q_copied, first_sc_done, first_sc_copied = (
            sem(n) for n in ("added", "first_q_done", "first_q_copied", "first_sc_done", "first_sc_copied"))
        gathered = [sem(f"gathered{k}") for k in range(RING)]
        slots_free, token, idx_ready, dots_done, gelu_done, w_ready, diag_ready, acc_free = (
            sem(n) for n in ("slots_free", "token", "idx_ready", "dots_done", "gelu_done", "w_ready", "diag_ready", "acc_free"))
        chain, top_ready, exp_done, iota_done, gate_loaded = (sem(n) for n in ("chain", "top_ready", "exp_done", "iota_done", "gate_loaded"))
        wq_loaded, keys_loaded, q_done, q_copied, sc_done, sc_copied = (
            sem(n) for n in ("wq_loaded", "keys_loaded", "q_done", "q_copied", "sc_done", "sc_copied"))
        table = self.dram["uv"][layer]
        last_layer = layer == LAYERS - 1
        out_gain = self.x[:, 1, :]
        rows_out = [self.h[:, i * D:(i + 1) * D] for i in range(CC)]
        out_scratch = self.h[:, CC * D:(CC + 1) * D]
        out_gain_loaded, out_sq, out_mean, out_std, out_ready, stored = (
            sem(n) for n in ("out_gain_loaded", "out_sq", "out_mean", "out_std", "out_ready", "stored"))
        if layer == 0:
            self.gqa_places()
        acc = ((self.bank[0], self.bank[1]), (self.bank[2], self.bank[3]))
        Q_BANK, S_BANK = self.bank[4], self.bank[5]
        first_jobs = 2 * lead
        qT_slots = 4 // first_jobs
        place = [divmod(i, nch) for i in range(body + 2)]

        def job_of(i, it):
            hd, c = place[i]
            return it * 4 + (2 * hd + c + first_jobs) if c < 2 else None

        def in_turn(norm, rest):
            norm(0)
            rest(0)
            norm(1)
            if nch > 2:
                norm(2)
            for i in range(1, nch):
                rest(i)
                if i + 2 < nch:
                    norm(i + 2)

        with nc.Block() as block:
            @block.sync
            def _(sp):
                for kd in kinds:
                    for dst, seg in ((gate_a[:, kd, :], G_A), (bc[:, 2 * kd, :], SC_F), (bc[:, 2 * kd + 1, :], SH_F)):
                        at = layer * MODW + seg * D
                        sp.dma_start(dst, self.modd[kd:kd + 1, at:at + D].broadcast_to([P, D])).then_inc(rows_loaded, 16)
                for kd in kinds:
                    seg = layer * MODW + G_F * D
                    sp.dma_start(gate_f[:, kd, :], self.modd[kd:kd + 1, seg:seg + D].broadcast_to([P, D])).then_inc(gate_loaded, 16)

                def load(j):
                    sp.wait_ge(q_done, j)
                    sp.dma_start(wq, self.w_query_rows(layer, j)).then_inc(wq_loaded, 16)
                    sp.wait_ge(sc_done, j)
                    sp.dma_start(keys, self.key_rows(layer, j)).then_inc(keys_loaded, 16)

                if last_layer:
                    sp.dma_start(out_gain, self.dram["norm_out"].broadcast_to([P, D])).then_inc(out_gain_loaded, 16)
                sp.sem_inc(wq_loaded, 16 * first_jobs)
                sp.sem_inc(keys_loaded, 16 * first_jobs)
                with sp.Fori(0, H // 2) as it:
                    for i in range(body):
                        j = job_of(i, it)
                        if j is not None:
                            load(j)
                if last_layer:
                    for i in range(CC):
                        sp.wait_ge(out_ready, i + 1)
                        sp.dma_start(self.out[0, i * P:(i + 1) * P, :], rows_out[i]).then_inc(stored, 16)
                    sp.wait_ge(stored, 16 * CC)
                else:
                    for g in (1, 2):
                        sp.wait_ge(slots_free, H * nch * NG + g + 1)
                        self.gqa_weights(sp, g)

            @block.gpsimd
            def _(pool):
                nc.gpsimd.iota(iota_i, pattern=[[1, TOPK]], base=0, channel_multiplier=0).then_inc(iota_done, 1)
                with pool.Fori(0, H // 2) as it:
                    for i in range(body):
                        pool.wait_ge(idx_ready, it * body + i + 1)
                        pool.sem_inc(token, 1)
                        for g in range(NG):
                            pool.wait_ge(slots_free, it * (body * NG) + i * NG + g + 1)
                            pool.sem_inc(token, 1)
                            for k in range(g * GRP, (g + 1) * GRP):
                                nc.gpsimd.indirect_dma_start(
                                    out=ring[:, k, :], out_offset=None, in_=table,
                                    in_offset=bass.IndirectOffsetOnAxis(ap=idx[:, i % 2, k:k + 1], axis=0)).then_inc(gathered[k], 16)

            @block.tensor
            def _(pe):
                pe.sem_inc(slots_free, 2)

                def project(i, n):
                    if i >= 2:
                        pe.wait_ge(gated, 2 * i + n - 3)
                    c = chunks[i]
                    for hd in range(H):
                        last = nc.tensor.matmul(self.bank[2 * (i % 2) + n][:], self.hT[:, hd, c * P:(c + 1) * P], self.w_o[:, hd, n * 512:(n + 1) * 512],
                                                start=(hd == 0), stop=(hd == H - 1))
                    last.then_inc(y_done, 1)

                def front(i):
                    c = chunks[i]
                    pe.wait_ge(h_ready, i + 1)
                    if i == nch - 1:
                        pe.sem_inc(slots_free, 1)
                    if i:
                        pe.wait_ge(t_copied, 2 * i)
                    for q in range(2):
                        for k in range(4):
                            kk = 4 * q + k
                            last = nc.tensor.transpose(self.bank[6 + q][:, k * P:(k + 1) * P], self.h[:, c * D + kk * P:c * D + (kk + 1) * P], self.ident[:])
                        last.then_inc(t_done, 1)
                    if i:
                        pe.wait_ge(first_q_copied, i)
                    else:
                        pe.wait_ge(self.first_loaded, 32 * first_jobs)
                    pe.wait_ge(t_copied, 2 * i + 2)
                    for j, (weights, sub) in enumerate(self.first):
                        for k in range(KD):
                            last = nc.tensor.matmul(Q_BANK[:, j * P:(j + 1) * P], weights[:, k, :], self.hT[:, k, c * P:(c + 1) * P],
                                                    start=(k == 0), stop=(k == KD - 1))
                    last.then_inc(first_q_done, 1)
                    pe.wait_ge(first_q_copied, i + 1)
                    if i:
                        pe.wait_ge(first_sc_copied, i)
                    for j, (weights, sub) in enumerate(self.first):
                        at = (first_jobs * (i % qT_slots) + j) * P
                        last = nc.tensor.matmul(S_BANK[:, j * NKEY:(j + 1) * NKEY], qT[:, at:at + P], sub, start=True, stop=True)
                    last.then_inc(first_sc_done, 1)

                def query(j):
                    pe.wait_ge(wq_loaded, j * 16 + 16)
                    for k in range(KD):
                        last = nc.tensor.matmul(Q_BANK[:, lo:hi], wq[:, k, :], self.hT[:, k, lo:hi], start=(k == 0), stop=(k == KD - 1))
                    last.then_inc(q_done, 1)

                def score(j):
                    pe.wait_ge(keys_loaded, j * 16 + 16)
                    pe.wait_ge(q_copied, j + 1)
                    for i, c in enumerate(chunks):
                        last = nc.tensor.matmul(S_BANK[:, i * NKEY:(i + 1) * NKEY], qT[:, c * P:(c + 1) * P], keys, start=True, stop=True)
                    last.then_inc(sc_done, 1)

                pe.wait_ge(self.w_o_loaded, 16)
                project(0, 0)
                project(0, 1)
                for i in range(1, nch):
                    project(i, 0)
                    if i == 1:
                        front(0)
                    project(i, 1)
                    if i == nch - 1:
                        pe.wait_ge(y_done, 2 * nch)
                        pe.sem_inc(slots_free, 1)
                    if i >= 2:
                        front(i - 1)
                front(nch - 1)
                pe.wait_ge(first_sc_copied, nch)
                pe.sem_inc(q_done, first_jobs)
                pe.sem_inc(sc_done, first_jobs)
                with pe.Fori(0, H // 2) as it:
                    for i in range(body):
                        j = job_of(i, it)
                        pe.wait_ge(acc_free, it * body + i + 1)
                        for g in range(NG):
                            pe.wait_ge(diag_ready, it * (body * NG) + i * NG + g + 1)
                            for k in range(GRP):
                                kk = g * GRP + k
                                for n in range(2):
                                    last = nc.tensor.matmul(acc[i % 2][n][:], diag[:, (g % 2) * GRP + k, :], ring[:, kk, D + n * 512:D + (n + 1) * 512],
                                                            start=(kk == 0), stop=(kk == TOPK - 1))
                            last.then_inc(slots_free, 1)
                            if j is not None and g == 0:
                                query(j)
                            if j is not None and g == 2:
                                pe.wait_ge(sc_copied, j)
                                score(j)

            @block.scalar
            def _(act):
                def copy_query(j):
                    act.wait_ge(q_done, j + 1)
                    nc.scalar.copy(qT[:, lo:hi], Q_BANK[:, lo:hi]).then_inc(q_copied, 1)

                def first_gates(u):
                    act.wait_ge(top_ready, u + 1)
                    nc.scalar.activation(gate[:, u, :], top, ACT.Exp, bias=nb, accum_out=es).then_inc(exp_done, 1)

                def norm(i):
                    c = chunks[i]
                    act.wait_ge(added, 2 * i + 2)
                    if i:
                        act.wait_ge(sq_done, i)
                    nc.scalar.activation(junk, self.x[:, c, :], ACT.Square, accum_out=ssq[:, c:c + 1]).then_inc(sq_done, 1)
                    act.wait_ge(mean_done, i + 1)
                    nc.scalar.activation(std[:, c:c + 1], var[:, c:c + 1], ACT.Sqrt).then_inc(sqrt_done, 1)

                def copies(i):
                    c = chunks[i]
                    for q in range(2):
                        act.wait_ge(t_done, 2 * i + q + 1)
                        nc.scalar.copy(self.hT[:, 4 * q:4 * q + 4, c * P:(c + 1) * P],
                                       self.bank[6 + q][:].rearrange("p (a b) -> p a b", a=4)).then_inc(t_copied, 1)
                    act.wait_ge(first_q_done, i + 1)
                    if i >= qT_slots:
                        act.wait_ge(first_sc_done, i + 1 - qT_slots)
                    at = first_jobs * (i % qT_slots) * P
                    nc.scalar.copy(qT[:, at:at + first_jobs * P], Q_BANK[:, 0:first_jobs * P]).then_inc(first_q_copied, 1)
                    if i < 2:
                        first_gates(i)

                in_turn(norm, copies)
                act.wait_ge(first_sc_done, nch)
                act.sem_inc(q_copied, first_jobs)
                with act.Fori(0, H // 2) as it:
                    for i in range(body):
                        u = i % 2
                        j = job_of(i, it)
                        for g in range(NG):
                            n = it * (body * NG) + i * NG + g
                            ks = slice(g * GRP, (g + 1) * GRP)
                            act.wait_ge(dots_done, n + 1)
                            nc.scalar.activation(w[:, u, ks], a[:, u, ks], ACT.Gelu).then_inc(gelu_done, 1)
                            act.wait_ge(w_ready, n + 1)
                            act.wait_ge(slots_free, n + 3)
                            for k in range(GRP):
                                last = nc.scalar.mul(diag[:, (g % 2) * GRP + k, :], self.ident[:], w[:, u, g * GRP + k:g * GRP + k + 1])
                            last.then_inc(diag_ready, 1)
                            if j is not None and g == 1:
                                act.wait_ge(sc_done, j)
                                copy_query(j)
                        act.wait_ge(top_ready, it * body + i + 3)
                        nc.scalar.activation(gate[:, u, :], top, ACT.Exp, bias=nb, accum_out=es).then_inc(exp_done, 1)
                if last_layer:
                    for i in range(CC):
                        act.wait_ge(acc_free, H * nch + 1 + i)
                        if i:
                            act.wait_ge(out_sq, i)
                        nc.scalar.activation(out_scratch, self.x[:, CC + i, :], ACT.Square, accum_out=ssq[:, i:i + 1]).then_inc(out_sq, 1)
                    act.wait_ge(out_mean, 1)
                    nc.scalar.activation(std[:, 0:CC], var[:, 0:CC], ACT.Sqrt).then_inc(out_std, 1)

            @block.vector
            def _(dve):
                count = [0]

                def link(ins):
                    count[0] += 1
                    ins.then_inc(chain, 1)
                    dve.wait_ge(chain, count[0])

                def restart():
                    dve.sem_clear(chain)
                    count[0] = 0

                def top16(out_v, out_i, src):
                    link(nc.vector.max(out_v[:, 0:8], src))
                    link(nc.vector.max_index(out_i[:, 0:8], out_v[:, 0:8], src))
                    link(nc.vector.match_replace(src, out_v[:, 0:8], src, NEG))
                    link(nc.vector.max(out_v[:, 8:16], src))
                    link(nc.vector.max_index(out_i[:, 8:16], out_v[:, 8:16], src))

                def choose(par, c, u, stage):
                    if stage == 0:
                        for side in range(2):
                            top16(val[:, side, :], ind[:, side, :], scores[:, par, c, side * NKEY:(side + 1) * NKEY])
                        link(nc.vector.tensor_copy(indf, ind))
                    if stage == 1:
                        link(nc.vector.tensor_tensor(C, val[:, 0, :].unsqueeze(2).broadcast_to([P, TOPK, TOPK]),
                                                     val[:, 1, :].unsqueeze(1).broadcast_to([P, TOPK, TOPK]), ALU.add))
                        top16(top, pos, C.rearrange("p a b -> p (a b)"))
                        link(nc.vector.tensor_scalar(posi[:, 0, :], pos, 4, None, ALU.logical_shift_right))
                        link(nc.vector.tensor_scalar(posi[:, 1, :], pos, TOPK - 1, None, ALU.bitwise_and))
                    if stage == 2:
                        for side in range(2):
                            link(nc.vector.tensor_tensor(OH, posi[:, side, :].unsqueeze(2).broadcast_to([P, TOPK, TOPK]),
                                                         iota.unsqueeze(1).broadcast_to([P, TOPK, TOPK]), ALU.is_equal))
                            link(nc.vector.tensor_tensor(OH, OH, indf[:, side, :].unsqueeze(1).broadcast_to([P, TOPK, TOPK]), ALU.mult))
                            link(nc.vector.tensor_reduce(sel[:, side, :], OH, AX.X, ALU.add))
                    if stage == 3:
                        link(nc.vector.scalar_tensor_tensor(out=idx[:, u, :], in0=sel[:, 0, :], scalar=float(NKEY), in1=sel[:, 1, :], op0=ALU.mult, op1=ALU.add))
                        dve.sem_inc(idx_ready, 1)
                        link(nc.vector.tensor_scalar(nb, top[:, 0:1], -1.0, None, ALU.mult))
                        dve.sem_inc(top_ready, 1)

                def finish_gates(u):
                    link(nc.vector.reciprocal(er, es))
                    link(nc.vector.tensor_scalar(gate[:, u, :], gate[:, u, :], er, None, ALU.mult))

                def copy_scores(j, par, side):
                    dve.wait_ge(sc_done, j + 1)
                    nc.vector.tensor_copy(scores[:, par, 0:nch, side * NKEY:(side + 1) * NKEY],
                                          S_BANK[:, 0:nch * NKEY].rearrange("p (c n) -> p c n", c=nch)).then_inc(sc_copied, 1)
                    dve.wait_ge(sc_copied, j + 1)

                def first_choice(u):
                    choose(0, u, u)
                    dve.wait_ge(exp_done, u + 1)
                    finish_gates(u)

                dve.wait_ge(iota_done, 1)
                link(nc.vector.tensor_copy(iota, iota_i))
                dve.wait_ge(rows_loaded, 3 * 16 * len(kinds))
                def add_and_norm(i):
                    c = chunks[i]
                    kd = kind(c)
                    for n in range(2):
                        dve.wait_ge(y_done, 2 * i + n + 1)
                        if i:
                            dve.wait_ge(added, 2 * i + n - 1)
                        nc.vector.tensor_tensor(y[:, n, :], self.bank[2 * (i % 2) + n][:], gate_a[:, kd, n * 512:(n + 1) * 512], ALU.mult).then_inc(gated, 1)
                        dve.wait_ge(gated, 2 * i + n + 1)
                        xs = self.x[:, c, n * 512:(n + 1) * 512]
                        nc.vector.tensor_tensor(xs, xs, y[:, n, :], ALU.add).then_inc(added, 1)
                    dve.wait_ge(sq_done, i + 1)
                    nc.vector.tensor_scalar(var[:, c:c + 1], ssq[:, c:c + 1], 1.0 / D, EPS, ALU.mult, ALU.add).then_inc(mean_done, 1)
                    dve.wait_ge(sqrt_done, i + 1)
                    link(nc.vector.reciprocal(rstd[:, c:c + 1], std[:, c:c + 1]))
                    hc = self.h[:, c * D:(c + 1) * D]
                    dve.wait_ge(added, 2 * i + 2)
                    link(nc.vector.scalar_tensor_tensor(out=hc, in0=self.x[:, c, :], scalar=rstd[:, c:c + 1], in1=bc[:, 2 * kd, :],
                                                        op0=ALU.mult, op1=ALU.mult))
                    nc.vector.tensor_tensor(hc, hc, bc[:, 2 * kd + 1, :], ALU.add).then_inc(h_ready, 1)

                def first_scores(i):
                    dve.wait_ge(first_sc_done, i + 1)
                    nc.vector.tensor_copy(scores[:, 0:lead, i, :], S_BANK[:, 0:first_jobs * NKEY].rearrange("p (a n) -> p a n", a=lead)).then_inc(first_sc_copied, 1)
                    dve.wait_ge(first_sc_copied, i + 1)
                    if i < 2:
                        for stage in range(4):
                            choose(0, i, i, stage)
                        dve.wait_ge(exp_done, i + 1)
                        finish_gates(i)

                in_turn(add_and_norm, first_scores)
                dve.sem_inc(sc_copied, first_jobs)
                dve.wait_ge(h_ready, nch)
                restart()
                dve.wait_ge(gate_loaded, 16 * len(kinds))
                dve.sem_inc(acc_free, 2)
                with dve.Fori(0, H // 2) as it:
                    for i in range(body):
                        u = i % 2
                        hd, c = place[i]
                        unit = it * body + i
                        j = job_of(i, it)
                        for g in range(NG):
                            for k in range(g * GRP, (g + 1) * GRP):
                                dve.wait_ge(gathered[k], unit * 16 + 16)
                                last = nc.vector.tensor_tensor_reduce(
                                    out=ring[:, k, 0:D], in0=ring[:, k, 0:D], in1=self.h[:, chunks[c] * D:(chunks[c] + 1) * D], scale=1.0, scalar=0.0,
                                    op0=ALU.mult, op1=ALU.add, accum_out=a[:, u, k:k + 1])
                            last.then_inc(dots_done, 1)
                            ks = slice(g * GRP, (g + 1) * GRP)
                            dve.wait_ge(gelu_done, unit * NG + g + 1)
                            nc.vector.tensor_tensor(w[:, u, ks], w[:, u, ks], gate[:, u, ks], ALU.mult).then_inc(w_ready, 1)
                            choose(place[i + 2][0] % 2, place[i + 2][1], u, g)
                        dve.wait_ge(exp_done, unit + 3)
                        finish_gates(u)
                        if j is not None:
                            copy_scores(j, (hd + lead) % 2, c)
                        dve.wait_ge(slots_free, unit * NG + 2 * NG)
                        for n in range(2):
                            s = acc[u][n][:]
                            link(nc.vector.tensor_tensor(s, s, gate_f[:, kind(chunks[c]), n * 512:(n + 1) * 512], ALU.mult))
                        for n in range(2):
                            xs = self.x[:, chunks[c], n * 512:(n + 1) * 512]
                            link(nc.vector.tensor_tensor(xs, xs, acc[u][n][:], ALU.add))
                        dve.sem_inc(acc_free, 1)
                        restart()
                if last_layer:
                    dve.wait_ge(out_sq, CC)
                    nc.vector.tensor_scalar(var[:, 0:CC], ssq[:, 0:CC], 1.0 / D, EPS, ALU.mult, ALU.add).then_inc(out_mean, 1)
                    dve.wait_ge(out_std, 1)
                    link(nc.vector.reciprocal(rstd[:, 0:CC], std[:, 0:CC]))
                    dve.wait_ge(out_gain_loaded, 16)
                    for i in range(CC):
                        nc.vector.scalar_tensor_tensor(out=rows_out[i], in0=self.x[:, CC + i, :], scalar=rstd[:, i:i + 1], in1=out_gain,
                                                       op0=ALU.mult, op1=ALU.mult).then_inc(out_ready, 1)

    def w_query_rows(self, layer, j):
        return self.dram["w_query"][layer, bass.ds(j, 1), :, :].rearrange("a p (k n) -> p (a k) n", k=KD)

    def key_rows(self, layer, j):
        return self.dram["keys"][layer, bass.ds(j, 1), :, :].rearrange("a p n -> p (a n)")

    def gqa_places(self):
        v = self.view
        self.w_qkv = v(self.arena, 6 * 2 * D, 3, KD, 512)
        self.rope_g = v(self.arena, 9984, NC, 2 * P)
        self.gain_g = v(self.arena, 11008, 2, P)
        self.w_o = v(self.arena, 8 * 2 * D, H, D)
        self.w_qkv_loaded = self.lasting_sem("w_qkv_loaded")

    def gqa_weights(self, sp, g):
        d, loaded = self.dram, self.w_qkv_loaded
        if g == 1:
            sp.dma_start(self.rope_g, d["rope_g"]).then_inc(loaded, 16)
            sp.dma_start(self.gain_g, d["gain_g"].broadcast_to([P, 2 * P]).rearrange("p (a b) -> p a b", a=2)).then_inc(loaded, 16)
        for n in {1: (0,), 2: (1, 2)}[g]:
            sp.dma_start(self.w_qkv[:, n], d["w_qkv"][:, n]).then_inc(loaded, 16)

    @phase
    def gqa_in(self):
        nc, v, sem = self.nc, self.view, self.sem
        NQK = H + GKV
        order = list(range(CC, NC)) + list(range(CC))
        V = self.gV = v(self.arena, 0, NC, GKV * P)
        qT = self.gqT = v(self.arena, 1024, H, TOK)
        kT = self.gkT = v(self.arena, 5120, GKV, TOK)
        n1 = v(self.arena, 6144, NQK, P)
        n2 = v(self.arena, 7424, NQK, P)
        n3 = v(self.arena, 8704, NQK, P)
        junk = v(self.aux, 0, NQK, P)
        ssq, var, std, rstd = (v(self.small, 128 + 40 * i, NC, NQK) for i in range(4))
        a_done, sq_done, chain, mean_done, sqrt_done, bank_free, r_ready, t_done, t_copied, v_copied = (
            sem(n) for n in ("a_done", "sq_done", "chain", "mean_done", "sqrt_done", "bank_free", "r_ready", "t_done", "t_copied", "v_copied"))

        norm = self.norm_steps(1, order, v(self.arena, 12 * 2 * D, 4, D), v(self.aux, 1280, D))

        def heads(i):
            c = order[i]
            return list(range(NQK)) if c >= CC else list(range(H, NQK))

        def src(i, j):
            b = self.bank[3 * (i % 2) + (2 if j >= H else j // 4)]
            return b[:, (j % 4 if j < H else j - H) * P:((j % 4 if j < H else j - H) + 1) * P]

        sq_before = [sum(len(heads(x)) for x in range(c)) for c in range(NC + 1)]
        t_before = [sum(3 if order[x] >= CC else 1 for x in range(c)) for c in range(NC + 1)]

        with nc.Block() as block:
            @block.sync
            def _(sp):
                norm.load(sp)

            @block.tensor
            def _(pe):
                def project(i):
                    c = order[i]
                    if i >= 2:
                        pe.wait_ge(t_copied, t_before[1])
                    norm.transposes(pe, i)
                    if i == 0:
                        pe.wait_ge(self.w_qkv_loaded, 80)
                    pe.wait_ge(norm.copied, 2 * i + 2)
                    if i >= 2:
                        pe.wait_ge(bank_free, i - 1)
                    for n in ((0, 1, 2) if c >= CC else (2,)):
                        for k in range(KD):
                            last = nc.tensor.matmul(self.bank[3 * (i % 2) + n][:], self.hT[:, k, c * P:(c + 1) * P], self.w_qkv[:, n, k, :],
                                                    start=(k == 0), stop=(k == KD - 1))
                    last.then_inc(a_done, 1)

                def transposes(i):
                    pe.wait_ge(r_ready, i + 1)
                    groups = ([list(range(0, 4)), list(range(4, 8))] if order[i] >= CC else []) + [[8, 9]]
                    for m, g in enumerate(groups):
                        n = t_before[i] + m
                        if n >= 2:
                            pe.wait_ge(t_copied, n - 1)
                        for jj, j in enumerate(g):
                            last = nc.tensor.transpose(self.bank[6 + n % 2][:, jj * P:(jj + 1) * P], n3[:, j, :], self.ident[:])
                        last.then_inc(t_done, 1)

                project(0)
                project(1)
                transposes(0)
                for i in range(2, NC):
                    project(i)
                for i in range(1, NC):
                    transposes(i)

            @block.scalar
            def _(act):
                norm.statistics(act)
                norm.copies(act, 0)
                for i, c in enumerate(order):
                    if i + 1 < NC:
                        norm.copies(act, i + 1)
                    act.wait_ge(a_done, i + 1)
                    if i:
                        act.wait_ge(sq_done, sq_before[i])
                    for j in heads(i):
                        nc.scalar.activation(junk[:, j, :], src(i, j), ACT.Square, accum_out=ssq[:, i, j:j + 1]).then_inc(sq_done, 1)
                    nc.scalar.copy(V[:, c, :], self.bank[3 * (i % 2) + 2][:, GKV * P:2 * GKV * P]).then_inc(v_copied, 1)
                    act.wait_ge(mean_done, i + 1)
                    j0 = heads(i)[0]
                    nc.scalar.activation(std[:, i, j0:], var[:, i, j0:], ACT.Sqrt).then_inc(sqrt_done, 1)

            @block.vector
            def _(dve):
                count = [0]

                def link(ins):
                    count[0] += 1
                    ins.then_inc(chain, 1)
                    dve.wait_ge(chain, count[0])

                norm.rows(dve)
                for i, c in enumerate(order):
                    j0 = heads(i)[0]
                    nh = NQK - j0
                    dve.wait_ge(sq_done, sq_before[i + 1])
                    nc.vector.tensor_scalar(var[:, i, j0:], ssq[:, i, j0:], 1.0 / P, EPS, ALU.mult, ALU.add).then_inc(mean_done, 1)
                    dve.wait_ge(sqrt_done, i + 1)
                    link(nc.vector.reciprocal(rstd[:, i, j0:], std[:, i, j0:]))
                    for b, (lo, hi) in enumerate(((0, 4), (4, 8), (8, 10))):
                        if lo < j0:
                            continue
                        link(nc.vector.tensor_tensor(n1[:, lo:hi, :], self.bank[3 * (i % 2) + b][:, 0:(hi - lo) * P].rearrange("p (a b) -> p a b", b=P),
                                                     rstd[:, i, lo:hi].unsqueeze(2).broadcast_to([P, hi - lo, P]), ALU.mult))
                    dve.wait_ge(v_copied, i + 1)
                    dve.sem_inc(bank_free, 1)
                    for lo, hi, g in ((0, H, 0), (H, NQK, 1)):
                        if lo < j0:
                            continue
                        link(nc.vector.tensor_tensor(n1[:, lo:hi, :], n1[:, lo:hi, :], self.gain_g[:, g, :].unsqueeze(1).broadcast_to([P, hi - lo, P]), ALU.mult))
                    if i:
                        dve.wait_ge(t_done, t_before[i])
                    hs = slice(j0, NQK)
                    link(nc.vector.tensor_tensor(n3[:, hs, :], n1[:, hs, :], self.rope_g[:, c, 0:P].unsqueeze(1).broadcast_to([P, nh, P]), ALU.mult))
                    for b in range(4):
                        o = b ^ 1
                        link(nc.vector.tensor_tensor(n2[:, hs, 32 * b:32 * b + 32], n1[:, hs, 32 * o:32 * o + 32],
                                                     self.rope_g[:, c, P + 32 * b:P + 32 * b + 32].unsqueeze(1).broadcast_to([P, nh, 32]), ALU.mult))
                    link(nc.vector.tensor_tensor(n3[:, hs, :], n3[:, hs, :], n2[:, hs, :], ALU.add))
                    dve.sem_inc(r_ready, 1)
                    cols = slice(c * P, (c + 1) * P)
                    groups = ([(qT, 0, 4), (qT, 4, 4)] if c >= CC else []) + [(kT, 0, 2)]
                    for k, (dst, at, m) in enumerate(groups):
                        n = t_before[i] + k
                        dve.wait_ge(t_done, n + 1)
                        nc.vector.tensor_copy(dst[:, at:at + m, cols], self.bank[6 + n % 2][:, 0:m * P].rearrange("p (a b) -> p a b", b=P)).then_inc(t_copied, 1)

    @phase
    def gqa_attention(self):
        self.w_o_loaded = self.lasting_sem("w_o_loaded")

        def pre(who, eng):
            if who == "sp":
                eng.dma_start(self.w_o, self.dram["w_o1"]).then_inc(self.w_o_loaded, 16)

        self.attention(
            1, list(range(CC, NC)), lambda c: TOK, lambda hd, t: self.gV[:, t, (hd // 4) * P:(hd // 4 + 1) * P],
            lambda hd, c: [(self.gqT[:, hd, c * P:(c + 1) * P], self.gkT[:, hd // 4, :])],
            1.0 / math.sqrt(P), pre=pre)

    def layer(self, i):
        every = list(range(NC))
        if i == 0:
            self.mla_in()
            self.mla_attention()
            ffn = every
        else:
            self.gqa_in()
            self.gqa_attention()
            ffn = list(range(CC, NC))
        self.peer(i, ffn)


def rope_tables(rot):
    rows = SEQ // 64
    row, col = np.repeat(np.arange(rows), 64), np.tile(np.arange(64), rows)
    half = rot // 2
    inv = 10000.0 ** (-np.arange(0, half, 2) / half)
    ar, ac = row[:, None] * inv, col[:, None] * inv
    ang = np.concatenate([ar, ar, ac, ac], axis=-1)
    sign = np.repeat([-1.0, 1.0, -1.0, 1.0], rot // 4)
    cos = np.concatenate([np.ones((CTX, rot)), np.cos(ang)])
    sin = np.concatenate([np.zeros((CTX, rot)), np.sin(ang) * sign])
    return cos.astype(np.float32), sin.astype(np.float32)


def kernel(**inputs):
    import concourse.bacc as bacc
    from concourse.bass_utils import run_bass_kernel_spmd as run

    g = {k: np.asarray(a) for k, a in inputs.items()}

    def tiles(w):
        return w.reshape(w.shape[0] // P, P, -1).transpose(1, 0, 2)

    def swap(w, n):
        s = w.shape
        return w.reshape(s[:-1] + (s[-1] // (2 * n), 2, n))[..., ::-1, :].reshape(s)

    def ahead(w):
        return np.concatenate([w, w[0:4]])

    cos, sin = rope_tables(ROPE)
    gcos, gsin = rope_tables(P)
    w_in = g["l0_mla_w_in"]
    uq = g["l0_mla_w_uq"].reshape(QR, H, NOPE + ROPE)
    uqr = uq[:, :, NOPE:]
    ukv = g["l0_mla_w_ukv"].reshape(KVR, H, 256)
    arrays = {
        "c_cols": np.stack([g["c"][0], g["c_ctx"]]).reshape(2, KD, P).transpose(2, 1, 0),
        "tokens": np.concatenate([g["ctx"][0], g["x"][0]]).reshape(NC, P, D).transpose(1, 0, 2),
        "ident": np.eye(P, dtype=np.float32),
        "ada": np.stack([g[f"l{i}_ada_w"].reshape(KD, P, ADA_ROUNDS, ADA).transpose(2, 0, 1, 3).reshape(-1, P, ADA) for i in range(LAYERS)]),
        "ada_b": np.stack([g[f"l{i}_ada_b"] for i in range(LAYERS)]),
        "gains": np.stack([np.concatenate([g[f"l{i}_norm_ffn"], g[f"l{i}_norm_mix"]]).reshape(NQ, 512) for i in range(LAYERS)]),
        "w_in": tiles(np.concatenate([w_in, swap(w_in[:, QR + KVR:], ROPE // 4)], axis=1)),
        "rope_rows": np.concatenate([cos, sin], axis=1).reshape(NC, P, 2 * ROPE).transpose(1, 0, 2),
        "rope_cols": np.concatenate([cos, sin], axis=1).T,
        "gcol": np.concatenate([g["l0_mla_q_norm"].reshape(KQ, P), g["l0_mla_kv_norm"].reshape(KKV, P)]).T,
        "w_uq": tiles(np.concatenate([uq, swap(uqr, ROPE // 4)], axis=2).reshape(QR, H * 256)),
        "w_uk": tiles(ukv[:, :, :P].reshape(KVR, H * P)),
        "w_uv": tiles(ukv[:, :, P:].reshape(KVR, H * P)),
        "w_o0": tiles(g["l0_mla_w_o"]),
        "w_o1": tiles(g["l1_gqa_w_o"]),
        "w_qkv": tiles(g["l1_gqa_w_qkv"]).reshape(P, KD, 3, 512).transpose(0, 2, 1, 3),
        "rope_g": np.concatenate([gcos, gsin], axis=1).reshape(NC, P, 2 * P).transpose(1, 0, 2),
        "gain_g": np.concatenate([g["l1_gqa_q_norm"], g["l1_gqa_k_norm"]])[None],
        "keys": np.stack([ahead(np.stack([g[f"l{i}_peer_k1"], g[f"l{i}_peer_k2"]], axis=1).transpose(0, 1, 3, 2).reshape(2 * H, P, NKEY)) for i in range(LAYERS)]),
        "w_query": np.stack([ahead(g[f"l{i}_peer_w_query"].reshape(KD, P, 2 * H, P).transpose(2, 1, 0, 3).reshape(2 * H, P, KD * P)) for i in range(LAYERS)]),
        "norm_out": g["norm_out"][None],
    }
    for i in range(LAYERS):
        arrays[f"uv{i}"] = np.concatenate([g[f"l{i}_peer_u"], g[f"l{i}_peer_v"]], axis=1)
    arrays = {k: np.ascontiguousarray(a) for k, a in arrays.items()}

    nc = bacc.Bacc("TRN2", target_bir_lowering=False, num_devices=1)
    dram = {k: nc.dram_tensor(f"in_{k}", a.shape, mybir.dt.from_np(a.dtype), kind="ExternalInput").ap() for k, a in arrays.items()}
    dram["uv"] = [dram[f"uv{i}"] for i in range(LAYERS)]
    out = nc.dram_tensor("out", (1, SEQ, D), F32, kind="ExternalOutput").ap()
    Kernel(nc, dram, out).build()
    r = run(nc, [{f"in_{k}": a for k, a in arrays.items()}], core_ids=[0])
    return r.results[0]["out"]
```
